# Optimizing a Trainium2 kernel written in Bass

```python
import jax, jax.numpy as jnp
from jax import lax
import numpy as np

D_MODEL = 1024
BATCH = 1
SEQ = 512
DEPTH = 1

CHUNK = 64
Q_BLOCK = 128
EPS = 1e-6

SB_HEADS = 8
SB_HEAD_DIM = 64
SB_WIDTH = SB_HEADS * SB_HEAD_DIM

MLA_HEADS = 8
MLA_NOPE_DIM = 64
MLA_ROPE_DIM = 32
MLA_V_DIM = 64
MLA_Q_LORA = 384
MLA_KV_LORA = 256
MLA_QK_DIM = MLA_NOPE_DIM + MLA_ROPE_DIM
MLA_WIDTH = MLA_HEADS * MLA_V_DIM
ROPE_THETA = 10000.0

N_BRANCH = 2
IN_SPLIT_SIZES = (SB_WIDTH, SB_WIDTH, SB_WIDTH, SB_WIDTH,
                  MLA_Q_LORA, MLA_KV_LORA, MLA_ROPE_DIM, MLA_WIDTH,
                  N_BRANCH * D_MODEL)
IN_COLS = sum(IN_SPLIT_SIZES)


def rmsnorm(x, g):
    x32 = x.astype(jnp.float32)
    inv = lax.rsqrt(jnp.mean(x32 * x32, axis=-1, keepdims=True) + EPS)
    return (x32 * inv).astype(x.dtype) * g

def rope_tables(seq_len):
    half = MLA_ROPE_DIM // 2
    inv_freq = ROPE_THETA ** (-jnp.arange(half, dtype=jnp.float32) / half)
    ang = jnp.arange(seq_len, dtype=jnp.float32)[:, None] * inv_freq[None, :]
    return jnp.cos(ang), jnp.sin(ang)

def apply_rope(x, cos, sin):
    half = x.shape[-1] // 2
    x32 = x.astype(jnp.float32)
    x1, x2 = x32[..., :half], x32[..., half:]
    c, s = cos[None, :, None, :], sin[None, :, None, :]
    return jnp.concatenate([x1 * c - x2 * s, x1 * s + x2 * c], axis=-1).astype(x.dtype)

def to_query_blocks(q):
    b, s, h, d = q.shape
    return q.reshape(b, s // Q_BLOCK, Q_BLOCK, h, d).transpose(1, 0, 3, 2, 4)

def from_query_blocks(o):
    nb, b, h, qb, d = o.shape
    return o.transpose(1, 0, 3, 2, 4).reshape(b, nb * qb, h, d)

def stick_breaking_attention(q, k, v):
    seq_len = q.shape[1]
    scale = q.shape[-1] ** -0.5
    key_pos = jnp.arange(seq_len)
    qb = to_query_blocks(q)

    def block(args):
        q_blk, i = args
        q_pos = i * Q_BLOCK + jnp.arange(Q_BLOCK)
        z = jnp.einsum("bhqd,bshd->bhqs", q_blk, k).astype(jnp.float32) * scale
        strict = key_pos[None, :] < q_pos[:, None]
        log_beta = jax.nn.log_sigmoid(z)
        log_1m = jnp.where(strict, jax.nn.log_sigmoid(-z), 0.0)
        later = lax.cumsum(log_1m, axis=3, reverse=True) - log_1m
        w = jnp.where(strict, jnp.exp(log_beta + later), 0.0)
        return jnp.einsum("bhqs,bshd->bhqd", w.astype(v.dtype), v)

    o = lax.map(block, (qb, jnp.arange(qb.shape[0])))
    return from_query_blocks(o)

def chunk_causal_softmax_attention(q, k, v):
    seq_len = q.shape[1]
    scale = q.shape[-1] ** -0.5
    key_chunk = jnp.arange(seq_len) // CHUNK
    qb = to_query_blocks(q)

    def block(args):
        q_blk, i = args
        q_chunk = (i * Q_BLOCK + jnp.arange(Q_BLOCK)) // CHUNK
        allowed = key_chunk[None, :] <= q_chunk[:, None]
        z = jnp.einsum("bhqd,bshd->bhqs", q_blk, k).astype(jnp.float32) * scale
        p = jax.nn.softmax(jnp.where(allowed, z, -jnp.inf), axis=-1)
        return jnp.einsum("bhqs,bshd->bhqd", p.astype(v.dtype), v)

    o = lax.map(block, (qb, jnp.arange(qb.shape[0])))
    return from_query_blocks(o)

def first_inputs(seed: int = 0) -> dict:
    key = jax.random.key(seed)
    ks = jax.random.split(key, 16)
    f32 = jnp.float32

    def nrm(k, shape, fan_in):
        return jax.random.normal(k, shape, f32) * (fan_in ** -0.5)

    def gain(k, n):
        return 1.0 + 0.01 * jax.random.normal(k, (DEPTH, n), f32)

    return {
        "x": jax.random.normal(ks[0], (BATCH, SEQ, D_MODEL), f32),
        "norm_in_g": gain(ks[1], D_MODEL),
        "w_in": nrm(ks[2], (DEPTH, D_MODEL, IN_COLS), D_MODEL),
        "b_gate": 0.1 * jax.random.normal(ks[3], (DEPTH, N_BRANCH * D_MODEL), f32),
        "q_norm_g": gain(ks[4], MLA_Q_LORA),
        "w_q_up": nrm(ks[5], (DEPTH, MLA_Q_LORA, MLA_HEADS * MLA_QK_DIM), MLA_Q_LORA),
        "kv_norm_g": gain(ks[6], MLA_KV_LORA),
        "w_kv_up": nrm(ks[7], (DEPTH, MLA_KV_LORA, MLA_HEADS * (MLA_NOPE_DIM + MLA_V_DIM)), MLA_KV_LORA),
        "w_o_sb": nrm(ks[8], (DEPTH, SB_WIDTH, D_MODEL), SB_WIDTH),
        "w_o_mla": nrm(ks[9], (DEPTH, MLA_WIDTH, D_MODEL), MLA_WIDTH),
        "w_out": nrm(ks[10], (DEPTH, D_MODEL, D_MODEL), D_MODEL),
        "norm_f_g": 1.0 + 0.01 * jax.random.normal(ks[11], (D_MODEL,), f32),
    }

def first_block(x, norm_in_g, w_in, b_gate, q_norm_g, w_q_up, kv_norm_g, w_kv_up,
              w_o_sb, w_o_mla, w_out, norm_f_g):
    b, s, _ = x.shape
    cos, sin = rope_tables(s)
    offsets = [int(o) for o in np.cumsum(IN_SPLIT_SIZES)[:-1]]

    for l in range(DEPTH):
        h = rmsnorm(x, norm_in_g[l])
        proj = jnp.einsum("bsd,de->bse", h, w_in[l])
        (q_sb, k_sb, v_sb, gate_sb, c_q, c_kv, k_rope,
         gate_mla, gate_logits) = jnp.split(proj, offsets, axis=-1)

        o_sb = stick_breaking_attention(
            q_sb.reshape(b, s, SB_HEADS, SB_HEAD_DIM),
            k_sb.reshape(b, s, SB_HEADS, SB_HEAD_DIM),
            v_sb.reshape(b, s, SB_HEADS, SB_HEAD_DIM)).reshape(b, s, SB_WIDTH)
        y_sb = jnp.einsum("bsc,cd->bsd", o_sb * jax.nn.silu(gate_sb), w_o_sb[l])

        q = jnp.einsum("bsr,re->bse", rmsnorm(c_q, q_norm_g[l]), w_q_up[l])
        q = q.reshape(b, s, MLA_HEADS, MLA_QK_DIM)
        q_nope, q_rope = q[..., :MLA_NOPE_DIM], q[..., MLA_NOPE_DIM:]
        q_rope = apply_rope(q_rope, cos, sin)
        kv = jnp.einsum("bsr,re->bse", rmsnorm(c_kv, kv_norm_g[l]), w_kv_up[l])
        kv = kv.reshape(b, s, MLA_HEADS, MLA_NOPE_DIM + MLA_V_DIM)
        k_nope, v_mla = kv[..., :MLA_NOPE_DIM], kv[..., MLA_NOPE_DIM:]
        k_rope = apply_rope(k_rope[:, :, None, :], cos, sin)
        q_full = jnp.concatenate([q_nope, q_rope], axis=-1)
        k_full = jnp.concatenate(
            [k_nope, jnp.broadcast_to(k_rope, (b, s, MLA_HEADS, MLA_ROPE_DIM))], axis=-1)
        o_mla = chunk_causal_softmax_attention(q_full, k_full, v_mla).reshape(b, s, MLA_WIDTH)
        y_mla = jnp.einsum("bsc,cd->bsd", o_mla * jax.nn.silu(gate_mla), w_o_mla[l])

        g = jax.nn.sigmoid(gate_logits + b_gate[l]).reshape(b, s, N_BRANCH, D_MODEL)
        merged = g[:, :, 0, :] * y_sb + g[:, :, 1, :] * y_mla
        x = x + jnp.einsum("bsd,de->bse", merged, w_out[l])

    return rmsnorm(x, norm_f_g)


DEPTH_2 = 2

N_MIXERS = 2
N_HEADS = 16
HEAD_DIM = D_MODEL // N_HEADS
CONV_WIDTH = 3
D_FF = 4 * D_MODEL
PLE_DIM = 256
N_ATTN = (DEPTH_2 + 1) // 2
N_CONV = DEPTH_2 // 2
RMS_EPS = 1e-6
NEG_INF = -1e30


def rmsnorm_2(x, g):
    xf = x.astype(jnp.float32)
    y = xf * lax.rsqrt(jnp.mean(xf * xf, axis=-1, keepdims=True) + RMS_EPS)
    return (y * g.astype(jnp.float32)).astype(x.dtype)

def fox_attention(h, w_in, b_f, w_out):
    B, S, D = h.shape
    proj = h @ w_in
    q = proj[..., :D].reshape(B, S, N_HEADS, HEAD_DIM).transpose(0, 2, 1, 3)
    k = proj[..., D:2 * D].reshape(B, S, N_HEADS, HEAD_DIM).transpose(0, 2, 1, 3)
    v = proj[..., 2 * D:3 * D].reshape(B, S, N_HEADS, HEAD_DIM).transpose(0, 2, 1, 3)
    q = q * jnp.asarray(HEAD_DIM ** -0.5, q.dtype)
    f_logit = (proj[..., 3 * D:] + b_f).astype(jnp.float32)
    log_f = jax.nn.log_sigmoid(f_logit)
    c = lax.cumsum(log_f, axis=1).transpose(0, 2, 1)
    k_pos = jnp.arange(S)

    def q_block(i):
        start = i * Q_BLOCK
        qb = lax.dynamic_slice_in_dim(q, start, Q_BLOCK, axis=2)
        cb = lax.dynamic_slice_in_dim(c, start, Q_BLOCK, axis=2)
        s = jnp.einsum('bhqd,bhkd->bhqk', qb, k, preferred_element_type=jnp.float32)
        s = s + cb[..., :, None] - c[..., None, :]
        q_pos = start + jnp.arange(Q_BLOCK)
        s = jnp.where(k_pos[None, :] <= q_pos[:, None], s, NEG_INF)
        pr = jax.nn.softmax(s, axis=-1)
        return jnp.einsum('bhqk,bhkd->bhqd', pr.astype(v.dtype), v)

    o = lax.map(q_block, jnp.arange(S // Q_BLOCK))
    o = o.transpose(1, 0, 3, 2, 4).reshape(B, S, D)
    return o @ w_out

def short_conv(h, w_in, conv_w, w_out):
    D = h.shape[-1]
    proj = h @ w_in
    b_gate = proj[..., :D]
    c_gate = proj[..., D:2 * D]
    u = proj[..., 2 * D:]
    z = c_gate * u
    zc = lax.conv_general_dilated(
        z, conv_w[:, None, :].astype(z.dtype), window_strides=(1,),
        padding=[(CONV_WIDTH - 1, 0)],
        dimension_numbers=('NWC', 'WIO', 'NWC'),
        feature_group_count=D)
    return (b_gate * zc) @ w_out

def sq_relu_mlp(h, w_up, w_down):
    return jnp.square(jax.nn.relu(h @ w_up)) @ w_down

def second_inputs(seed: int = 0) -> dict:
    key = jax.random.key(seed)
    ks = jax.random.split(key, 14)
    f32 = jnp.float32
    nrm = lambda k, shape, scale: jax.random.normal(k, shape, f32) * scale
    x = jax.random.normal(ks[0], (BATCH, SEQ, D_MODEL), f32)
    p = jax.random.normal(ks[1], (DEPTH_2, BATCH, SEQ, PLE_DIM), f32)
    norm_g = 1.0 + nrm(ks[2], (DEPTH_2, 6, D_MODEL), 0.05)
    w_attn_in = nrm(ks[3], (N_ATTN, D_MODEL, 3 * D_MODEL + N_HEADS), D_MODEL ** -0.5)
    b_forget = 2.0 + nrm(ks[4], (N_ATTN, N_HEADS), 0.5)
    w_attn_out = nrm(ks[5], (N_ATTN, D_MODEL, D_MODEL), D_MODEL ** -0.5)
    w_conv_in = nrm(ks[6], (N_CONV, D_MODEL, 3 * D_MODEL), D_MODEL ** -0.5)
    conv_w = nrm(ks[7], (N_CONV, CONV_WIDTH, D_MODEL), CONV_WIDTH ** -0.5)
    w_conv_out = nrm(ks[8], (N_CONV, D_MODEL, D_MODEL), D_MODEL ** -0.5)
    w_mlp_up = nrm(ks[9], (DEPTH_2, D_MODEL, D_FF), D_MODEL ** -0.5)
    w_mlp_down = nrm(ks[10], (DEPTH_2, D_FF, D_MODEL), D_FF ** -0.5)
    w_ple_proj = nrm(ks[11], (DEPTH_2, PLE_DIM, D_MODEL), PLE_DIM ** -0.5)
    w_ple_gate = nrm(ks[12], (DEPTH_2, D_MODEL, D_MODEL), D_MODEL ** -0.5)
    return {"x": x, "p": p, "norm_g": norm_g, "w_attn_in": w_attn_in,
            "b_forget": b_forget, "w_attn_out": w_attn_out, "w_conv_in": w_conv_in,
            "conv_w": conv_w, "w_conv_out": w_conv_out, "w_mlp_up": w_mlp_up,
            "w_mlp_down": w_mlp_down, "w_ple_proj": w_ple_proj, "w_ple_gate": w_ple_gate}

def second_block(x, p, norm_g, w_attn_in, b_forget, w_attn_out, w_conv_in, conv_w,
              w_conv_out, w_mlp_up, w_mlp_down, w_ple_proj, w_ple_gate):
    for i in range(DEPTH_2):
        g = norm_g[i]
        hn = rmsnorm_2(x, g[0])
        j = i // N_MIXERS
        if i % N_MIXERS == 0:
            m = fox_attention(hn, w_attn_in[j], b_forget[j], w_attn_out[j])
        else:
            m = short_conv(hn, w_conv_in[j], conv_w[j], w_conv_out[j])
        x = x + rmsnorm_2(m, g[1])
        f = sq_relu_mlp(rmsnorm_2(x, g[2]), w_mlp_up[i], w_mlp_down[i])
        x = x + rmsnorm_2(f, g[3])
        gate = jax.nn.sigmoid(rmsnorm_2(x, g[4]) @ w_ple_gate[i])
        e = (p[i] @ w_ple_proj[i]) * gate
        x = x + rmsnorm_2(e, g[5])
    return x


def setup_inputs(seed=0):
    out = dict(first_inputs(seed))
    for name, value in second_inputs(seed + 1).items():
        if name != "x":
            out[name + "_2"] = value
    return out


def reference(
    x, norm_in_g, w_in, b_gate, q_norm_g, w_q_up, kv_norm_g, w_kv_up, w_o_sb, w_o_mla, w_out,
    norm_f_g, p_2, norm_g_2, w_attn_in_2, b_forget_2, w_attn_out_2, w_conv_in_2, conv_w_2,
    w_conv_out_2, w_mlp_up_2, w_mlp_down_2, w_ple_proj_2, w_ple_gate_2,
):
    x = first_block(
        x, norm_in_g, w_in, b_gate, q_norm_g, w_q_up, kv_norm_g, w_kv_up, w_o_sb, w_o_mla,
        w_out, norm_f_g,
    )
    return second_block(
        x, p_2, norm_g_2, w_attn_in_2, b_forget_2, w_attn_out_2, w_conv_in_2, conv_w_2,
        w_conv_out_2, w_mlp_up_2, w_mlp_down_2, w_ple_proj_2, w_ple_gate_2,
    )


_drawn_inputs = setup_inputs


def setup_inputs(seed=0):
    import zlib

    import numpy as np

    out = dict(_drawn_inputs(seed))
    spreads = {}
    factors = {'norm_in_g': 8.0, 'b_gate': 5.283, 'q_norm_g': 8.0, 'kv_norm_g': 8.0, 'norm_f_g': 4.138}
    for name, (base, spread) in spreads.items():
        noise = np.random.default_rng([zlib.crc32(name.encode()), seed]).standard_normal(out[name].shape)
        drawn = base * np.exp(spread * noise) if base else spread * noise
        out[name] = __import__('jax').numpy.asarray(drawn.astype(out[name].dtype))
    for name, factor in factors.items():
        out[name] = (out[name] * factor).astype(out[name].dtype)
    return out
```

```python
from contextlib import ExitStack

import concourse.bass as bass
import numpy as np
from concourse import mybir

F32 = mybir.dt.float32
F32R = mybir.dt.float32r
ALU = mybir.AluOpType
ACT = mybir.ActivationFunctionType
AX = mybir.AxisListType.X

P = 128
S = 512
D = 1024
KT = D // P
TT = S // P
HD = 64
SB_HEADS = MLA_HEADS = 8
FOX_HEADS = 16
QK = 96
ROPE = 32
Q_LORA, KV_LORA = 384, 256
D_FF = 4096
CHUNK = 64
EPS = 1e-6
FREE = 1
MASKED = -float(2.0 ** 100)
SOFTPLUS_LINEAR = 20.0
UNIT = 2048
CONST_COLS = dict(ident=128, ones=128, sel=16, rope=S, strict=128, tri=128, negones=128, foxmask=384, mlamask=384, sbmask=384)
KEPT = 128 + 128 + 16 + S + 128
CONST_LOADS = 11
CONST_SPLITS = 9


def const_offsets():
    at, out = 0, {}
    for name, n in CONST_COLS.items():
        out[name] = slice(at, at + n)
        at += n
    return out, at


def constants():
    cols, width = const_offsets()
    c = np.zeros((P, width), np.float32)
    row, col = np.arange(P)[:, None], np.arange(P)[None, :]
    c[:, cols["ident"]] = np.eye(P)
    c[:, cols["tri"]] = np.where(row >= col, -1.0, 0.0)
    c[:, cols["negones"]] = -1.0
    c[:, cols["ones"]] = 1.0
    c[:, cols["strict"]] = np.where(row < col, 1.0, 0.0)
    c[:, cols["sbmask"]][:, P:2 * P] = np.where(row < col, 0.0, MASKED)
    c[:, cols["foxmask"]][:, P:2 * P] = np.where(col <= row, 0.0, MASKED)
    c[:, cols["mlamask"]][:, P:2 * P] = np.where(col // CHUNK <= row // CHUNK, 0.0, MASKED)
    for h in range(FOX_HEADS):
        c[h, cols["sel"].start + h] = 1.0
        c[32 + h, cols["sel"].start + h] = 1.0
    half = ROPE // 2
    inv_freq = (np.float32(10000.0) ** (-np.arange(half, dtype=np.float32) / np.float32(half))).astype(np.float32)
    ang = np.arange(S, dtype=np.float32)[None, :] * inv_freq[:, None]
    cos, sin = np.cos(ang), np.sin(ang)
    for base in (0, 64):
        c[base:base + 32, cols["rope"]] = np.concatenate([cos, cos])
        c[base + 32:base + 64, cols["rope"]] = np.concatenate([-sin, sin])
    return c


SB_Q, SB_K, SB_V, SB_GATE, C_Q = 0, 512, 1024, 1536, 2048
K_ROPE = C_Q + Q_LORA + KV_LORA
MLA_GATE = K_ROPE + ROPE
GATES = MLA_GATE + 512

UNIT_GROUPS = [
    ("sb_qk", 4, 2, 1), ("sb_v", 2, 4, 1), ("sb_gate", 2, 2, 1), ("o_sb", 2, 4, 1),
    ("c_qkv", 2, 2, 1), ("c_rope", 1, 2, 3), ("mla_gate", 2, 2, 1), ("q_up", 2, 4, 12), ("kv_up", 1, 12, 1),
    ("o_mla", 2, 4, 1), ("gate0", 4, 2, 1), ("gate1", 4, 2, 1), ("w_out", 4, 2, 1),
    ("fox_qk", 8, 2, 1), ("fox_v", 4, 4, 1), ("fox_out", 4, 2, 1),
    ("ple_proj0", 2, 4, 1), ("mlp0", 32, 2, 1), ("ple_gate0", 4, 2, 1),
    ("conv_in", 12, 2, 1), ("conv_out", 4, 2, 1),
    ("ple_proj1", 2, 4, 1), ("mlp1", 32, 2, 1), ("ple_gate1", 4, 2, 1),
]
EXTRA_TILES = {"sb_qk": 2 + KT, "fox_qk": 1, "ple_proj0": 2, "ple_proj1": 2}


class UnitTable:

    def __init__(self):
        self.first = {}
        self.tile = []
        self.end = []
        self.landed = []
        self.extra = {}
        t, slots = 0, [0, 0]
        for name, n, tiles, dmas in UNIT_GROUPS:
            self.first[name] = len(self.tile)
            self.extra[name] = t
            t += EXTRA_TILES.get(name, 0)
            for _ in range(n):
                self.tile.append(t)
                t += tiles
                self.end.append(t)
                slots[len(self.landed) % 2] += 16 * dmas
                self.landed.append(slots[len(self.landed) % 2])
        self.count = len(self.tile)
        self.tiles = t


class Place:

    def __init__(self, tab, name, j, i=0, per=0, passes=1, ahead=0):
        assert per % 2 == 0
        self.tab, self.i, self.per, self.passes = tab, i, per, passes
        self.at = tab.first[name] + j + ahead
        self.slot = self.at % 2
        self.exists = self.at < tab.count
        self.u = self.at + per * i

    def column(self, column, v):
        step = 0
        if self.passes > 1 and self.per:
            step = column[v + self.per] - column[v]
            assert all(column[v + self.per * n] == column[v] + step * n for n in range(self.passes))
        return column[v] + step * self.i

    @property
    def landed(self):
        return self.column(self.tab.landed, self.at)

    @property
    def tile(self):
        return self.column(self.tab.tile, self.at)

    @property
    def bank(self):
        assert self.passes == 1 or not self.per or (self.tab.tile[self.at + self.per] - self.tab.tile[self.at]) % 4 == 0
        return self.tab.tile[self.at] % 4

    @property
    def freed(self):
        return self.column(self.tab.tile, self.at - 1) if self.at >= 2 else None


class Steps:

    def __init__(self):
        self.n = {}

    def add(self, name, k=1):
        self.n[name] = self.n.get(name, 0) + k
        return self.n[name]

    def __getitem__(self, name):
        return self.n.get(name, 0)


def hybrid_block_kernel(nc, ins, out):
    tab = UnitTable()
    ccols, cwidth = const_offsets()

    ctx = ExitStack()
    with ctx:
        def sb(name, shape, dt=F32):
            return ctx.enter_context(nc.sbuf_tensor(name, shape, dt))

        def sem(name):
            return ctx.enter_context(nc.semaphore(name))

        raw = sb("raw_weights", [P, 2, UNIT])
        wsp = sb("split_weights", [P, 2, 2, UNIT], F32R)
        act_a = sb("act_a", [P, 2, KT, S], F32R)
        act_b = sb("act_b", [P, 2, KT, S], F32R)
        head_qk = sb("head_qk", [P, 4, S], F32R)
        head_v = sb("head_v", [P, 2, 2, TT, HD], F32R)
        decay_row = sb("decay_row", [48, 2, S], F32R)
        consts = sb("consts", [P, KEPT])
        identr = sb("identr", [P, P], F32R)
        trir = sb("trir", [P, P], F32R)
        negonesr = sb("negonesr", [P, P], F32R)
        onesr = sb("onesr", [48, P], F32R)
        maskr = sb("maskr", [P, 3, 384], F32R)
        wf_raw = sb("wf_raw", [P, KT * FOX_HEADS])
        wf = sb("wf", [P, 2, KT, FOX_HEADS], F32R)
        work = sb("work", [P, 32 * S])
        tmp = sb("tmp", [P, 4, S])
        sq = sb("sq", [P, 2, S])
        ssum = sb("ssum", [P, S])
        rstd = sb("rstd", [P, S])
        rstd_tok = sb("rstd_tok", [P, TT])
        gains = sb("gains", [P, 160])
        b_forget = sb("b_forget", [FOX_HEADS, 1])
        eps = sb("eps", [P, 1])
        free_mark = sb("free_mark", [1, 12])
        negmax = sb("negmax", [P, 8])
        rowsum = sb("rowsum", [P, 8])
        rinv = sb("rinv", [P, 8])
        banks = [ctx.enter_context(nc.psum_tensor(f"bank{i}", [P, S], F32)) for i in range(8)]
        x_stash = nc.dram_tensor("x_stash", [P, KT * S], F32, kind="Internal").ap()

        ident = consts[:, ccols["ident"]]
        ones = consts[:, ccols["ones"]]
        rope = consts[:, ccols["rope"]]
        strict = consts[:, ccols["strict"]]
        rest = {name: work[:, 10 * S + at.start - KEPT:10 * S + at.stop - KEPT] for name, at in ccols.items()
                if at.start >= KEPT}

        G_NORM2, G_CONV = 0, 96
        G_IN, G_F, G_BGATE, G_Q, G_KV = 120, 128, 136, 152, 155
        vec_raw = work[:, 8 * S:8 * S + 2 * P].rearrange("p (a n) -> p a n", a=2)

        def wt(i):
            return work[:, bass.ds(i * S, S)]

        X = 24

        def col(c):
            return gains[:, bass.ds(c, 1)]

        const_landed = sem("const_landed")
        x_landed = sem("x_landed")
        raw_landed = [sem("raw_landed0"), sem("raw_landed1")]
        w_hi = sem("w_hi")
        w_split = sem("w_split")
        tile_done = sem("tile_done")
        tile_read = sem("tile_read")
        const_split = sem("const_split")
        prologue_ready = sem("prologue_ready")
        stash_saved = sem("stash_saved")
        stash_back = sem("stash_back")
        sq_done = sem("sq_done")
        sq_zero = sem("sq_zero")
        sq_added = sem("sq_added")
        stat_done = sem("stat_done")
        ln_done = sem("ln_done")
        rstd_ready = sem("rstd_ready")
        rstd_turned = sem("rstd_turned")
        rstd_tok_ready = sem("rstd_tok_ready")
        x_ready = sem("x_ready")
        in_hi = sem("in_hi")
        in_ready = sem("in_ready")
        silu_done = sem("silu_done")
        gate_out = sem("gate_out")
        gated = sem("gated")
        gate_merge = sem("gate_merge")
        merged_hi = sem("merged_hi")
        merged = sem("merged")
        sum_zero = sem("sum_zero")
        conv_pad = sem("conv_pad")
        dve_step = sem("dve_step")
        hid_square = sem("hid_square")
        hid_hi = sem("hid_hi")
        hid_ready = sem("hid_ready")
        pad_zero = sem("pad_zero")
        c_normed = sem("c_normed")
        c_hi = sem("c_hi")
        c_ready = sem("c_ready")
        rope_k = sem("rope_k")
        rope_spread = sem("rope_spread")
        decay_done = sem("decay_done")
        forget_log = sem("forget_log")
        p_landed = sem("p_landed")
        p_split = sem("p_split")
        p_ready = sem("p_ready")
        conv_y = sem("conv_y")
        conv_hi = sem("conv_hi")
        conv_ready = sem("conv_ready")
        out_tile = sem("out_tile")
        out_saved = sem("out_saved")

        ATT = {}
        for kind in ("sb", "mla", "fox"):
            ATT[kind] = {n: sem(f"{kind}_{n}") for n in (
                "q_hi", "stage_hi", "staged", "scores", "turned", "clipped", "softplus", "masked", "part_hi",
                "part_ready", "summed", "w_exp", "w_masked", "negmax", "exp", "normed", "pt_hi", "pt_ready",
                "out", "gathered", "o_hi", "o_ready", "step")}

        block = ctx.enter_context(nc.Block())

        def by_k(w):
            return w.rearrange("(k p) n -> p k n", p=P)

        w_in = by_k(ins["w_in"][0])
        attn_in = by_k(ins["w_attn_in_2"][0])
        conv_in = by_k(ins["w_conv_in_2"][0])

        def slot_of(s, k, n):
            return raw[:, s, 0:k * n].rearrange("p (k n) -> p k n", k=k)

        MASK = {"fox": 0, "mla": 1, "sb": 2}
        STARTS_FREE = {"sb": ("summed", "out", "gathered", "o_ready"),
                       "mla": ("scores", "out", "gathered", "o_ready"),
                       "fox": ("scores", "out", "gathered", "o_ready")}
        STAGES = {"fox": 4, "mla": 3}

        def qk_main(a):
            return head_qk[:, a, :]

        def qk_spare(a):
            return act_b[:, a // 2, 4 + a % 2, :]

        QK_PARTS = {"fox": (qk_main, qk_spare), "mla": (qk_main, qk_main), "sb": (qk_main, qk_main)}
        PE_ORDER = {
            "fox": "z0 z1 z2 t0 z3 t1 z4 t2 z5 t3 z6 t4 v0 z7 t5 t6 t7 v1",
            "mla": "z0 z1 z2 t0 z3 t1 t2 t3 z4 z5 v0 z6 t4 z7 t5 t6 t7 v1",
        }
        ACT_ORDER = {
            "fox": "s0 e0 s1 e1 e2 p0 e3 p1 e4 p2 e5 p3 e6 p4 e7 p5 p6 p7 o0",
            "mla": "s0 e0 e1 e2 p0 e3 p1 s1 p2 p3 e4 e5 e6 p4 e7 p5 p6 p7 o0",
        }
        DVE_ORDER = {
            "fox": "s0 m0 m1 n0 m2 s1 n1 p0 m3 n2 p1 m4 n3 p2 m5 n4 p3 m6 n5 p4 m7 n6 g0 p5 n7 p6 p7 g1 o0",
            "mla": "s0 m0 m1 n0 m2 n1 p0 m3 n2 p1 n3 s1 p2 p3 m4 m5 n4 m6 g0 n5 p4 m7 n6 p5 n7 p6 p7 g1 o0",
        }

        def steps(order):
            return [(w[0], int(w[1:])) for w in order.split()]

        TILES = {"sb": dict(q=8, k=12, v=16, gate=20), "mla": dict(q=12, k=24, v=20, gate=8), "fox": dict(q=0, k=8, v=16)}
        SCALE = {"sb": HD ** -0.5, "fox": HD ** -0.5, "mla": QK ** -0.5}

        def head_rows(kind, which, i, hh):
            if kind == "mla":
                return wt(TILES[kind][which] + 2 * i + hh)[0:QK, :]
            return wt(TILES[kind][which] + i)[hh * HD:(hh + 1) * HD, :]

        def head_values(kind, i, hh):
            width = (FOX_HEADS if kind == "fox" else SB_HEADS) * HD
            v = work[:, TILES[kind]["v"] * S:TILES[kind]["v"] * S + TT * width].rearrange("p (a n) -> p a n", a=TT)
            return v[:, :, bass.ds(2 * HD * i + hh * HD, HD)]

        gathered_o = sq[:, 0, :]

        def out_parts(kind, hl, i):
            if kind == "fox":
                return act_a[:, hl, bass.ds(i, 1), :].rearrange("p a n -> p (a n)")
            return act_b[:, hl, bass.ds(4 + i, 1), :].rearrange("p a n -> p (a n)")

        def valid(kt):
            return slice(kt * P, S)

        def stick_hi(act, A, h, r, offset):
            kt = TT - 1 - r
            act.wait_ge(A["w_exp" if offset else "masked"], 4 * h + r + 1)
            if r == 0 and offset == 0:
                act.wait_ge(A["out"], FREE + h)
            if r == 0 and offset:
                act.wait_ge(A["summed"], FREE + 4 * h + TT)
            nc.scalar.activation(act_b[:, 0, kt, valid(kt)], tmp[:, kt, valid(kt)], ACT.Copy).then_inc(A["part_hi"], 1)

        @block.sync
        def _(sp):
            def load(pl, dst, src, first=True):
                if first and pl.at >= 2:
                    sp.wait_ge(w_split, pl.u - 1)
                    sp.nop(nofuse=True)
                sp.dma_start(dst, src).then_inc(raw_landed[pl.slot], 16)

            def loop(name, passes, per, source, k=KT, n=256):
                with sp.Fori(0, passes) as i:
                    for j in range(per):
                        pl = Place(tab, name, j, i, per, passes)
                        load(pl, slot_of(pl.slot, k, n), source(i, j))

            sp.dma_start(work[:, 0:8 * S].rearrange("p (a n) -> p a n", a=TT),
                         ins["x"][0].rearrange("(a p) n -> p a n", p=P)).then_inc(x_landed, 16)
            sp.dma_start(consts[:, :], ins["consts"][:, 0:KEPT]).then_inc(const_landed, 16)
            sp.dma_start(work[:, 10 * S:10 * S + cwidth - KEPT], ins["consts"][:, KEPT:cwidth]).then_inc(const_landed, 16)

            def rows(v, n):
                return v.rearrange("(k p) -> k p", p=P)[0:n, :]

            sp.dma_start(vec_raw[0:96, 0, :], ins["norm_g_2"].rearrange("l n (k p) -> (l n k) p", p=P))\
                .then_inc(const_landed, 16)
            sp.dma_start(vec_raw[96:120, 0, :], ins["conv_w_2"][0].rearrange("j (k p) -> (j k) p", p=P))\
                .then_inc(const_landed, 16)
            at = 0
            for name, n in (("norm_in_g", 8), ("norm_f_g", 8), ("b_gate", 16), ("q_norm_g", 3), ("kv_norm_g", 2)):
                v = ins[name] if name == "norm_f_g" else ins[name][0]
                sp.dma_start(vec_raw[at:at + n, 1, :], rows(v, n)).then_inc(const_landed, 16)
                at += n
            sp.dma_start(b_forget[:, :], ins["b_forget_2"].rearrange("a h -> h a")).then_inc(const_landed, 16)
            sp.dma_start(wf_raw[:, :].rearrange("p (k n) -> p k n", k=KT),
                         attn_in[:, :, 3 * D:3 * D + FOX_HEADS]).then_inc(const_landed, 16)

            def w_in_cols(c):
                return lambda i, j: w_in[:, :, bass.ds(c + 512 * i + 256 * j, 256)]

            for j in range(2):
                load(Place(tab, "sb_qk", j), slot_of(j, KT, 256), w_in_cols(SB_Q)(0, j))
            with sp.Fori(1, 2) as i:
                for j in range(2):
                    pl = Place(tab, "sb_qk", j, i, 2, 2)
                    sp.wait_ge(w_split, pl.u - 1)
                    sp.nop(nofuse=True)
                    sp.dma_start(slot_of(pl.slot, KT, 256), w_in_cols(SB_Q)(i, j)).then_inc(raw_landed[pl.slot], 16)
            sp.wait_ge(in_ready, KT)
            sp.dma_start(x_stash, work[:, X * S:(X + KT) * S]).then_inc(stash_saved, 16)
            loop("sb_v", 1, 2, w_in_cols(SB_V))
            loop("sb_gate", 1, 2, w_in_cols(SB_GATE))
            o_sb = by_k(ins["w_o_sb"][0])
            loop("o_sb", 1, 2, lambda i, j: o_sb[:, :, 512 * j:512 * j + 512], k=4, n=512)
            for j in range(2):
                pl = Place(tab, "c_qkv", j)
                load(pl, slot_of(pl.slot, KT, 256), w_in[:, :, C_Q + 256 * j:C_Q + 256 * j + 256])
            pl = Place(tab, "c_rope", 0)
            dst = slot_of(pl.slot, KT, 192)
            load(pl, dst[:, :, 0:160], w_in[:, :, C_Q + 512:MLA_GATE])
            load(pl, dst[:, :, 160:176], w_in[:, :, K_ROPE + 16:K_ROPE + 32], first=False)
            load(pl, dst[:, :, 176:192], w_in[:, :, K_ROPE:K_ROPE + 16], first=False)
            for j in range(2):
                pl = Place(tab, "mla_gate", j)
                load(pl, slot_of(pl.slot, KT, 256), w_in[:, :, MLA_GATE + 256 * j:MLA_GATE + 256 * j + 256])
            q_up = ins["w_q_up"][0].rearrange("(k p) n -> p k n", p=P)
            for j in range(2):
                pl = Place(tab, "q_up", j)
                for h in range(4):
                    src = q_up[:, :, QK * (4 * j + h):QK * (4 * j + h + 1)]
                    dst = raw[:, pl.slot, 0:3 * 512].rearrange("p (k h n) -> p k h n", k=3, h=4)[:, :, h, :]
                    if h == 0:
                        load(pl, dst[:, :, 0:96], src)
                    else:
                        load(pl, dst[:, :, 0:96], src, first=False)
                    load(pl, dst[:, :, 96:112], src[:, :, 80:96], first=False)
                    load(pl, dst[:, :, 112:128], src[:, :, 64:80], first=False)
            kv_up = ins["w_kv_up"][0].rearrange("(k p) n -> p k n", p=P)
            pl = Place(tab, "kv_up", 0)
            load(pl, slot_of(pl.slot, 2, 1024), kv_up)
            sp.wait_ge(rope_k, 1)
            sp.wait_ge(c_ready, 5)
            for h in range(MLA_HEADS):
                sp.dma_start(work[64:96, (24 + h) * S:(25 + h) * S], tmp[0:32, 2, :]).then_inc(rope_spread, 16)
            o_mla = by_k(ins["w_o_mla"][0])
            loop("o_mla", 1, 2, lambda i, j: o_mla[:, :, 512 * j:512 * j + 512], k=4, n=512)
            loop("gate0", 2, 2, w_in_cols(GATES))
            sp.wait_ge(ATT["mla"]["o_ready"], FREE + MLA_HEADS // 2)
            sp.dma_start(work[:, X * S:(X + KT) * S], x_stash).then_inc(stash_back, 16)
            loop("gate1", 2, 2, w_in_cols(GATES + D))
            w_out = by_k(ins["w_out"][0])
            loop("w_out", 2, 2, lambda i, j: w_out[:, :, bass.ds(512 * i + 256 * j, 256)])

            def mlp(layer):
                up = by_k(ins["w_mlp_up_2"][layer])
                down = ins["w_mlp_down_2"][layer].rearrange("(c k p) n -> p c k n", p=P, k=KT)
                chunks = D_FF // D

                def source(i, j):
                    if j < 4:
                        return up[:, :, bass.ds(D * i + 256 * j, 256)]
                    return down[:, bass.ds(i, 1), :, 256 * (j - 4):256 * (j - 3)].rearrange("p a k n -> p (a k) n")

                loop(f"mlp{layer}", chunks, 8, source)

            def embedding(layer):
                sp.dma_start(work[:, 16 * S:18 * S].rearrange("p (a n) -> p a n", a=TT),
                             ins["p_2"][layer, 0].rearrange("(a p) n -> p a n", p=P)).then_inc(p_landed, 16)

            def embed_project(layer):
                proj = ins["w_ple_proj_2"][layer].rearrange("(k p) n -> p k n", p=P)
                loop(f"ple_proj{layer}", 1, 2, lambda i, j: proj[:, :, 512 * j:512 * j + 512], k=2, n=512)

            def embed_gate(layer):
                gate = by_k(ins["w_ple_gate_2"][layer])
                loop(f"ple_gate{layer}", 2, 2, lambda i, j: gate[:, :, bass.ds(512 * i + 256 * j, 256)])

            loop("fox_qk", 4, 2, lambda i, j: attn_in[:, :, bass.ds(512 * i + 256 * j, 256)])
            loop("fox_v", 2, 2, lambda i, j: attn_in[:, :, bass.ds(2 * D + 512 * i + 256 * j, 256)])
            fox_out = by_k(ins["w_attn_out_2"][0])
            for j in range(2):
                pl = Place(tab, "fox_out", j)
                load(pl, slot_of(pl.slot, KT, 256), fox_out[:, :, 256 * j:256 * j + 256])
            sp.wait_ge(ATT["fox"]["staged"], 4 * FOX_HEADS)
            embedding(0)
            for j in range(2, 4):
                pl = Place(tab, "fox_out", j)
                load(pl, slot_of(pl.slot, KT, 256), fox_out[:, :, 256 * j:256 * j + 256])
            embed_project(0)
            mlp(0)
            embed_gate(0)

            sp.wait_ge(x_ready, 3 * KT)
            embedding(1)

            def conv_source(i, j):
                part, half = j % 3, j // 3
                return conv_in[:, :, bass.ds((D, 2 * D, 0)[part] + 512 * i + 256 * half, 256)]

            loop("conv_in", 2, 6, conv_source)
            conv_out = by_k(ins["w_conv_out_2"][0])
            loop("conv_out", 2, 2, lambda i, j: conv_out[:, :, bass.ds(512 * i + 256 * j, 256)])
            embed_project(1)
            mlp(1)
            embed_gate(1)

            for n in range(TT):
                sp.wait_ge(tile_read, tab.tiles + 2 * (n + 1))
                sp.dma_start(out[0, n * P:(n + 1) * P, :], work[:, 2 * n * S:2 * (n + 1) * S]).then_inc(out_saved, 16)
            sp.wait_ge(out_saved, 16 * TT)

        @block.tensor
        def _(pe):
            n = Steps()

            def weights(pl, hl, a, b):
                return wsp[:, pl.slot, hl, a:b]

            def bank(pl, m):
                return banks[(pl.bank + m) % 4]

            def empty(tile, m=0):
                if not isinstance(tile, int) or tile + m >= 4:
                    pe.wait_ge(tile_read, tile + m - 3)

            def three(dst, w, a, first, last, done=None):
                nc.tensor.matmul(dst, w[0], a[0], start=first, stop=False)
                nc.tensor.matmul(dst, w[0], a[1], start=False, stop=False)
                mm = nc.tensor.matmul(dst, w[1], a[0], start=False, stop=last)
                if done is not None:
                    mm.then_inc(done, 1)

            def unit(pl, k_tiles, width, m_tiles, x, ready=None):
                pe.wait_ge(w_split, pl.u + 1)
                for m in range(m_tiles):
                    empty(pl.tile, m)
                for k in range(k_tiles):
                    if ready:
                        pe.wait_ge(ready[0], ready[1] + k + 1)
                    for m in range(m_tiles):
                        c = k * width + m * P
                        three(bank(pl, m)[:, :], [weights(pl, hl, c, c + P) for hl in (0, 1)],
                              [x(hl, k) for hl in (0, 1)], k == 0, k == k_tiles - 1,
                              tile_done if k == k_tiles - 1 else None)

            def unit_tokens(pl, k_tiles, x, cols, rhs, skip=0):
                pe.wait_ge(w_split, pl.u + 1)
                for a in range(TT):
                    empty(pl.tile, skip + a)
                    for k in range(k_tiles):
                        three(bank(pl, skip + a)[:, 0:cols], [x(hl, k)[:, a * P:(a + 1) * P] for hl in (0, 1)],
                              [rhs(hl, k) for hl in (0, 1)], k == 0, k == k_tiles - 1,
                              tile_done if k == k_tiles - 1 else None)

            def from_a(hl, k):
                return act_a[:, hl, k, :]

            def from_b(hl, k):
                return act_b[:, hl, k, :]

            def upper_b(hl, k):
                return act_b[:, hl, 4 + k, :]

            def project(name, passes, x, ready=None, stats=False):
                first = 0
                if stats:
                    unit(Place(tab, name, 0), KT, 256, 2, x, ready)
                    statistics(KT)
                    unit(Place(tab, name, 1), KT, 256, 2, x)
                    first = 1
                with pe.Fori(first, passes) as i:
                    for j in range(2):
                        unit(Place(tab, name, j, i, 2, passes), KT, 256, 2, x, ready if j == 0 and not stats else None)

            def statistics(tiles):
                pe.wait_ge(sq_added, n.add("sq", tiles))
                if n["stat"]:
                    pe.wait_ge(rstd_ready, n["stat"])
                if n["turned"]:
                    pe.wait_ge(rstd_tok_ready, n["turned"])
                nc.tensor.matmul(banks[7][:, :], ones, ssum[:, :], start=True, stop=True).then_inc(stat_done, 1)
                n.add("stat")

            def turn_rstd():
                pe.wait_ge(rstd_ready, n["stat"])
                for a in range(TT):
                    mm = nc.tensor.matmul(banks[7][:, a:a + 1], rstd[0:1, a * P:(a + 1) * P], ones[0:1, 0:1],
                                          start=a == 0, stop=a == TT - 1)
                mm.then_inc(rstd_turned, 1)
                n.add("turned")

            tile = tab.extra["sb_qk"]
            pe.wait_ge(const_landed, 16 * CONST_LOADS)
            for r, rows in ((0, 120), (1, 37)):
                nc.tensor.transpose(banks[tile % 4][:, 0:rows], vec_raw[0:rows, r, :], ident[0:rows, 0:rows])\
                    .then_inc(tile_done, 1)
                tile += 1
            pe.wait_ge(x_landed, 16)
            for k in range(KT):
                empty(tile)
                for a in range(TT):
                    tr = nc.tensor.transpose(banks[tile % 4][:, a * P:(a + 1) * P],
                                             work[:, a * D + k * P:a * D + (k + 1) * P], ident)
                tr.then_inc(tile_done, 1)
                tile += 1

            project("sb_qk", 2, from_a, (in_ready, 0), stats=True)
            turn_rstd()
            for j in range(2):
                pl = Place(tab, "sb_v", j)
                unit_tokens(pl, KT, from_a, 256, lambda hl, k: weights(pl, hl, k * 256, (k + 1) * 256))
            for j in range(2):
                unit(Place(tab, "sb_gate", j), KT, 256, 2, from_a)

            A = ATT["sb"]
            pe.wait_ge(pad_zero, 1)
            pe.wait_ge(const_split, CONST_SPLITS)
            with pe.Fori(0, SB_HEADS // 2) as i:
                for hh in range(2):
                    h = 2 * i + hh
                    pe.wait_ge(A["staged"], 3 * h + 3)

                    def scores(kt, last, done=None):
                        c = min(kt * P, S - 2 * P)
                        three(banks[kt][:, c:S], [head_qk[0:HD, 2 + hl, kt * P:(kt + 1) * P] for hl in (0, 1)],
                              [head_qk[0:HD, hl, c:S] for hl in (0, 1)], True, last, done)

                    for kt in reversed(range(TT)):
                        scores(kt, True, A["scores"])
                    for kt in reversed(range(TT)):
                        pe.wait_ge(A["part_ready"], 8 * h + TT - kt)
                        scores(kt, False)
                        for later in range(kt, TT):
                            c = min(later * P, S - 2 * P)
                            m = trir if later == kt else negonesr
                            for hl in (0, 1):
                                nc.tensor.matmul(banks[kt][:, c:S], m[:, :], act_b[:, hl, later, c:S],
                                                 start=False, stop=False)
                        c = min(kt * P, S - 2 * P)
                        m = maskr[:, MASK["sb"], 0:2 * P] if kt == TT - 1 else maskr[:, MASK["sb"], P:3 * P]
                        nc.tensor.matmul(banks[kt][:, c:c + 2 * P], identr[:, :], m, start=False, stop=True)\
                            .then_inc(A["summed"], 1)
                    pe.wait_ge(A["part_ready"], 8 * h + 8)
                    pe.wait_ge(A["gathered"], FREE + 2 * i)
                    for kt in range(TT):
                        c = min(kt * P, S - 2 * P)
                        three(banks[4 + hh][0:HD, c:S], [head_v[:, hh, hl, kt, :] for hl in (0, 1)],
                              [act_b[:, hl, kt, c:S] for hl in (0, 1)], kt == 0, kt == TT - 1,
                              A["out"] if kt == TT - 1 else None)
            pe.wait_ge(A["o_ready"], FREE + SB_HEADS // 2)
            for j in range(2):
                unit(Place(tab, "o_sb", j), 4, 512, 4, upper_b)

            for j in range(2):
                unit(Place(tab, "c_qkv", j), KT, 256, 2, from_a)
            pl = Place(tab, "c_rope", 0)
            pe.wait_ge(w_split, pl.u + 1)
            for m, rows in ((0, P), (1, 64)):
                empty(pl.tile, m)
                for k in range(KT):
                    c = k * 192 + m * P
                    three(bank(pl, m)[0:rows, :], [weights(pl, hl, c, c + rows) for hl in (0, 1)],
                          [from_a(hl, k) for hl in (0, 1)], k == 0, k == KT - 1, tile_done if k == KT - 1 else None)
            unit(Place(tab, "mla_gate", 0), KT, 256, 2, from_a)
            statistics(3)
            statistics(2)
            unit(Place(tab, "mla_gate", 1), KT, 256, 2, from_a)
            for j in range(2):
                unit(Place(tab, "q_up", j), 3, 512, 4, from_b, (c_ready, 0) if j == 0 else None)
            pl = Place(tab, "kv_up", 0)
            pe.wait_ge(w_split, pl.u + 1)
            pe.wait_ge(c_ready, 5)
            for h in range(MLA_HEADS):
                empty(pl.tile, h)
                for k in range(2):
                    c = k * 1024 + h * P
                    three(bank(pl, h)[0:HD, :], [weights(pl, hl, c, c + HD) for hl in (0, 1)],
                          [upper_b(hl, k) for hl in (0, 1)], k == 0, k == 1, tile_done if k == 1 else None)

            def v_cols(hl, k):
                return weights(pl, hl, k * 1024, (k + 1) * 1024).rearrange("p (h c) -> p h c", h=8)[:, :, HD:P]

            unit_tokens(pl, 2, upper_b, S, v_cols, skip=MLA_HEADS)

            def softmax_attention(kind, heads, width):
                A = ATT[kind]
                mask = maskr[:, MASK[kind], :]
                stages = STAGES[kind]

                def scores(i, s):
                    hh, j = divmod(s, TT)
                    qk = QK_PARTS[kind][hh]
                    if j == 0:
                        pe.wait_ge(A["staged"], stages * (2 * i + hh) + stages)
                    cols = max((j + 1) * P, 2 * P)
                    dst = banks[s % 4][:, 0:cols]
                    for pass_, (a, b) in enumerate(((0, 2), (0, 3), (1, 2))):
                        nc.tensor.matmul(dst, qk(a)[0:width, j * P:(j + 1) * P], qk(b)[0:width, 0:cols],
                                         start=pass_ == 0, stop=False)
                    if kind == "fox":
                        nc.tensor.matmul(dst, onesr[:, :], decay_row[:, hh, 0:cols], start=False, stop=False)
                    c = max(j - 1, 0) * P
                    m = mask[:, P:3 * P] if j == 0 else mask[:, 0:2 * P]
                    nc.tensor.matmul(banks[s % 4][:, c:c + 2 * P], identr[:, :], m, start=False, stop=True)\
                        .then_inc(A["scores"], 1)

                def turn(i, s):
                    pe.wait_ge(A["normed"], 8 * i + s + 1)
                    if s >= 2:
                        pe.wait_ge(A["pt_ready"], 8 * i + s - 1)
                    for b in range(s % TT + 1):
                        tr = nc.tensor.transpose(banks[4 + s % 2][:, b * P:(b + 1) * P],
                                                 tmp[:, s % 4, b * P:(b + 1) * P], ident)
                    tr.then_inc(A["turned"], 1)

                def values(i, hh):
                    pe.wait_ge(A["pt_ready"], 8 * i + 4 * hh + 4)
                    pe.wait_ge(A["gathered"], FREE + 2 * i)
                    for kt in range(TT):
                        c = min(kt * P, S - 2 * P)
                        three(banks[6 + hh][0:HD, c:S], [head_v[:, hh, hl, kt, :] for hl in (0, 1)],
                              [act_b[:, hl, kt, c:S] for hl in (0, 1)], kt == 0, kt == TT - 1,
                              A["out"] if kt == TT - 1 else None)

                with pe.Fori(0, heads // 2) as i:
                    for what, s in steps(PE_ORDER[kind]):
                        {"z": scores, "t": turn, "v": values}[what](i, s)

            pe.wait_ge(pad_zero, 2)
            softmax_attention("mla", MLA_HEADS, QK)
            pe.wait_ge(ATT["mla"]["o_ready"], FREE + MLA_HEADS // 2)
            for j in range(2):
                unit(Place(tab, "o_mla", j), 4, 512, 4, upper_b)
            project("gate0", 2, from_a)
            project("gate1", 2, from_a)
            project("w_out", 2, from_b, (merged, 0))
            statistics(KT)

            n.add("in", KT)
            tile = tab.extra["fox_qk"]
            empty(tile)
            for k in range(KT):
                pe.wait_ge(in_ready, n["in"] + k + 1)
                three(banks[tile % 4][0:FOX_HEADS, :], [wf[:, hl, k, :] for hl in (0, 1)],
                      [from_a(hl, k) for hl in (0, 1)], k == 0, k == KT - 1, tile_done if k == KT - 1 else None)
            n.add("in", KT)
            statistics(KT)
            project("fox_qk", 4, from_a)
            turn_rstd()
            with pe.Fori(0, 2) as i:
                for j in range(2):
                    pl = Place(tab, "fox_v", j, i, 2, 2)
                    unit_tokens(pl, KT, from_a, 256, lambda hl, k: weights(pl, hl, k * 256, (k + 1) * 256))
            pe.wait_ge(pad_zero, 3)
            softmax_attention("fox", FOX_HEADS, HD)
            pe.wait_ge(ATT["fox"]["o_ready"], FREE + FOX_HEADS // 2)
            project("fox_out", 2, from_a)

            def embed_project(layer):
                tile = tab.extra[f"ple_proj{layer}"]
                pe.wait_ge(p_landed, 16 * (layer + 1))
                for k in range(2):
                    empty(tile)
                    for a in range(TT):
                        c = 16 * S + a * 256 + k * P
                        tr = nc.tensor.transpose(banks[tile % 4][:, a * P:(a + 1) * P], work[:, c:c + P], ident)
                    tr.then_inc(tile_done, 1)
                    tile += 1

                def embedding(hl, k):
                    return head_qk[:, 2 * hl + k, :]

                unit(Place(tab, f"ple_proj{layer}", 0), 2, 512, 4, embedding, (p_ready, 2 * layer))
                statistics(KT)
                unit(Place(tab, f"ple_proj{layer}", 1), 2, 512, 4, embedding)

            def mlp(layer):
                chunks = D_FF // D
                base = n.add("in", KT) - KT
                hid = n.add("hid", KT * chunks) - KT * chunks

                def chunk(i, first=False):
                    for j in range(8):
                        pl = Place(tab, f"mlp{layer}", j, i, 8, chunks)
                        if j < 4:
                            unit(pl, KT, 256, 2, from_a, (in_ready, base) if first and j == 0 else None)
                        else:
                            unit(pl, KT, 256, 2, from_b, (hid_ready, hid + KT * i) if j == 4 else None)
                        if first and j == 0:
                            statistics(KT)

                chunk(0, first=True)
                with pe.Fori(1, chunks - 1) as i:
                    chunk(i)
                chunk(chunks - 1)
                statistics(KT)

            def embed_gate(layer):
                project(f"ple_gate{layer}", 2, from_a, (in_ready, n.add("in", KT) - KT), stats=True)
                statistics(KT)

            embed_project(0)
            mlp(0)
            embed_gate(0)

            base = n.add("in", KT) - KT
            unit(Place(tab, "conv_in", 0), KT, 256, 2, from_a, (in_ready, base))
            statistics(KT)
            for j in range(1, 6):
                unit(Place(tab, "conv_in", j), KT, 256, 2, from_a)
            for j in range(6, 12):
                unit(Place(tab, "conv_in", j), KT, 256, 2, from_a)
            project("conv_out", 2, from_b, (conv_ready, 0))
            embed_project(1)
            mlp(1)
            embed_gate(1)

            tile = tab.tiles
            pe.wait_ge(x_ready, 7 * KT)
            for a in range(TT):
                for half in range(2):
                    empty(tile)
                    for k in range(4):
                        tr = nc.tensor.transpose(banks[tile % 4][:, k * P:(k + 1) * P],
                                                 wt(X + 4 * half + k)[:, a * P:(a + 1) * P], ident)
                    tr.then_inc(tile_done, 1)
                    tile += 1

        @block.scalar
        def _(act):
            n = Steps()

            def table(name):
                nc.scalar.preload_act_table_set(name)

            def split(pl):
                if not pl.exists:
                    return
                act.wait_ge(raw_landed[pl.slot], pl.landed)
                if pl.freed is not None:
                    act.wait_ge(tile_done, pl.freed)
                nc.scalar.activation(wsp[:, pl.slot, 0, :], raw[:, pl.slot, :], ACT.Copy).then_inc(w_hi, 1)

            def ahead(name, j, i=0, per=0, passes=1):
                split(Place(tab, name, j, i, per, passes, ahead=1))

            def square(src, at, parity):
                if not isinstance(at, int) or at >= 2:
                    act.wait_ge(sq_added, at - 1)
                nc.scalar.activation(sq[:, parity, :], src, ACT.Square).then_inc(sq_done, 1)

            def norm_input(gain, first=False):
                base, x0 = n["in"], n["x"]
                for k in range(KT):
                    if first:
                        act.wait_ge(tile_read, 2 + k + 1)
                    else:
                        act.wait_ge(x_ready, x0 + k + 1)
                    nc.scalar.activation(act_a[:, 0, k, :], wt(X + k), ACT.Copy, scale=col(gain + k)).then_inc(in_hi, 1)
                    square(wt(X + k), n["sq"] + k, (n["sq"] + k) % 2)
                n.add("in", KT)
                n.add("sq", KT)
                if not first:
                    n.add("x", KT)

            def make_rstd(dst, width):
                act.wait_ge(stat_done, n.add("stat"))
                nc.scalar.activation(dst, banks[7][:, :], ACT.Ln, bias=eps[:, :], scale=1.0 / width).then_inc(ln_done, 1)
                act.wait_ge(ln_done, n["stat"])
                nc.scalar.activation(dst, dst, ACT.Exp, scale=-0.5).then_inc(rstd_ready, 1)

            def squares_of(name, tiles_at, passes, per=2):
                base, t0 = n["sq"], tab.tile[tab.first[name]]
                with act.Fori(0, passes) as i:
                    for j in range(per):
                        ahead(name, j, i, per, passes)
                        pl = Place(tab, name, j, i, per, passes)
                        for m in range(2):
                            act.wait_ge(tile_read, pl.tile + m + 1)
                            square(wt(tiles_at + 4 * i + 2 * j + m), base + 4 * i + 2 * j + m, (base + m) % 2)
                n.add("sq", 2 * per * passes)

            def splits(name, passes, per=2):
                with act.Fori(0, passes) as i:
                    for j in range(per):
                        ahead(name, j, i, per, passes)

            table("natural_log_exp_and_others")
            act.wait_ge(prologue_ready, 1)
            act.wait_ge(tile_read, 2)
            norm_input(G_IN, first=True)
            split(Place(tab, "sb_qk", 0))
            ahead("sb_qk", 0)
            make_rstd(rstd[:, :], D)
            for j in range(1, 4):
                ahead("sb_qk", j)
            for j in range(2):
                ahead("sb_v", j)
            table("sigmoid_and_others")
            for j in range(2):
                ahead("sb_gate", j)
                pl = Place(tab, "sb_gate", j)
                for m in range(2):
                    act.wait_ge(tile_read, pl.tile + m + 1)
                    if j:
                        act.wait_ge(silu_done, m + 1)
                    nc.scalar.activation(tmp[:, m, :], wt(20 + 2 * j + m), ACT.Sigmoid).then_inc(gate_out, 1)
            table("natural_log_exp_and_others")

            def stage(kind, i, hh):
                A = ATT[kind]
                qk = QK_PARTS[kind][hh]
                rows = QK if kind == "mla" else HD
                act.wait_ge(A["summed" if kind == "sb" else "scores"], FREE + 8 * i + (0 if hh == 0 or kind == "fox" else TT))
                nc.scalar.activation(qk(0)[0:rows, :], head_rows(kind, "q", i, hh), ACT.Copy, scale=SCALE[kind])\
                    .then_inc(A["stage_hi"], 1)
                nc.scalar.activation(qk(2)[0:rows, :], head_rows(kind, "k", i, hh), ACT.Copy).then_inc(A["stage_hi"], 1)
                if hh == 1 or kind == "sb":
                    act.wait_ge(A["out"], FREE + 2 * i)
                nc.scalar.activation(head_v[:, hh, 0, :, :], head_values(kind, i, hh), ACT.Copy).then_inc(A["stage_hi"], 1)

            A = ATT["sb"]
            act.wait_ge(tile_read, tab.end[tab.first["sb_v"] + 1])
            with act.Fori(0, SB_HEADS // 2) as i:
                for hh in range(2):
                    h = 2 * i + hh
                    stage("sb", i, hh)
                    for r, kt in enumerate(reversed(range(TT))):
                        t = tmp[:, kt, valid(kt)]
                        act.wait_ge(A["clipped"], 4 * h + r + 1)
                        nc.scalar.activation(t, t, ACT.Exp).then_inc(A["exp"], 1)
                        act.wait_ge(A["exp"], 4 * h + r + 1)
                        nc.scalar.activation(t, t, ACT.Ln, bias=1.0).then_inc(A["softplus"], 1)
                        if r:
                            stick_hi(act, A, h, r - 1, 0)
                    stick_hi(act, A, h, TT - 1, 0)
                    for r, kt in enumerate(reversed(range(TT))):
                        act.wait_ge(A["summed"], FREE + 4 * h + r + 1)
                        nc.scalar.activation(tmp[:, kt, valid(kt)], banks[kt][:, valid(kt)], ACT.Exp).then_inc(A["w_exp"], 1)
                        if r:
                            stick_hi(act, A, h, r - 1, TT)
                    stick_hi(act, A, h, TT - 1, TT)
                act.wait_ge(A["gathered"], FREE + 2 * i + 2)
                nc.scalar.activation(out_parts("sb", 0, i), gathered_o, ACT.Copy).then_inc(A["o_hi"], 1)

            for j in range(2):
                ahead("o_sb", j)
            latents = tab.tile[tab.first["c_qkv"]]
            for j in range(2):
                ahead("c_qkv", j)
                if j == 1:
                    for k in range(2):
                        act.wait_ge(tile_read, latents + k + 1)
                        square(wt(24 + k), n["sq"], n["sq"] % 2)
                        n.add("sq")
            ahead("c_rope", 0)
            for k in range(2, 5):
                act.wait_ge(tile_read, latents + k + 1)
                square(wt(24 + k), n["sq"], n["sq"] % 2)
                n.add("sq")
            ahead("mla_gate", 0)
            make_rstd(wt(29), Q_LORA)
            make_rstd(wt(30), KV_LORA)
            for k in range(5):
                act.wait_ge(c_normed, k + 1)
                dst = act_b[:, 0, k if k < 3 else k + 1, :]
                nc.scalar.activation(dst, wt(24 + k), ACT.Copy).then_inc(c_hi, 1)
            ahead("mla_gate", 1)
            table("sigmoid_and_others")
            for m in range(4):
                act.wait_ge(tile_read, Place(tab, "mla_gate", m // 2).tile + m % 2 + 1)
                if m >= 2:
                    act.wait_ge(silu_done, 4 + m - 1)
                nc.scalar.activation(tmp[:, m % 2, :], wt(8 + m), ACT.Sigmoid).then_inc(gate_out, 1)
            table("natural_log_exp_and_others")
            for j in range(2):
                ahead("q_up", j)
            ahead("kv_up", 0)

            def softmax_attention(kind, heads):
                A = ATT[kind]

                def exponentials(i, s):
                    j = s % TT
                    act.wait_ge(A["negmax"], 8 * i + s + 1)
                    nc.scalar.activation(tmp[:, s % 4, 0:(j + 1) * P], banks[s % 4][:, 0:(j + 1) * P], ACT.Exp,
                                         bias=negmax[:, s:s + 1], accum_out=rowsum[:, s:s + 1]).then_inc(A["exp"], 1)

                def turned_hi(i, s):
                    hh, j = divmod(s, TT)
                    act.wait_ge(A["turned"], 8 * i + s + 1)
                    if j == 0:
                        act.wait_ge(A["out"], FREE + 2 * i + hh)
                    src = banks[4 + s % 2][:, 0:(j + 1) * P].rearrange("p (b n) -> p b n", b=j + 1)
                    nc.scalar.activation(act_b[:, 0, 0:j + 1, j * P:(j + 1) * P], src, ACT.Copy).then_inc(A["pt_hi"], 1)

                def output_hi(i, _):
                    act.wait_ge(A["gathered"], FREE + 2 * i + 2)
                    nc.scalar.activation(out_parts(kind, 0, i), gathered_o, ACT.Copy).then_inc(A["o_hi"], 1)

                with act.Fori(0, heads // 2) as i:
                    for what, s in steps(ACT_ORDER[kind]):
                        {"s": lambda i, s: stage(kind, i, s), "e": exponentials, "p": turned_hi, "o": output_hi}[what](i, s)

            act.wait_ge(tile_read, tab.end[tab.first["kv_up"]])
            act.wait_ge(rope_spread, 16 * MLA_HEADS)
            softmax_attention("mla", MLA_HEADS)
            for j in range(2):
                ahead("o_mla", j)
            table("sigmoid_and_others")

            def output_gates(name, first):
                with act.Fori(0, 2) as i:
                    for j in range(2):
                        ahead(name, j, i, 2, 2)
                        pl = Place(tab, name, j, i, 2, 2)
                        for m in range(2):
                            c = 4 * i + 2 * j + m
                            act.wait_ge(tile_read, pl.tile + m + 1)
                            nc.scalar.activation(tmp[:, 2 + m, :], tmp[:, m, :], ACT.Sigmoid,
                                                 bias=col(G_BGATE + first + c)).then_inc(gate_out, 1)
                        if first:
                            for m in range(2):
                                c = 4 * i + 2 * j + m
                                act.wait_ge(gate_merge, c + 1)
                                nc.scalar.activation(act_b[:, 0, bass.ds(c, 1), :].rearrange("p a n -> p (a n)"),
                                                     wt(c), ACT.Copy).then_inc(merged_hi, 1)

            output_gates("gate0", 0)
            output_gates("gate1", KT)
            table("natural_log_exp_and_others")
            squares_of("w_out", X, 2)
            make_rstd(rstd[:, :], D)

            norm_input(G_NORM2)
            make_rstd(rstd[:, :], D)
            act.wait_ge(decay_done, 1)
            f = tmp[0:FOX_HEADS, 1, :]
            nc.scalar.activation(f, f, ACT.Exp).then_inc(forget_log, 1)
            act.wait_ge(forget_log, 1)
            nc.scalar.activation(f, f, ACT.Ln, bias=1.0).then_inc(forget_log, 1)
            act.wait_ge(decay_done, 2)
            nc.scalar.activation(decay_row[0:FOX_HEADS, 0, :], tmp[0:FOX_HEADS, 2, :], ACT.Copy).then_inc(forget_log, 1)
            splits("fox_qk", 4)
            splits("fox_v", 2)
            act.wait_ge(tile_read, tab.end[tab.first["fox_v"] + 3])
            softmax_attention("fox", FOX_HEADS)

            def mixer_end(name, layer):
                squares_of(name, 8, 2)
                ahead(f"ple_proj{layer}", 0)
                for k in range(2):
                    act.wait_ge(tile_read, tab.extra[f"ple_proj{layer}"] + k + 1)
                    nc.scalar.activation(head_qk[:, k, :], tmp[:, k, :], ACT.Copy).then_inc(p_split, 1)
                make_rstd(rstd[:, :], D)
                ahead(f"ple_proj{layer}", 1)
                norm_input(G_NORM2 + 48 * layer + 16)

            def mlp(layer):
                chunks = D_FF // D
                name = f"mlp{layer}"

                def chunk(i, first=False, last=False):
                    for j in range(8):
                        ahead(name, j, i, 8, chunks)
                        if first and j == 0:
                            make_rstd(rstd[:, :], D)
                        for m in range(2):
                            if j < 4:
                                pl = Place(tab, name, j, i, 8, chunks)
                                act.wait_ge(tile_read, pl.tile + m + 1)
                                nc.scalar.activation(act_b[:, 0, 2 * j + m, :], tmp[:, m, :], ACT.Square)\
                                    .then_inc(hid_hi, 1)
                            elif last:
                                pl = Place(tab, name, j, i, 8, chunks)
                                act.wait_ge(tile_read, pl.tile + m + 1)
                                square(wt(16 + 2 * (j - 4) + m), n["sq"], n["sq"] % 2)
                                n.add("sq")

                chunk(0, first=True)
                with act.Fori(1, chunks - 1) as i:
                    chunk(i)
                chunk(chunks - 1, last=True)
                make_rstd(rstd[:, :], D)
                norm_input(G_NORM2 + 48 * layer + 32)

            def embed_gate(layer):
                name = f"ple_gate{layer}"
                for j in range(4):
                    ahead(name, j)
                    if j == 0:
                        make_rstd(rstd[:, :], D)
                        table("sigmoid_and_others")
                    pl = Place(tab, name, j)
                    for m in range(2):
                        act.wait_ge(tile_read, pl.tile + m + 1)
                        nc.scalar.activation(tmp[:, 2 + m, :], tmp[:, m, :], ACT.Sigmoid).then_inc(gate_out, 1)
                    for m in range(2):
                        act.wait_ge(gated, 2 * KT + n.add("gated"))
                        square(wt(2 * j + m), n["sq"], n["sq"] % 2)
                        n.add("sq")
                table("natural_log_exp_and_others")
                make_rstd(rstd[:, :], D)

            mixer_end("fox_out", 0)
            mlp(0)
            embed_gate(0)

            norm_input(G_NORM2 + 48)
            for j in range(12):
                ahead("conv_in", j)
                if j == 0:
                    make_rstd(rstd[:, :], D)
                if j % 3 == 2:
                    for m in range(2):
                        k = 2 * (j // 3) + m
                        act.wait_ge(conv_y, k + 1)
                        nc.scalar.activation(act_b[:, 0, k, :], tmp[:, 2 + m, :], ACT.Copy).then_inc(conv_hi, 1)
            mixer_end("conv_out", 1)
            mlp(1)
            embed_gate(1)

        @block.vector
        def _(dve):
            n = Steps()
            V = nc.vector

            def chain(ins, i=0, per=0):
                ins.then_inc(dve_step, 1)
                dve.wait_ge(dve_step, n.add("step") + per * i)

            def split(pl):
                if not pl.exists:
                    return
                dve.wait_ge(w_hi, pl.u + 1)
                V.tensor_tensor(wsp[:, pl.slot, 1, :], raw[:, pl.slot, :], wsp[:, pl.slot, 0, :].bitcast(F32),
                                ALU.subtract).then_inc(w_split, 1)

            def ahead(name, j, i=0, per=0, passes=1):
                split(Place(tab, name, j, i, per, passes, ahead=1))

            def done(pl, m=0):
                dve.wait_ge(tile_done, pl.tile + m + 1)
                return banks[(pl.bank + m) % 4]

            def scaled(dst, pl, m=0):
                V.tensor_tensor(dst, done(pl, m)[:, :], rstd[:, :], ALU.mult).then_inc(tile_read, 1)

            def wait_rstd(k=1):
                dve.wait_ge(rstd_ready, n.add("stat", k))

            def low(dst, src, hi, sem_, scale=None):
                if scale is None:
                    V.tensor_tensor(dst, src, hi.bitcast(F32), ALU.subtract).then_inc(sem_, 1)
                else:
                    V.scalar_tensor_tensor(out=dst, in0=src, scalar=scale, in1=hi.bitcast(F32), op0=ALU.mult,
                                           op1=ALU.subtract).then_inc(sem_, 1)

            def input_lo(k, gain):
                dve.wait_ge(in_hi, n["in"] + k + 1)
                low(act_a[:, 1, k, :], wt(X + k), act_a[:, 0, k, :], in_ready, col(gain + k))

            def add_normed(tiles_at, gain, next_gain):
                wait_rstd()
                for k in range(KT):
                    m = wt(tiles_at + k)
                    chain(V.scalar_tensor_tensor(out=m, in0=m, scalar=col(gain + k), in1=rstd[:, :], op0=ALU.mult,
                                                 op1=ALU.mult))
                    V.tensor_tensor(wt(X + k), wt(X + k), m, ALU.add).then_inc(x_ready, 1)
                    if k and next_gain is not None:
                        input_lo(k - 1, next_gain)
                if next_gain is not None:
                    input_lo(KT - 1, next_gain)
                    n.add("in", KT)

            def project(name, passes, tiles_at, factor=True, first=0):
                with dve.Fori(first, passes) as i:
                    for j in range(2):
                        ahead(name, j, i, 2, passes)
                        pl = Place(tab, name, j, i, 2, passes)
                        for m in range(2):
                            dst = wt(tiles_at + 4 * i + 2 * j + m)
                            if factor:
                                scaled(dst, pl, m)
                            else:
                                V.tensor_copy(dst, done(pl, m)[:, :]).then_inc(tile_read, 1)

            def values_out(name, j, at, width, i=0, per=0, passes=1):
                pl = Place(tab, name, j, i, per, passes)
                ahead(name, j, i, per, passes)
                for a in range(TT):
                    c = at * S + a * width + 256 * j
                    V.tensor_scalar(work[:, bass.ds(c + 256 * per * i, 256)], done(pl, a)[:, 0:256],
                                    rstd_tok[:, a:a + 1], None, ALU.mult).then_inc(tile_read, 1)

            def turned_rstd():
                dve.wait_ge(rstd_turned, n.add("turned"))
                V.tensor_copy(rstd_tok[:, :], banks[7][:, 0:TT]).then_inc(rstd_tok_ready, 1)
                dve.wait_ge(rstd_tok_ready, n["turned"])

            V.memset(eps[:, :], EPS).then_inc(prologue_ready, 1)
            marks = [(kind, what) for kind in ATT for what in STARTS_FREE[kind]]
            for mark, (kind, what) in enumerate(marks):
                V.memset(free_mark[:, mark:mark + 1], 0.0).then_inc(ATT[kind][what], FREE)
            tile = tab.extra["sb_qk"]
            for at, width in ((0, 120), (120, 37)):
                dve.wait_ge(tile_done, tile + 1)
                V.tensor_copy(gains[:, at:at + width], banks[tile % 4][:, 0:width]).then_inc(tile_read, 1)
                tile += 1
            for k in range(KT):
                dve.wait_ge(tile_done, tile + 1)
                V.tensor_copy(wt(X + k), banks[tile % 4][:, :]).then_inc(tile_read, 1)
                tile += 1
                if k:
                    dve.wait_ge(tile_read, tile - 1)
                    input_lo(k - 1, G_IN)
            dve.wait_ge(tile_read, tile)
            input_lo(KT - 1, G_IN)
            n.add("in", KT)
            split(Place(tab, "sb_qk", 0))
            ahead("sb_qk", 0)
            for dst, src in ((identr[:, :], ident), (trir[:, :], rest["tri"]), (negonesr[:, :], rest["negones"]),
                             (maskr[:, 0, :], rest["foxmask"]), (maskr[:, 1, :], rest["mlamask"]),
                             (maskr[:, 2, :], rest["sbmask"])):
                V.tensor_copy(dst, src).then_inc(const_split, 1)
            V.tensor_copy(onesr[:, :], ones[0:48, :]).then_inc(const_split, 1)
            wf_flat = wf[:, :, :, :].rearrange("p a k n -> p a (k n)")
            V.tensor_copy(wf_flat[:, 0, :], wf_raw[:, :]).then_inc(const_split, 1)
            dve.wait_ge(const_split, CONST_SPLITS - 1)
            low(wf_flat[:, 1, :], wf_raw[:, :], wf_flat[:, 0, :], const_split)

            wait_rstd()
            pl = Place(tab, "sb_qk", 0)
            for m in range(2):
                scaled(wt(8 + m), pl, m)
            ahead("sb_qk", 1)
            pl = Place(tab, "sb_qk", 1)
            for m in range(2):
                scaled(wt(10 + m), pl, m)
            project("sb_qk", 2, 8, first=1)
            turned_rstd()
            for j in range(2):
                values_out("sb_v", j, 16, SB_HEADS * HD)

            def silu(at, m):
                dve.wait_ge(gate_out, n.add("gate"))
                V.tensor_tensor(wt(at), wt(at), tmp[:, m, :], ALU.mult).then_inc(silu_done, 1)

            for j in range(2):
                pl = Place(tab, "sb_gate", j)
                ahead("sb_gate", j)
                for m in range(2):
                    scaled(wt(20 + 2 * j + m), pl, m)
                for m in range(2):
                    silu(20 + 2 * j + m, m)

            def stage(kind, i, hh):
                A = ATT[kind]
                qk = QK_PARTS[kind][hh]
                rows = QK if kind == "mla" else HD
                first = 3 * (2 * i + hh)
                dve.wait_ge(A["stage_hi"], first + 1)
                low(qk(1)[0:rows, :], head_rows(kind, "q", i, hh), qk(0)[0:rows, :], A["staged"], SCALE[kind])
                dve.wait_ge(A["stage_hi"], first + 2)
                low(qk(3)[0:rows, :], head_rows(kind, "k", i, hh), qk(2)[0:rows, :], A["staged"])
                dve.wait_ge(A["stage_hi"], first + 3)
                low(head_v[:, hh, 1, :, :], head_values(kind, i, hh), head_v[:, hh, 0, :, :], A["staged"])
                if kind == "fox":
                    pick = consts[0:48, bass.ds(ccols["sel"].start + 2 * i + hh, 1)]
                    V.tensor_scalar(decay_row[:, hh, :], rstd[0:48, :], pick, None, ALU.mult).then_inc(A["staged"], 1)

            def clear_padding():
                V.memset(act_b[:, 0:2, TT - 1, 2 * P:3 * P].bitcast(F32), 0.0).then_inc(pad_zero, 1)

            def gather(kind, i, hh):
                A = ATT[kind]
                dve.wait_ge(A["out"], FREE + 2 * i + hh + 1)
                if hh == 0:
                    dve.wait_ge(A["o_ready"], FREE + i)
                rows = slice(hh * HD, (hh + 1) * HD)
                src = banks[(4 if kind == "sb" else 6) + hh][0:HD, :]
                if kind == "fox":
                    V.tensor_copy(gathered_o[rows, :], src).then_inc(A["gathered"], 1)
                else:
                    V.tensor_tensor(gathered_o[rows, :], src, wt(TILES[kind]["gate"] + i)[rows, :], ALU.mult)                        .then_inc(A["gathered"], 1)

            def output_lo(kind, i):
                A = ATT[kind]
                dve.wait_ge(A["o_hi"], i + 1)
                low(out_parts(kind, 1, i), gathered_o, out_parts(kind, 0, i), A["o_ready"])

            A = ATT["sb"]
            clear_padding()
            dve.wait_ge(silu_done, 4)
            dve.wait_ge(tile_read, tab.end[tab.first["sb_v"] + 1])
            with dve.Fori(0, SB_HEADS // 2) as i:
                for hh in range(2):
                    h = 2 * i + hh
                    stage("sb", i, hh)

                    def part_lo(r, offset):
                        kt = TT - 1 - r
                        dve.wait_ge(A["part_hi"], 8 * h + offset + r + 1)
                        low(act_b[:, 1, kt, valid(kt)], tmp[:, kt, valid(kt)], act_b[:, 0, kt, valid(kt)], A["part_ready"])

                    def clip(r):
                        kt = TT - 1 - r
                        dve.wait_ge(A["scores"], 4 * h + r + 1)
                        V.tensor_scalar(tmp[:, kt, valid(kt)], banks[kt][:, valid(kt)], SOFTPLUS_LINEAR, None, ALU.min)                            .then_inc(A["clipped"], 1)

                    def softplus(r):
                        kt = TT - 1 - r
                        t = tmp[:, kt, valid(kt)]
                        dve.wait_ge(A["softplus"], 4 * h + r + 1)
                        V.tensor_tensor(t, banks[kt][:, valid(kt)], t, ALU.max).then_inc(A["normed"], 1)

                    clip(0)
                    clip(1)
                    softplus(0)
                    clip(2)
                    softplus(1)
                    part_lo(0, 0)
                    clip(3)
                    softplus(2)
                    part_lo(1, 0)
                    softplus(3)
                    part_lo(2, 0)
                    part_lo(3, 0)
                    for r in range(TT):
                        part_lo(r, TT)
                    gather("sb", i, hh)
                output_lo("sb", i)
            for j in range(2):
                pl = Place(tab, "o_sb", j)
                ahead("o_sb", j)
                for m in range(4):
                    V.tensor_copy(wt(4 * j + m), done(pl, m)[:, :]).then_inc(tile_read, 1)

            dve.wait_ge(stash_saved, 16)
            for j in range(2):
                pl = Place(tab, "c_qkv", j)
                ahead("c_qkv", j)
                for m in range(2):
                    V.tensor_tensor(wt(24 + 2 * j + m), done(pl, m)[:, :], rstd[:, :], ALU.mult).then_inc(tile_read, 1)
            ahead("c_rope", 0)
            pl = Place(tab, "c_rope", 0)
            V.tensor_tensor(wt(28), done(pl)[:, :], rstd[:, :], ALU.mult).then_inc(tile_read, 1)
            V.tensor_tensor(tmp[0:64, 2, :], done(pl, 1)[0:64, :], rstd[0:64, :], ALU.mult).then_inc(tile_read, 1)
            dve.wait_ge(tile_read, pl.tile + 2)
            V.tensor_tensor(tmp[0:32, 3, :], tmp[32:64, 2, :], rope[32:64, :], ALU.mult).then_inc(dve_step, 1)
            V.tensor_tensor(tmp[0:32, 2, :], tmp[0:32, 2, :], rope[0:32, :], ALU.mult).then_inc(dve_step, 1)
            dve.wait_ge(dve_step, n.add("step", 2))
            V.tensor_tensor(tmp[0:32, 2, :], tmp[0:32, 2, :], tmp[0:32, 3, :], ALU.add).then_inc(rope_k, 1)

            def gate_pair(j):
                pl = Place(tab, "mla_gate", j)
                for m in range(2):
                    scaled(wt(8 + 2 * j + m), pl, m)

            ahead("mla_gate", 0)
            gate_pair(0)
            for k in range(5):
                if k in (0, 3):
                    wait_rstd()
                r = wt(29 if k < 3 else 30)
                V.scalar_tensor_tensor(out=wt(24 + k), in0=wt(24 + k), scalar=col((G_Q if k < 3 else G_KV - 3) + k),
                                       in1=r, op0=ALU.mult, op1=ALU.mult).then_inc(c_normed, 1)
            for k in range(5):
                dve.wait_ge(c_hi, k + 1)
                at = k if k < 3 else k + 1
                low(act_b[:, 1, at, :], wt(24 + k), act_b[:, 0, at, :], c_ready)
            ahead("mla_gate", 1)
            for m in range(2):
                silu(8 + m, m % 2)
            gate_pair(1)
            for m in range(2):
                silu(10 + m, m % 2)
            dve.wait_ge(silu_done, 8)
            for j in range(2):
                pl = Place(tab, "q_up", j)
                ahead("q_up", j)
                for m in range(4):
                    bank, dst = done(pl, m), wt(12 + 4 * j + m)
                    V.tensor_copy(dst[0:HD, :], bank[0:HD, :]).then_inc(dve_step, 1)
                    parts = [tmp[64:96, 2 * (m % 2) + a, :] for a in (0, 1)]
                    dve.wait_ge(tile_read, pl.tile + m - 1)
                    V.tensor_tensor(parts[0], bank[96:128, :], rope[96:128, :], ALU.mult).then_inc(dve_step, 1)
                    V.tensor_tensor(parts[1], bank[64:96, :], rope[64:96, :], ALU.mult).then_inc(dve_step, 1)
                    dve.wait_ge(dve_step, n.add("step", 3))
                    V.tensor_tensor(dst[64:96, :], parts[0], parts[1], ALU.add).then_inc(tile_read, 1)
            pl = Place(tab, "kv_up", 0)
            ahead("kv_up", 0)
            for h in range(MLA_HEADS):
                V.tensor_copy(wt(24 + h)[0:HD, :], done(pl, h)[0:HD, :]).then_inc(tile_read, 1)
            for a in range(TT):
                V.tensor_copy(wt(20 + a), done(pl, MLA_HEADS + a)[:, :]).then_inc(tile_read, 1)

            def softmax_attention(kind, heads):
                A = ATT[kind]

                def maxima(i, s):
                    dve.wait_ge(A["scores"], FREE + 8 * i + s + 1)
                    V.reduce_max(negmax[:, s:s + 1], banks[s % 4][:, 0:(s % TT + 1) * P], AX, negate=True)                        .then_inc(A["negmax"], 1)

                def normalize(i, s):
                    dve.wait_ge(A["exp"], 8 * i + s + 1)
                    V.reciprocal(rinv[:, s:s + 1], rowsum[:, s:s + 1]).then_inc(A["step"], 1)
                    dve.wait_ge(A["step"], 8 * i + s + 1)
                    t = tmp[:, s % 4, 0:(s % TT + 1) * P]
                    V.tensor_scalar(t, t, rinv[:, s:s + 1], None, ALU.mult).then_inc(A["normed"], 1)

                def turned_lo(i, s):
                    j = s % TT
                    dve.wait_ge(A["pt_hi"], 8 * i + s + 1)
                    src = banks[4 + s % 2][:, 0:(j + 1) * P].rearrange("p (b n) -> p b n", b=j + 1)
                    dst = [act_b[:, hl, 0:j + 1, j * P:(j + 1) * P] for hl in (0, 1)]
                    low(dst[1], src, dst[0], A["pt_ready"])

                with dve.Fori(0, heads // 2) as i:
                    for what, s in steps(DVE_ORDER[kind]):
                        if what == "s":
                            stage(kind, i, s)
                        elif what == "g":
                            gather(kind, i, s)
                        elif what == "o":
                            output_lo(kind, i)
                        else:
                            {"m": maxima, "n": normalize, "p": turned_lo}[what](i, s)

            dve.wait_ge(rope_spread, 16 * MLA_HEADS)
            dve.wait_ge(tile_read, tab.end[tab.first["kv_up"]])
            clear_padding()
            softmax_attention("mla", MLA_HEADS)
            for j in range(2):
                pl = Place(tab, "o_mla", j)
                ahead("o_mla", j)
                for m in range(4):
                    V.tensor_copy(wt(12 + 4 * j + m), done(pl, m)[:, :]).then_inc(tile_read, 1)

            o_end = tab.end[tab.first["o_mla"] + 1]

            def output_gates(name, second):
                gate0 = n["gate"]
                with dve.Fori(0, 2) as i:
                    for j in range(2):
                        ahead(name, j, i, 2, 2)
                        pl = Place(tab, name, j, i, 2, 2)
                        for m in range(2):
                            scaled(tmp[:, m, :], pl, m)
                        for m in range(2):
                            c = 4 * i + 2 * j + m
                            dve.wait_ge(gate_out, gate0 + c + 1)
                            if not second:
                                V.tensor_tensor(wt(c), wt(c), tmp[:, 2 + m, :], ALU.mult).then_inc(gated, 1)
                            else:
                                V.tensor_tensor(tmp[:, 2 + m, :], wt(12 + c), tmp[:, 2 + m, :], ALU.mult)                                    .then_inc(gated, 1)
                        if second:
                            for m in range(2):
                                c = 4 * i + 2 * j + m
                                dve.wait_ge(gated, KT + c + 1)
                                V.tensor_tensor(wt(c), wt(c), tmp[:, 2 + m, :], ALU.add).then_inc(gate_merge, 1)
                            for m in range(2):
                                c = 4 * i + 2 * j + m
                                dve.wait_ge(merged_hi, c + 1)
                                parts = [act_b[:, hl, bass.ds(c, 1), :].rearrange("p a n -> p (a n)") for hl in (0, 1)]
                                low(parts[1], wt(c), parts[0], merged)
                n.add("gate", KT)

            dve.wait_ge(tile_read, o_end)
            output_gates("gate0", False)
            dve.wait_ge(gated, KT)
            output_gates("gate1", True)
            dve.wait_ge(stash_back, 16)
            with dve.Fori(0, 2) as i:
                for j in range(2):
                    ahead("w_out", j, i, 2, 2)
                    pl = Place(tab, "w_out", j, i, 2, 2)
                    for m in range(2):
                        x = wt(X + 4 * i + 2 * j + m)
                        V.tensor_tensor(x, done(pl, m)[:, :], x, ALU.add).then_inc(tile_read, 1)
            wait_rstd()
            dve.wait_ge(tile_read, tab.end[tab.first["w_out"] + 3])
            for k in range(KT):
                V.scalar_tensor_tensor(out=wt(X + k), in0=wt(X + k), scalar=col(G_F + k), in1=rstd[:, :], op0=ALU.mult,
                                       op1=ALU.mult).then_inc(x_ready, 1)
                if k:
                    dve.wait_ge(x_ready, k)
                    input_lo(k - 1, G_NORM2)
            dve.wait_ge(x_ready, KT)
            input_lo(KT - 1, G_NORM2)
            n.add("in", KT)

            wait_rstd()
            tile = tab.extra["fox_qk"]
            f, t, total = (tmp[0:FOX_HEADS, a, :] for a in range(3))
            dve.wait_ge(tile_done, tile + 1)
            V.tensor_tensor(f, banks[tile % 4][0:FOX_HEADS, :], rstd[0:FOX_HEADS, :], ALU.mult).then_inc(tile_read, 1)
            dve.wait_ge(tile_read, tile + 1)
            chain(V.tensor_scalar(f, f, b_forget[:, :], None, ALU.add))
            V.tensor_scalar(t, f, -1.0, SOFTPLUS_LINEAR, ALU.mult, ALU.min).then_inc(decay_done, 1)
            dve.wait_ge(forget_log, 2)
            chain(V.scalar_tensor_tensor(out=t, in0=f, scalar=-1.0, in1=t, op0=ALU.mult, op1=ALU.max))
            V.tensor_tensor_scan(total, t, t, 0.0, ALU.add, ALU.max).then_inc(decay_done, 1)
            project("fox_qk", 4, 0)
            turned_rstd()
            dve.wait_ge(forget_log, 3)
            dve.wait_ge(tile_read, tab.end[tab.first["fox_qk"] + 7])
            chain(V.memset(rstd[0:48, :], 0.0))
            hi = decay_row[0:FOX_HEADS, 0, :].bitcast(F32)
            V.tensor_copy(rstd[0:FOX_HEADS, :], hi).then_inc(dve_step, 1)
            n.add("step")
            chain(V.tensor_tensor(rstd[32:32 + FOX_HEADS, :], total, hi, ALU.subtract))
            with dve.Fori(0, 2) as i:
                for j in range(2):
                    values_out("fox_v", j, 16, FOX_HEADS * HD, i, 2, 2)
            dve.wait_ge(tile_read, tab.end[tab.first["fox_v"] + 3])
            clear_padding()
            softmax_attention("fox", FOX_HEADS)

            def mixer_end(name, layer):
                project(name, 2, 8, factor=False)
                tile = tab.extra[f"ple_proj{layer}"]
                ahead(f"ple_proj{layer}", 0)
                for k in range(2):
                    dve.wait_ge(tile_done, tile + k + 1)
                    V.tensor_copy(tmp[:, k, :], banks[(tile + k) % 4][:, :]).then_inc(tile_read, 1)
                dve.wait_ge(tile_read, tile + 2)
                for k in range(2):
                    dve.wait_ge(p_split, 2 * layer + k + 1)
                    low(head_qk[:, 2 + k, :], tmp[:, k, :], head_qk[:, k, :], p_ready)
                for j in range(2):
                    pl = Place(tab, f"ple_proj{layer}", j)
                    if j:
                        ahead(f"ple_proj{layer}", j)
                    for m in range(4):
                        V.tensor_copy(wt(4 * j + m), done(pl, m)[:, :]).then_inc(tile_read, 1)
                add_normed(8, G_NORM2 + 48 * layer + 8, G_NORM2 + 48 * layer + 16)

            def mlp(layer):
                chunks = D_FF // D
                name = f"mlp{layer}"
                hid = n["hid"]
                for k in range(KT):
                    V.memset(wt(16 + k), 0.0).then_inc(sum_zero, 1)
                dve.wait_ge(sum_zero, n.add("zero", KT))

                def chunk(i, first=False):
                    for j in range(8):
                        ahead(name, j, i, 8, chunks)
                        pl = Place(tab, name, j, i, 8, chunks)
                        if first and j == 0:
                            wait_rstd()
                        if j < 4:
                            h = hid + KT * i + 2 * j
                            for m in range(2):
                                V.scalar_tensor_tensor(out=tmp[:, m, :], in0=done(pl, m)[:, :], scalar=0.0,
                                                       in1=rstd[:, :], op0=ALU.max, op1=ALU.mult).then_inc(tile_read, 1)
                            for m in range(2):
                                dve.wait_ge(tile_read, pl.tile + m + 1)
                                V.tensor_tensor(tmp[:, 2 + m, :], tmp[:, m, :], tmp[:, m, :], ALU.mult)                                    .then_inc(hid_square, 1)
                            for m in range(2):
                                dve.wait_ge(hid_square, h + m + 1)
                                dve.wait_ge(hid_hi, h + m + 1)
                                k = 2 * j + m
                                low(act_b[:, 1, k, :], tmp[:, 2 + m, :], act_b[:, 0, k, :], hid_ready)
                        else:
                            for m in range(2):
                                t = wt(16 + 2 * (j - 4) + m)
                                V.tensor_tensor(t, done(pl, m)[:, :], t, ALU.add).then_inc(tile_read, 1)

                chunk(0, first=True)
                with dve.Fori(1, chunks - 1) as i:
                    chunk(i)
                chunk(chunks - 1)
                n.add("hid", KT * chunks)
                add_normed(16, G_NORM2 + 48 * layer + 24, G_NORM2 + 48 * layer + 32)

            def embed_gate(layer):
                name = f"ple_gate{layer}"
                for j in range(4):
                    ahead(name, j)
                    pl = Place(tab, name, j)
                    if j == 0:
                        wait_rstd()
                    for m in range(2):
                        scaled(tmp[:, m, :], pl, m)
                    for m in range(2):
                        dve.wait_ge(gate_out, n.add("gate"))
                        e = wt(2 * j + m)
                        V.tensor_tensor(e, e, tmp[:, 2 + m, :], ALU.mult).then_inc(gated, 1)
                dve.wait_ge(gated, 2 * KT + KT * (layer + 1))
                add_normed(0, G_NORM2 + 48 * layer + 40, G_NORM2 + 48 if layer == 0 else None)

            mixer_end("fox_out", 0)
            mlp(0)
            embed_gate(0)

            padded = [work[:, (2 + 2 * m) * S:(2 + 2 * m) * S + S + 2] for m in range(2)]
            for m in range(2):
                V.memset(padded[m][:, 0:2], 0.0).then_inc(conv_pad, 1)
            for j in range(12):
                ahead("conv_in", j)
                pl = Place(tab, "conv_in", j)
                if j == 0:
                    wait_rstd()
                part, pair = j % 3, j // 3
                if part == 0:
                    for m in range(2):
                        scaled(wt(m), pl, m)
                elif part == 1:
                    for m in range(2):
                        scaled(tmp[:, m, :], pl, m)
                    dve.wait_ge(tile_read, pl.tile + 2)
                    for m in range(2):
                        V.tensor_tensor(padded[m][:, 2:S + 2], tmp[:, m, :], wt(m), ALU.mult).then_inc(dve_step, 1)
                    n.add("step", 2)
                    dve.wait_ge(dve_step, n["step"])
                    if pair == 0:
                        dve.wait_ge(conv_pad, 2)
                    for tap in range(3):
                        for m in range(2):
                            w = col(G_CONV + KT * tap + 2 * pair + m)
                            src = padded[m][:, tap:tap + S]
                            if tap == 0:
                                ins_ = V.tensor_scalar(tmp[:, m, :], src, w, None, ALU.mult)
                            else:
                                ins_ = V.scalar_tensor_tensor(out=tmp[:, m, :], in0=src, scalar=w, in1=tmp[:, m, :],
                                                              op0=ALU.mult, op1=ALU.add)
                            ins_.then_inc(dve_step, 1)
                        n.add("step", 2)
                        dve.wait_ge(dve_step, n["step"])
                else:
                    for m in range(2):
                        scaled(tmp[:, 2 + m, :], pl, m)
                    dve.wait_ge(tile_read, pl.tile + 2)
                    for m in range(2):
                        V.tensor_tensor(tmp[:, 2 + m, :], tmp[:, 2 + m, :], tmp[:, m, :], ALU.mult).then_inc(conv_y, 1)
                    for m in range(2):
                        k = 2 * pair + m
                        dve.wait_ge(conv_y, k + 1)
                        dve.wait_ge(conv_hi, k + 1)
                        low(act_b[:, 1, k, :], tmp[:, 2 + m, :], act_b[:, 0, k, :], conv_ready)
            mixer_end("conv_out", 1)
            mlp(1)
            embed_gate(1)

            tile = tab.tiles
            for a in range(2 * TT):
                dve.wait_ge(tile_done, tile + 1)
                V.tensor_copy(wt(a), banks[tile % 4][:, :]).then_inc(tile_read, 1)
                tile += 1

        @block.gpsimd
        def _(pool):
            n = Steps()

            def sum_squares(tiles):
                if n["stat"]:
                    pool.wait_ge(stat_done, n["stat"])
                nc.gpsimd.memset(ssum[:, :], 0.0).then_inc(sq_zero, 1)
                pool.wait_ge(sq_zero, n.add("stat"))
                base = n.add("sq", tiles) - tiles

                def add(at, parity):
                    pool.wait_ge(sq_done, at + 1)
                    nc.gpsimd.tensor_tensor(ssum[:, :], ssum[:, :], sq[:, parity, :], ALU.add).then_inc(sq_added, 1)
                    pool.wait_ge(sq_added, at + 1)

                if tiles == KT:
                    with pool.Fori(0, KT // 2) as i:
                        for m in range(2):
                            add(base + 2 * i + m, (base + m) % 2)
                else:
                    for k in range(tiles):
                        add(base + k, (base + k) % 2)

            sum_squares(KT)
            A = ATT["sb"]
            with pool.Fori(0, SB_HEADS // 2) as i:
                for hh in range(2):
                    h = 2 * i + hh
                    for r in range(TT):
                        kt = TT - 1 - r
                        diagonal = tmp[:, kt, kt * P:(kt + 1) * P]
                        pool.wait_ge(A["normed"], 4 * h + r + 1)
                        nc.gpsimd.tensor_tensor(diagonal, diagonal, strict, ALU.mult).then_inc(A["masked"], 1)
            sum_squares(Q_LORA // P)
            sum_squares(KV_LORA // P)
            for norm in range(13):
                sum_squares(KT)



_INS = ["x", "norm_in_g", "w_in", "b_gate", "q_norm_g", "w_q_up", "kv_norm_g", "w_kv_up", "w_o_sb", "w_o_mla", "w_out",
        "norm_f_g", "p_2", "norm_g_2", "w_attn_in_2", "b_forget_2", "w_attn_out_2", "w_conv_in_2", "conv_w_2",
        "w_conv_out_2", "w_mlp_up_2", "w_mlp_down_2", "w_ple_proj_2", "w_ple_gate_2"]


def kernel(**inputs):
    import numpy as _np
    import concourse.bacc as _bacc
    from concourse import mybir as _mybir
    from concourse.bass_utils import run_bass_kernel_spmd as _run

    nc = _bacc.Bacc("TRN2", target_bir_lowering=False, num_devices=1, dynamic_dma_scratch_size=1024)
    arrays, args = {}, {}
    for name in _INS:
        arrays[f"in_{name}"] = _np.ascontiguousarray(inputs[name])
    arrays["in_consts"] = constants()
    for name, a in arrays.items():
        args[name[3:]] = nc.dram_tensor(name, a.shape, _mybir.dt.from_np(a.dtype), kind="ExternalInput").ap()
    out = nc.dram_tensor("out_0", (1, S, D), F32, kind="ExternalOutput").ap()
    hybrid_block_kernel(nc, args, out)
    r = _run(nc, [arrays], core_ids=[0])
    return r.results[0]["out_0"]
```

```python
from contextlib import ExitStack

import concourse.bass as bass
import numpy as np
from concourse import mybir

F32 = mybir.dt.float32
F32R = mybir.dt.float32r
ALU = mybir.AluOpType
ACT = mybir.ActivationFunctionType
AX = mybir.AxisListType.X

P = 128
S = 512
D = 1024
KT = D // P
TT = S // P
HD = 64
SB_HEADS = MLA_HEADS = 8
FOX_HEADS = 16
QK = 96
ROPE = 32
Q_LORA, KV_LORA = 384, 256
D_FF = 4096
CHUNK = 64
EPS = 1e-6
FREE = 1
MASKED = -float(2.0 ** 100)
SOFTPLUS_LINEAR = 20.0
UNIT = 2048
CONST_COLS = dict(ident=128, ones=128, sel=16, rope=S, strict=128, tri=128, negones=128, foxmask=384, mlamask=384, sbmask=384)
KEPT = 128 + 128 + 16 + S + 128
CONST_LOADS = 11
CONST_SPLITS = 9


def const_offsets():
    at, out = 0, {}
    for name, n in CONST_COLS.items():
        out[name] = slice(at, at + n)
        at += n
    return out, at


def constants():
    cols, width = const_offsets()
    c = np.zeros((P, width), np.float32)
    row, col = np.arange(P)[:, None], np.arange(P)[None, :]
    c[:, cols["ident"]] = np.eye(P)
    c[:, cols["tri"]] = np.where(row >= col, -1.0, 0.0)
    c[:, cols["negones"]] = -1.0
    c[:, cols["ones"]] = 1.0
    c[:, cols["strict"]] = np.where(row < col, 1.0, 0.0)
    c[:, cols["sbmask"]][:, P:2 * P] = np.where(row < col, 0.0, MASKED)
    c[:, cols["foxmask"]][:, P:2 * P] = np.where(col <= row, 0.0, MASKED)
    c[:, cols["mlamask"]][:, P:2 * P] = np.where(col // CHUNK <= row // CHUNK, 0.0, MASKED)
    for h in range(FOX_HEADS):
        c[h, cols["sel"].start + h] = 1.0
        c[32 + h, cols["sel"].start + h] = 1.0
    half = ROPE // 2
    inv_freq = (np.float32(10000.0) ** (-np.arange(half, dtype=np.float32) / np.float32(half))).astype(np.float32)
    ang = np.arange(S, dtype=np.float32)[None, :] * inv_freq[:, None]
    cos, sin = np.cos(ang), np.sin(ang)
    for base in (0, 64):
        c[base:base + 32, cols["rope"]] = np.concatenate([cos, cos])
        c[base + 32:base + 64, cols["rope"]] = np.concatenate([-sin, sin])
    return c


SB_Q, SB_K, SB_V, SB_GATE, C_Q = 0, 512, 1024, 1536, 2048
K_ROPE = C_Q + Q_LORA + KV_LORA
MLA_GATE = K_ROPE + ROPE
GATES = MLA_GATE + 512

UNIT_GROUPS = [
    ("sb_qk", 4, 2, 1), ("sb_v", 2, 4, 1), ("sb_gate", 2, 2, 1),
    ("gate0", 4, 2, 1), ("mla_gate", 2, 2, 1), ("c_qkv", 2, 2, 1),
    ("c_rope", 1, 2, 1), ("o_sb", 2, 4, 1), ("q_up", 2, 4, 12), ("kv_up", 1, 12, 1),
    ("gate1", 4, 2, 1),
    ("o_mla", 2, 4, 1), ("w_out", 4, 2, 1), ("fox_qk", 2, 2, 2), ("fox_v", 4, 4, 1),
    ("fox_qk_next", 6, 2, 2),
    ("fox_out", 4, 2, 2),
    ("ple_proj0", 2, 4, 1), ("mlp0", 32, 2, 1), ("ple_gate0", 4, 2, 1),
    ("conv_in", 12, 2, 1), ("conv_out", 4, 2, 1),
    ("ple_proj1", 2, 4, 1), ("mlp1", 32, 2, 1), ("ple_gate1", 4, 2, 1),
]
EXTRA_TILES = {"sb_qk": 2 + KT, "fox_qk": 1, "ple_proj0": 2, "ple_proj1": 2}


class UnitTable:

    def __init__(self):
        self.first = {}
        self.tile = []
        self.end = []
        self.landed = []
        self.extra = {}
        t, slots = 0, [0, 0]
        for name, n, tiles, dmas in UNIT_GROUPS:
            self.first[name] = len(self.tile)
            self.extra[name] = t
            t += EXTRA_TILES.get(name, 0)
            for _ in range(n):
                self.tile.append(t)
                t += tiles
                self.end.append(t)
                slots[len(self.landed) % 2] += 16 * dmas
                self.landed.append(slots[len(self.landed) % 2])
        self.count = len(self.tile)
        self.tiles = t


class Place:

    def __init__(self, tab, name, j, i=0, per=0, passes=1, ahead=0):
        assert per % 2 == 0
        self.tab, self.i, self.per, self.passes = tab, i, per, passes
        self.at = tab.first[name] + j + ahead
        self.slot = self.at % 2
        self.exists = self.at < tab.count
        self.u = self.at + per * i

    def column(self, column, v):
        step = 0
        if self.passes > 1 and self.per:
            step = column[v + self.per] - column[v]
            assert all(column[v + self.per * n] == column[v] + step * n for n in range(self.passes))
        return column[v] + step * self.i

    @property
    def landed(self):
        return self.column(self.tab.landed, self.at)

    @property
    def tile(self):
        return self.column(self.tab.tile, self.at)

    @property
    def bank(self):
        assert self.passes == 1 or not self.per or (self.tab.tile[self.at + self.per] - self.tab.tile[self.at]) % 4 == 0
        return self.tab.tile[self.at] % 4

    @property
    def freed(self):
        return self.column(self.tab.tile, self.at - 1) if self.at >= 2 else None


class Steps:

    def __init__(self):
        self.n = {}

    def add(self, name, k=1):
        self.n[name] = self.n.get(name, 0) + k
        return self.n[name]

    def __getitem__(self, name):
        return self.n.get(name, 0)


def hybrid_block_kernel(nc, ins, out):
    tab = UnitTable()
    ccols, cwidth = const_offsets()

    ctx = ExitStack()
    with ctx:
        def sb(name, shape, dt=F32):
            return ctx.enter_context(nc.sbuf_tensor(name, shape, dt))

        def sem(name):
            return ctx.enter_context(nc.semaphore(name))

        raw = sb("raw_weights", [P, 2, UNIT])
        wsp = sb("split_weights", [P, 2, 2, UNIT], F32R)
        act_a = sb("act_a", [P, 2, KT, S], F32R)
        act_b = sb("act_b", [P, 2, KT, S], F32R)
        head_qk = sb("head_qk", [P, 4, S], F32R)
        head_v = sb("head_v", [P, 2, 2, TT, HD], F32R)
        decay_row = sb("decay_row", [48, 2, S], F32R)
        consts = sb("consts", [P, KEPT])
        identr = sb("identr", [P, P], F32R)
        trir = sb("trir", [P, P], F32R)
        negonesr = sb("negonesr", [P, P], F32R)
        onesr = sb("onesr", [48, P], F32R)
        maskr = sb("maskr", [P, 3, 384], F32R)
        wf_raw = sb("wf_raw", [P, KT * FOX_HEADS])
        wf = sb("wf", [P, 2, KT, FOX_HEADS], F32R)
        work = sb("work", [P, 32 * S])
        tmp = sb("tmp", [P, 4, S])
        sq = sb("sq", [P, 2, S])
        ssum = sb("ssum", [P, S])
        rstd = sb("rstd", [P, S])
        rstd_tok = sb("rstd_tok", [P, TT])
        gains = sb("gains", [P, 160])
        b_forget = sb("b_forget", [FOX_HEADS, 1])
        eps = sb("eps", [P, 1])
        free_mark = sb("free_mark", [1, 9])
        negmax = sb("negmax", [P, 8])
        rowsum = sb("rowsum", [P, 8])
        rinv = sb("rinv", [P, 8])
        banks = [ctx.enter_context(nc.psum_tensor(f"bank{i}", [P, S], F32)) for i in range(8)]
        x_stash = nc.dram_tensor("x_stash", [P, KT * S], F32, kind="Internal").ap()

        ident = consts[:, ccols["ident"]]
        ones = consts[:, ccols["ones"]]
        rope = consts[:, ccols["rope"]]
        strict = consts[:, ccols["strict"]]
        rest = {name: work[:, 10 * S + at.start - KEPT:10 * S + at.stop - KEPT] for name, at in ccols.items()
                if at.start >= KEPT}

        G_NORM2, G_CONV = 0, 96
        G_IN, G_F, G_BGATE, G_Q, G_KV = 120, 128, 136, 152, 155
        vec_raw = work[:, 8 * S:8 * S + 2 * P].rearrange("p (a n) -> p a n", a=2)

        def wt(i):
            return work[:, bass.ds(i * S, S)]

        X = 24

        def col(c):
            return gains[:, bass.ds(c, 1)]

        const_landed = sem("const_landed")
        x_landed = sem("x_landed")
        raw_landed = [sem("raw_landed0"), sem("raw_landed1")]
        w_hi = sem("w_hi")
        w_split = sem("w_split")
        tile_done = sem("tile_done")
        tile_read = sem("tile_read")
        const_split = sem("const_split")
        prologue_ready = sem("prologue_ready")
        stash_saved = sem("stash_saved")
        stash_back = sem("stash_back")
        sq_done = sem("sq_done")
        sq_zero = sem("sq_zero")
        sq_added = sem("sq_added")
        stat_done = sem("stat_done")
        ln_done = sem("ln_done")
        rstd_ready = sem("rstd_ready")
        rstd_turned = sem("rstd_turned")
        rstd_tok_ready = sem("rstd_tok_ready")
        x_ready = sem("x_ready")
        in_hi = sem("in_hi")
        in_ready = sem("in_ready")
        silu_done = sem("silu_done")
        gate_out = sem("gate_out")
        gated = sem("gated")
        branch_gate = sem("branch_gate")
        gate_merge = sem("gate_merge")
        merged_hi = sem("merged_hi")
        merged = sem("merged")
        sum_zero = sem("sum_zero")
        conv_pad = sem("conv_pad")
        dve_step = sem("dve_step")
        hid_square = sem("hid_square")
        hid_hi = sem("hid_hi")
        hid_ready = sem("hid_ready")
        pad_zero = sem("pad_zero")
        c_normed = sem("c_normed")
        c_hi = sem("c_hi")
        c_ready = sem("c_ready")
        rope_k = sem("rope_k")
        rope_swapped = sem("rope_swapped")
        rope_spread = sem("rope_spread")
        decay_done = sem("decay_done")
        forget_log = sem("forget_log")
        p_landed = sem("p_landed")
        p_split = sem("p_split")
        p_ready = sem("p_ready")
        conv_y = sem("conv_y")
        conv_hi = sem("conv_hi")
        conv_ready = sem("conv_ready")
        out_tile = sem("out_tile")
        out_saved = sem("out_saved")

        ATT = {}
        for kind in ("sb", "mla", "fox"):
            ATT[kind] = {n: sem(f"{kind}_{n}") for n in (
                "q_hi", "stage_hi", "staged", "scores", "turned", "clipped", "softplus", "masked", "part_hi",
                "part_ready", "summed", "w_exp", "w_masked", "negmax", "exp", "normed", "pt_hi", "pt_ready",
                "out", "gathered", "o_hi", "o_ready", "step")}

        block = ctx.enter_context(nc.Block())

        def by_k(w):
            return w.rearrange("(k p) n -> p k n", p=P)

        w_in = by_k(ins["w_in"][0])
        attn_in = by_k(ins["w_attn_in_2"][0])
        conv_in = by_k(ins["w_conv_in_2"][0])

        def slot_of(s, k, n):
            return raw[:, s, 0:k * n].rearrange("p (k n) -> p k n", k=k)

        MASK = {"fox": 0, "mla": 1, "sb": 2}
        STARTS_FREE = {"sb": ("summed", "out", "gathered"),
                       "mla": ("scores", "out", "gathered"),
                       "fox": ("scores", "out", "gathered")}
        STAGES = {"fox": 4, "mla": 3}

        def qk_main(a):
            return head_qk[:, a, :]

        def qk_spare(a):
            return act_b[:, a // 2, 4 + a % 2, :]

        QK_PARTS = (qk_main, qk_spare)
        PE_ORDER = "z0 z1 z2 g0 t0 z3 g1 t1 z4 g2 t2 z5 g3 t3 z6 g4 t4 v0 z7 g5 t5 t6 g6 t7 g7 v1"
        ACT_ORDER = "e0 s1 e1 e2 p0 e3 p1 e4 p2 e5 p3 e6 s2 p4 w0 e7 p5 p6 p7"
        DVE_ORDER = "m0 m1 n0 s1 m2 n1 p0 m3 n2 p1 m4 n3 p2 m5 n4 p3 m6 n5 p4 g0 s2 m7 n6 w0 p5 n7 p6 p7 x0 x1 g1"

        def steps(order):
            return [(w[0], int(w[1:])) for w in order.split()]

        TILES = {"sb": dict(q=0, k=4, v=8, gate=12), "mla": dict(q=8, k=16, v=28, gate=24), "fox": dict(q=0, k=8, v=16)}
        Y_SB, Y_GATE0, Y_GATE1 = 0, 16, 8
        LATENTS = (28, 29, 30, 31, 8)
        BESIDE = {"sb": "gate0", "mla": "gate1", "fox": "fox_qk_next"}
        BESIDE_PASSES = {"mla": MLA_HEADS // 4, "fox": FOX_HEADS // 4 - 1}
        SCALE = {"sb": HD ** -0.5, "fox": HD ** -0.5, "mla": QK ** -0.5}

        def head_rows(kind, which, i, hh):
            if kind == "mla":
                return wt(TILES[kind][which] + 2 * i + hh)[0:QK, :]
            return wt(TILES[kind][which] + i)[hh * HD:(hh + 1) * HD, :]

        def head_values(kind, i, hh):
            width = (FOX_HEADS if kind == "fox" else SB_HEADS) * HD
            v = work[:, TILES[kind]["v"] * S:TILES[kind]["v"] * S + TT * width].rearrange("p (a n) -> p a n", a=TT)
            return v[:, :, bass.ds(2 * HD * i + hh * HD, HD)]

        decay_parts = ssum[0:48, :]

        def output_tile(kind, i):
            return wt(TILES[kind]["k"] + 2 * i if kind == "mla" else TILES[kind]["q"] + i)

        def out_parts(kind, hl, k):
            return act_a[:, hl, k, :] if kind == "fox" else act_b[:, hl, 4 + k, :]

        def valid(kt):
            return slice(kt * P, S)

        def stick_hi(act, A, h, r, offset):
            kt = TT - 1 - r
            act.wait_ge(A["w_exp" if offset else "masked"], 4 * h + r + 1)
            if r == 0 and offset == 0:
                act.wait_ge(A["out"], FREE + h)
            if r == 0 and offset:
                act.wait_ge(A["summed"], FREE + 4 * h + TT)
            nc.scalar.activation(act_b[:, 0, kt, valid(kt)], tmp[:, kt, valid(kt)], ACT.Copy).then_inc(A["part_hi"], 1)

        @block.sync
        def _(sp):
            def load(pl, dst, src, first=True):
                if first and pl.at >= 2:
                    sp.wait_ge(w_split, pl.u - 1)
                    sp.nop(nofuse=True)
                sp.dma_start(dst, src).then_inc(raw_landed[pl.slot], 16)

            def loop(name, passes, per, source, k=KT, n=256):
                with sp.Fori(0, passes) as i:
                    for j in range(per):
                        pl = Place(tab, name, j, i, per, passes)
                        load(pl, slot_of(pl.slot, k, n), source(i, j))

            sp.dma_start(work[:, 0:8 * S].rearrange("p (a n) -> p a n", a=TT),
                         ins["x"][0].rearrange("(a p) n -> p a n", p=P)).then_inc(x_landed, 16)
            sp.dma_start(consts[:, :], ins["consts"][:, 0:KEPT]).then_inc(const_landed, 16)
            sp.dma_start(work[:, 10 * S:10 * S + cwidth - KEPT], ins["consts"][:, KEPT:cwidth]).then_inc(const_landed, 16)

            def rows(v, n):
                return v.rearrange("(k p) -> k p", p=P)[0:n, :]

            sp.dma_start(vec_raw[0:96, 0, :], ins["norm_g_2"].rearrange("l n (k p) -> (l n k) p", p=P))\
                .then_inc(const_landed, 16)
            sp.dma_start(vec_raw[96:120, 0, :], ins["conv_w_2"][0].rearrange("j (k p) -> (j k) p", p=P))\
                .then_inc(const_landed, 16)
            at = 0
            for name, n in (("norm_in_g", 8), ("norm_f_g", 8), ("b_gate", 16), ("q_norm_g", 3), ("kv_norm_g", 2)):
                v = ins[name] if name == "norm_f_g" else ins[name][0]
                sp.dma_start(vec_raw[at:at + n, 1, :], rows(v, n)).then_inc(const_landed, 16)
                at += n
            sp.dma_start(b_forget[:, :], ins["b_forget_2"].rearrange("a h -> h a")).then_inc(const_landed, 16)
            sp.dma_start(wf_raw[:, :].rearrange("p (k n) -> p k n", k=KT),
                         attn_in[:, :, 3 * D:3 * D + FOX_HEADS]).then_inc(const_landed, 16)

            def w_in_cols(c):
                return lambda i, j: w_in[:, :, bass.ds(c + 512 * i + 256 * j, 256)]

            for j in range(2):
                load(Place(tab, "sb_qk", j), slot_of(j, KT, 256), w_in_cols(SB_Q)(0, j))
            with sp.Fori(1, 2) as i:
                for j in range(2):
                    pl = Place(tab, "sb_qk", j, i, 2, 2)
                    sp.wait_ge(w_split, pl.u - 1)
                    sp.nop(nofuse=True)
                    sp.dma_start(slot_of(pl.slot, KT, 256), w_in_cols(SB_Q)(i, j)).then_inc(raw_landed[pl.slot], 16)
            sp.wait_ge(in_ready, KT)
            sp.dma_start(x_stash, work[:, X * S:(X + KT) * S]).then_inc(stash_saved, 16)
            loop("sb_v", 1, 2, w_in_cols(SB_V))
            loop("sb_gate", 1, 2, w_in_cols(SB_GATE))
            loop("gate0", 2, 2, w_in_cols(GATES))
            for name, c in (("mla_gate", MLA_GATE), ("c_qkv", C_Q)):
                for j in range(2):
                    pl = Place(tab, name, j)
                    load(pl, slot_of(pl.slot, KT, 256), w_in[:, :, c + 256 * j:c + 256 * j + 256])
            pl = Place(tab, "c_rope", 0)
            load(pl, slot_of(pl.slot, KT, 160), w_in[:, :, C_Q + 512:MLA_GATE])
            o_sb = by_k(ins["w_o_sb"][0])
            for j in range(2):
                pl = Place(tab, "o_sb", j)
                load(pl, slot_of(pl.slot, 4, 512), o_sb[:, :, 512 * j:512 * j + 512])
            sp.wait_ge(tile_read, tab.end[tab.first["c_rope"]])
            sp.dma_start(tmp[32:48, 2, :], tmp[16:32, 2, :]).then_inc(rope_swapped, 16)
            sp.dma_start(tmp[48:64, 2, :], tmp[0:16, 2, :]).then_inc(rope_swapped, 16)
            def spread():
                sp.wait_ge(rope_k, 1)
                sp.wait_ge(tile_read, tab.end[tab.first["o_sb"] + 1])
                for h in range(MLA_HEADS):
                    at = TILES["mla"]["k"] + h
                    sp.dma_start(work[64:96, at * S:(at + 1) * S], tmp[0:32, 2, :]).then_inc(rope_spread, 16)

            q_up = ins["w_q_up"][0].rearrange("(k p) n -> p k n", p=P)
            for j in range(2):
                pl = Place(tab, "q_up", j)
                for h in range(4):
                    src = q_up[:, :, QK * (4 * j + h):QK * (4 * j + h + 1)]
                    dst = raw[:, pl.slot, 0:3 * 512].rearrange("p (k h n) -> p k h n", k=3, h=4)[:, :, h, :]
                    if h == 0:
                        load(pl, dst[:, :, 0:96], src)
                    else:
                        load(pl, dst[:, :, 0:96], src, first=False)
                    load(pl, dst[:, :, 96:112], src[:, :, 80:96], first=False)
                    load(pl, dst[:, :, 112:128], src[:, :, 64:80], first=False)
            kv_up = ins["w_kv_up"][0].rearrange("(k p) n -> p k n", p=P)
            pl = Place(tab, "kv_up", 0)
            load(pl, slot_of(pl.slot, 2, 1024), kv_up)
            spread()
            loop("gate1", 2, 2, w_in_cols(GATES + D))
            o_mla = by_k(ins["w_o_mla"][0])
            loop("o_mla", 1, 2, lambda i, j: o_mla[:, :, 512 * j:512 * j + 512], k=4, n=512)
            sp.wait_ge(ATT["mla"]["o_ready"], MLA_HEADS // 2)
            sp.dma_start(work[:, X * S:(X + KT) * S], x_stash).then_inc(stash_back, 16)
            w_out = by_k(ins["w_out"][0])
            loop("w_out", 2, 2, lambda i, j: w_out[:, :, bass.ds(512 * i + 256 * j, 256)])

            def mlp(layer):
                up = by_k(ins["w_mlp_up_2"][layer])
                down = ins["w_mlp_down_2"][layer].rearrange("(c k p) n -> p c k n", p=P, k=KT)
                chunks = D_FF // D

                def source(i, j):
                    if j < 4:
                        return up[:, :, bass.ds(D * i + 256 * j, 256)]
                    return down[:, bass.ds(i, 1), :, 256 * (j - 4):256 * (j - 3)].rearrange("p a k n -> p (a k) n")

                loop(f"mlp{layer}", chunks, 8, source)

            def embedding(layer):
                sp.dma_start(work[:, 16 * S:18 * S].rearrange("p (a n) -> p a n", a=TT),
                             ins["p_2"][layer, 0].rearrange("(a p) n -> p a n", p=P)).then_inc(p_landed, 16)

            def embed_project(layer):
                proj = ins["w_ple_proj_2"][layer].rearrange("(k p) n -> p k n", p=P)
                loop(f"ple_proj{layer}", 1, 2, lambda i, j: proj[:, :, 512 * j:512 * j + 512], k=2, n=512)

            def embed_gate(layer):
                gate = by_k(ins["w_ple_gate_2"][layer])
                loop(f"ple_gate{layer}", 2, 2, lambda i, j: gate[:, :, bass.ds(512 * i + 256 * j, 256)])

            def load_qk(pl, pair):
                for b in range(2):
                    load(pl, slot_of(pl.slot, KT, 256)[:, :, b * P:(b + 1) * P],
                         attn_in[:, :, bass.ds(b * D + P * pair, P)], first=b == 0)

            for j in range(2):
                load_qk(Place(tab, "fox_qk", j), j)
            loop("fox_v", 2, 2, lambda i, j: attn_in[:, :, bass.ds(2 * D + 512 * i + 256 * j, 256)])
            with sp.Fori(0, 3) as i:
                for j in range(2):
                    load_qk(Place(tab, "fox_qk_next", j, i, 2, 3), 2 + 2 * i + j)
            fox_out = by_k(ins["w_attn_out_2"][0])

            def load_out(pl, j):
                for part in range(2):
                    rows = slice(4 * part, 4 * part + 4)
                    load(pl, slot_of(pl.slot, KT, 256)[:, rows, :], fox_out[:, rows, 256 * j:256 * j + 256],
                         first=part == 0)

            for j in range(2):
                pl = Place(tab, "fox_out", j)
                load_out(pl, j)
            sp.wait_ge(ATT["fox"]["staged"], 4 * FOX_HEADS)
            embedding(0)
            for j in range(2, 4):
                pl = Place(tab, "fox_out", j)
                load_out(pl, j)
            embed_project(0)
            mlp(0)
            embed_gate(0)

            sp.wait_ge(x_ready, 3 * KT)
            embedding(1)

            def conv_source(i, j):
                part, half = j % 3, j // 3
                return conv_in[:, :, bass.ds((D, 2 * D, 0)[part] + 512 * i + 256 * half, 256)]

            loop("conv_in", 2, 6, conv_source)
            conv_out = by_k(ins["w_conv_out_2"][0])
            loop("conv_out", 2, 2, lambda i, j: conv_out[:, :, bass.ds(512 * i + 256 * j, 256)])
            embed_project(1)
            mlp(1)
            embed_gate(1)

            for n in range(TT):
                sp.wait_ge(tile_read, tab.tiles + 2 * (n + 1))
                sp.dma_start(out[0, n * P:(n + 1) * P, :], work[:, 2 * n * S:2 * (n + 1) * S]).then_inc(out_saved, 16)
            sp.wait_ge(out_saved, 16 * TT)

        @block.tensor
        def _(pe):
            n = Steps()

            def weights(pl, hl, a, b):
                return wsp[:, pl.slot, hl, a:b]

            def bank(pl, m):
                return banks[(pl.bank + m) % 4]

            def empty(tile, m=0):
                if not isinstance(tile, int) or tile + m >= 4:
                    pe.wait_ge(tile_read, tile + m - 3)

            def three(dst, w, a, first, last, done=None):
                nc.tensor.matmul(dst, w[0], a[0], start=first, stop=False)
                nc.tensor.matmul(dst, w[0], a[1], start=False, stop=False)
                mm = nc.tensor.matmul(dst, w[1], a[0], start=False, stop=last)
                if done is not None:
                    mm.then_inc(done, 1)

            def unit(pl, k_tiles, width, m_tiles, x, ready=None):
                pe.wait_ge(w_split, pl.u + 1)
                for m in range(m_tiles):
                    empty(pl.tile, m)
                for k in range(k_tiles):
                    if ready:
                        pe.wait_ge(ready[0], ready[1] + k + 1)
                    for m in range(m_tiles):
                        c = k * width + m * P
                        three(bank(pl, m)[:, :], [weights(pl, hl, c, c + P) for hl in (0, 1)],
                              [x(hl, k) for hl in (0, 1)], k == 0, k == k_tiles - 1,
                              tile_done if k == k_tiles - 1 else None)

            def beside(pl, share):
                if share == 0:
                    pe.wait_ge(w_split, pl.u + 1)
                    pe.wait_ge(tile_read, pl.tile)
                for m in range(2):
                    c = share * 256 + m * P
                    three(banks[6 + m][:, :], [weights(pl, hl, c, c + P) for hl in (0, 1)],
                          [from_a(hl, share) for hl in (0, 1)], share == 0, share == KT - 1,
                          tile_done if share == KT - 1 else None)

            def unit_tokens(pl, k_tiles, x, cols, rhs, skip=0):
                pe.wait_ge(w_split, pl.u + 1)
                for a in range(TT):
                    empty(pl.tile, skip + a)
                    for k in range(k_tiles):
                        three(bank(pl, skip + a)[:, 0:cols], [x(hl, k)[:, a * P:(a + 1) * P] for hl in (0, 1)],
                              [rhs(hl, k) for hl in (0, 1)], k == 0, k == k_tiles - 1,
                              tile_done if k == k_tiles - 1 else None)

            def from_a(hl, k):
                return act_a[:, hl, k, :]

            def from_b(hl, k):
                return act_b[:, hl, k, :]

            def upper_b(hl, k):
                return act_b[:, hl, 4 + k, :]

            def project(name, passes, x, ready=None, stats=False):
                first = 0
                if stats:
                    unit(Place(tab, name, 0), KT, 256, 2, x, ready)
                    statistics(KT)
                    unit(Place(tab, name, 1), KT, 256, 2, x)
                    first = 1
                with pe.Fori(first, passes) as i:
                    for j in range(2):
                        unit(Place(tab, name, j, i, 2, passes), KT, 256, 2, x, ready if j == 0 and not stats else None)

            def statistics(tiles):
                pe.wait_ge(sq_added, n.add("sq", tiles))
                if n["stat"]:
                    pe.wait_ge(rstd_ready, n["stat"])
                if n["turned"]:
                    pe.wait_ge(rstd_tok_ready, n["turned"])
                nc.tensor.matmul(banks[7][:, :], ones, ssum[:, :], start=True, stop=True).then_inc(stat_done, 1)
                n.add("stat")

            def turn_rstd():
                pe.wait_ge(rstd_ready, n["stat"])
                for a in range(TT):
                    mm = nc.tensor.matmul(banks[7][:, a:a + 1], rstd[0:1, a * P:(a + 1) * P], ones[0:1, 0:1],
                                          start=a == 0, stop=a == TT - 1)
                mm.then_inc(rstd_turned, 1)
                n.add("turned")

            tile = tab.extra["sb_qk"]
            pe.wait_ge(const_landed, 16 * CONST_LOADS)
            for r, rows in ((0, 120), (1, 37)):
                nc.tensor.transpose(banks[tile % 4][:, 0:rows], vec_raw[0:rows, r, :], ident[0:rows, 0:rows])\
                    .then_inc(tile_done, 1)
                tile += 1
            pe.wait_ge(x_landed, 16)
            for k in range(KT):
                empty(tile)
                for a in range(TT):
                    tr = nc.tensor.transpose(banks[tile % 4][:, a * P:(a + 1) * P],
                                             work[:, a * D + k * P:a * D + (k + 1) * P], ident)
                tr.then_inc(tile_done, 1)
                tile += 1

            project("sb_qk", 2, from_a, (in_ready, 0), stats=True)
            turn_rstd()
            for j in range(2):
                pl = Place(tab, "sb_v", j)
                unit_tokens(pl, KT, from_a, 256, lambda hl, k: weights(pl, hl, k * 256, (k + 1) * 256))
            for j in range(2):
                unit(Place(tab, "sb_gate", j), KT, 256, 2, from_a)

            A = ATT["sb"]
            pe.wait_ge(pad_zero, 1)
            pe.wait_ge(const_split, CONST_SPLITS)
            with pe.Fori(0, SB_HEADS // 2) as i:
                for hh in range(2):
                    h = 2 * i + hh
                    pl = Place(tab, BESIDE["sb"], hh, i, 2, SB_HEADS // 2)
                    pe.wait_ge(A["staged"], 3 * h + 3)

                    qk = QK_PARTS[hh]

                    def scores(kt, last, done=None):
                        c = min(kt * P, S - 2 * P)
                        three(banks[kt][:, c:S], [qk(2 + hl)[0:HD, kt * P:(kt + 1) * P] for hl in (0, 1)],
                              [qk(hl)[0:HD, c:S] for hl in (0, 1)], True, last, done)

                    for kt in reversed(range(TT)):
                        scores(kt, True, A["scores"])
                    beside(pl, 0)
                    beside(pl, 1)
                    for kt in reversed(range(TT)):
                        pe.wait_ge(A["part_ready"], 8 * h + TT - kt)
                        scores(kt, False)
                        for later in range(kt, TT):
                            c = min(later * P, S - 2 * P)
                            m = trir if later == kt else negonesr
                            for hl in (0, 1):
                                nc.tensor.matmul(banks[kt][:, c:S], m[:, :], act_b[:, hl, later, c:S],
                                                 start=False, stop=False)
                        c = min(kt * P, S - 2 * P)
                        m = maskr[:, MASK["sb"], 0:2 * P] if kt == TT - 1 else maskr[:, MASK["sb"], P:3 * P]
                        nc.tensor.matmul(banks[kt][:, c:c + 2 * P], identr[:, :], m, start=False, stop=True)\
                            .then_inc(A["summed"], 1)
                        if kt:
                            beside(pl, 1 + TT - kt)
                    for share in range(5, KT):
                        beside(pl, share)
                    pe.wait_ge(A["part_ready"], 8 * h + 8)
                    pe.wait_ge(A["gathered"], FREE + 2 * i)
                    for kt in range(TT):
                        c = min(kt * P, S - 2 * P)
                        three(banks[4 + hh][0:HD, c:S], [head_v[:, hh, hl, kt, :] for hl in (0, 1)],
                              [act_b[:, hl, kt, c:S] for hl in (0, 1)], kt == 0, kt == TT - 1,
                              A["out"] if kt == TT - 1 else None)

            pl = Place(tab, "c_rope", 0)
            pe.wait_ge(w_split, pl.u + 1)
            for m, rows in ((0, P), (1, ROPE)):
                empty(pl.tile, m)
                for k in range(KT):
                    c = k * 160 + m * P
                    three(bank(pl, m)[0:rows, :], [weights(pl, hl, c, c + rows) for hl in (0, 1)],
                          [from_a(hl, k) for hl in (0, 1)], k == 0, k == KT - 1, tile_done if k == KT - 1 else None)
            pe.wait_ge(A["o_ready"], SB_HEADS // 2)
            unit(Place(tab, "o_sb", 0), 4, 512, 4, upper_b)
            statistics(3)
            statistics(2)
            unit(Place(tab, "o_sb", 1), 4, 512, 4, upper_b)
            for j in range(2):
                unit(Place(tab, "q_up", j), 3, 512, 4, from_b, (c_ready, 0) if j == 0 else None)
            pl = Place(tab, "kv_up", 0)
            pe.wait_ge(w_split, pl.u + 1)
            pe.wait_ge(c_ready, 5)

            def kv_latents(hl, k):
                return head_qk[:, 2 * hl + k, :]

            for h in range(MLA_HEADS):
                empty(pl.tile, h)
                for k in range(2):
                    c = k * 1024 + h * P
                    three(bank(pl, h)[0:HD, :], [weights(pl, hl, c, c + HD) for hl in (0, 1)],
                          [kv_latents(hl, k) for hl in (0, 1)], k == 0, k == 1, tile_done if k == 1 else None)

            def v_cols(hl, k):
                return weights(pl, hl, k * 1024, (k + 1) * 1024).rearrange("p (h c) -> p h c", h=8)[:, :, HD:P]

            unit_tokens(pl, 2, kv_latents, S, v_cols, skip=MLA_HEADS)

            def softmax_attention(kind, heads, width):
                A = ATT[kind]
                mask = maskr[:, MASK[kind], :]
                stages = STAGES[kind]

                def scores(i, s):
                    hh, j = divmod(s, TT)
                    qk = QK_PARTS[hh]
                    if j == 0:
                        pe.wait_ge(A["staged"], stages * (2 * i + hh) + stages)
                    cols = max((j + 1) * P, 2 * P)
                    dst = banks[s % 3][:, 0:cols]
                    for pass_, (a, b) in enumerate(((0, 2), (0, 3), (1, 2))):
                        nc.tensor.matmul(dst, qk(a)[0:width, j * P:(j + 1) * P], qk(b)[0:width, 0:cols],
                                         start=pass_ == 0, stop=False)
                    if kind == "fox":
                        nc.tensor.matmul(dst, onesr[:, :], decay_row[:, hh, 0:cols], start=False, stop=False)
                    c = max(j - 1, 0) * P
                    m = mask[:, P:3 * P] if j == 0 else mask[:, 0:2 * P]
                    nc.tensor.matmul(banks[s % 3][:, c:c + 2 * P], identr[:, :], m, start=False, stop=True)\
                        .then_inc(A["scores"], 1)

                def turn(i, s):
                    pe.wait_ge(A["normed"], 8 * i + s + 1)
                    if s >= 2:
                        pe.wait_ge(A["pt_ready"], 8 * i + s - 1)
                    for b in range(s % TT + 1):
                        tr = nc.tensor.transpose(banks[3 + s % 2][:, b * P:(b + 1) * P],
                                                 tmp[:, s % 4, b * P:(b + 1) * P], ident)
                    tr.then_inc(A["turned"], 1)

                def values(i, hh):
                    pe.wait_ge(A["pt_ready"], 8 * i + 4 * hh + 4)
                    pe.wait_ge(A["gathered"], FREE + 2 * i + hh)
                    for kt in range(TT):
                        c = min(kt * P, S - 2 * P)
                        three(banks[5][0:HD, c:S], [head_v[:, hh, hl, kt, :] for hl in (0, 1)],
                              [act_b[:, hl, kt, c:S] for hl in (0, 1)], kt == 0, kt == TT - 1,
                              A["out"] if kt == TT - 1 else None)

                def two_pairs(i, with_unit=True):
                    for a in range(2):
                        for what, s in steps(PE_ORDER):
                            if what != "g":
                                {"z": scores, "t": turn, "v": values}[what](2 * i + a, s)
                            elif with_unit:
                                beside(Place(tab, BESIDE[kind], a, i, 2, passes), s)

                passes = BESIDE_PASSES[kind]
                with pe.Fori(0, heads // 4 - 1) as i:
                    two_pairs(i)
                two_pairs(heads // 4 - 1, with_unit=passes == heads // 4)

            pe.wait_ge(pad_zero, 2)
            softmax_attention("mla", MLA_HEADS, QK)
            pe.wait_ge(ATT["mla"]["o_ready"], MLA_HEADS // 2)
            for j in range(2):
                unit(Place(tab, "o_mla", j), 4, 512, 4, upper_b)
            project("w_out", 2, from_a, (merged, 0))
            statistics(KT)

            n.add("in", KT)
            tile = tab.extra["fox_qk"]
            empty(tile)
            for k in range(KT):
                pe.wait_ge(in_ready, n["in"] + k + 1)
                three(banks[tile % 4][0:FOX_HEADS, :], [wf[:, hl, k, :] for hl in (0, 1)],
                      [from_a(hl, k) for hl in (0, 1)], k == 0, k == KT - 1, tile_done if k == KT - 1 else None)
            n.add("in", KT)
            statistics(KT)
            for j in range(2):
                unit(Place(tab, "fox_qk", j), KT, 256, 2, from_a)
            turn_rstd()
            with pe.Fori(0, 2) as i:
                for j in range(2):
                    pl = Place(tab, "fox_v", j, i, 2, 2)
                    unit_tokens(pl, KT, from_a, 256, lambda hl, k: weights(pl, hl, k * 256, (k + 1) * 256))
            pe.wait_ge(pad_zero, 3)
            softmax_attention("fox", FOX_HEADS, HD)
            project("fox_out", 2, from_a, (ATT["fox"]["o_ready"], 0))

            def embed_project(layer):
                tile = tab.extra[f"ple_proj{layer}"]
                pe.wait_ge(p_landed, 16 * (layer + 1))
                for k in range(2):
                    empty(tile)
                    for a in range(TT):
                        c = 16 * S + a * 256 + k * P
                        tr = nc.tensor.transpose(banks[tile % 4][:, a * P:(a + 1) * P], work[:, c:c + P], ident)
                    tr.then_inc(tile_done, 1)
                    tile += 1

                def embedding(hl, k):
                    return head_qk[:, 2 * hl + k, :]

                unit(Place(tab, f"ple_proj{layer}", 0), 2, 512, 4, embedding, (p_ready, 2 * layer))
                statistics(KT)
                unit(Place(tab, f"ple_proj{layer}", 1), 2, 512, 4, embedding)

            def mlp(layer):
                chunks = D_FF // D
                base = n.add("in", KT) - KT
                hid = n.add("hid", KT * chunks) - KT * chunks

                def chunk(i, first=False):
                    for j in range(8):
                        pl = Place(tab, f"mlp{layer}", j, i, 8, chunks)
                        if j < 4:
                            unit(pl, KT, 256, 2, from_a, (in_ready, base) if first and j == 0 else None)
                        else:
                            unit(pl, KT, 256, 2, from_b, (hid_ready, hid + KT * i) if j == 4 else None)
                        if first and j == 0:
                            statistics(KT)

                chunk(0, first=True)
                with pe.Fori(1, chunks - 1) as i:
                    chunk(i)
                chunk(chunks - 1)
                statistics(KT)

            def embed_gate(layer):
                project(f"ple_gate{layer}", 2, from_a, (in_ready, n.add("in", KT) - KT), stats=True)
                statistics(KT)

            embed_project(0)
            mlp(0)
            embed_gate(0)

            base = n.add("in", KT) - KT
            unit(Place(tab, "conv_in", 0), KT, 256, 2, from_a, (in_ready, base))
            statistics(KT)
            for j in range(1, 6):
                unit(Place(tab, "conv_in", j), KT, 256, 2, from_a)
            for j in range(6, 12):
                unit(Place(tab, "conv_in", j), KT, 256, 2, from_a)
            project("conv_out", 2, from_b, (conv_ready, 0))
            embed_project(1)
            mlp(1)
            embed_gate(1)

            tile = tab.tiles
            pe.wait_ge(x_ready, 7 * KT)
            for a in range(TT):
                for half in range(2):
                    empty(tile)
                    for k in range(4):
                        tr = nc.tensor.transpose(banks[tile % 4][:, k * P:(k + 1) * P],
                                                 wt(X + 4 * half + k)[:, a * P:(a + 1) * P], ident)
                    tr.then_inc(tile_done, 1)
                    tile += 1

        @block.scalar
        def _(act):
            n = Steps()

            def table(name):
                nc.scalar.preload_act_table_set(name)

            def split(pl):
                if not pl.exists:
                    return
                act.wait_ge(raw_landed[pl.slot], pl.landed)
                if pl.freed is not None:
                    act.wait_ge(tile_done, pl.freed)
                nc.scalar.activation(wsp[:, pl.slot, 0, :], raw[:, pl.slot, :], ACT.Copy).then_inc(w_hi, 1)

            def ahead(name, j, i=0, per=0, passes=1):
                split(Place(tab, name, j, i, per, passes, ahead=1))

            def square(src, at, parity):
                if not isinstance(at, int) or at >= 2:
                    act.wait_ge(sq_added, at - 1)
                nc.scalar.activation(sq[:, parity, :], src, ACT.Square).then_inc(sq_done, 1)

            def norm_input(gain, first=False):
                base, x0 = n["in"], n["x"]
                for k in range(KT):
                    if first:
                        act.wait_ge(tile_read, 2 + k + 1)
                    else:
                        act.wait_ge(x_ready, x0 + k + 1)
                    nc.scalar.activation(act_a[:, 0, k, :], wt(X + k), ACT.Copy, scale=col(gain + k)).then_inc(in_hi, 1)
                    square(wt(X + k), n["sq"] + k, (n["sq"] + k) % 2)
                n.add("in", KT)
                n.add("sq", KT)
                if not first:
                    n.add("x", KT)

            def make_rstd(dst, width):
                act.wait_ge(stat_done, n.add("stat"))
                nc.scalar.activation(dst, banks[7][:, :], ACT.Ln, bias=eps[:, :], scale=1.0 / width).then_inc(ln_done, 1)
                act.wait_ge(ln_done, n["stat"])
                nc.scalar.activation(dst, dst, ACT.Exp, scale=-0.5).then_inc(rstd_ready, 1)

            def squares_of(name, tiles_at, passes, per=2):
                base, t0 = n["sq"], tab.tile[tab.first[name]]
                with act.Fori(0, passes) as i:
                    for j in range(per):
                        ahead(name, j, i, per, passes)
                        pl = Place(tab, name, j, i, per, passes)
                        for m in range(2):
                            act.wait_ge(tile_read, pl.tile + m + 1)
                            square(wt(tiles_at + 4 * i + 2 * j + m), base + 4 * i + 2 * j + m, (base + m) % 2)
                n.add("sq", 2 * per * passes)

            def splits(name, passes, per=2):
                with act.Fori(0, passes) as i:
                    for j in range(per):
                        ahead(name, j, i, per, passes)

            table("natural_log_exp_and_others")
            act.wait_ge(prologue_ready, 1)
            act.wait_ge(tile_read, 2)
            norm_input(G_IN, first=True)
            split(Place(tab, "sb_qk", 0))
            ahead("sb_qk", 0)
            make_rstd(rstd[:, :], D)
            for j in range(1, 4):
                ahead("sb_qk", j)
            for j in range(2):
                ahead("sb_v", j)
            table("sigmoid_and_others")
            for j in range(2):
                ahead("sb_gate", j)
                pl = Place(tab, "sb_gate", j)
                for m in range(2):
                    act.wait_ge(tile_read, pl.tile + m + 1)
                    if j:
                        act.wait_ge(silu_done, m + 1)
                    nc.scalar.activation(tmp[:, m, :], wt(TILES["sb"]["gate"] + 2 * j + m), ACT.Sigmoid).then_inc(gate_out, 1)
            table("natural_log_exp_and_others")

            def stage(kind, i, hh, first=False):
                A = ATT[kind]
                qk = QK_PARTS[hh]
                rows = QK if kind == "mla" else HD
                if not first:
                    act.wait_ge(A["summed" if kind == "sb" else "scores"], FREE + TT * (2 * i + hh - 1))
                nc.scalar.activation(qk(0)[0:rows, :], head_rows(kind, "q", i, hh), ACT.Copy, scale=SCALE[kind])\
                    .then_inc(A["stage_hi"], 1)
                nc.scalar.activation(qk(2)[0:rows, :], head_rows(kind, "k", i, hh), ACT.Copy).then_inc(A["stage_hi"], 1)
                if not first:
                    act.wait_ge(A["out"], FREE + 2 * i + hh - 1)
                nc.scalar.activation(head_v[:, hh, 0, :, :], head_values(kind, i, hh), ACT.Copy).then_inc(A["stage_hi"], 1)

            A = ATT["sb"]
            act.wait_ge(tile_read, tab.end[tab.first["sb_v"] + 1])

            def stick_pair(i, last=False):
                for hh in range(2):
                    h = 2 * i + hh
                    for r, kt in enumerate(reversed(range(TT))):
                        t = tmp[:, kt, valid(kt)]
                        act.wait_ge(A["clipped"], 4 * h + r + 1)
                        nc.scalar.activation(t, t, ACT.Exp).then_inc(A["exp"], 1)
                        act.wait_ge(A["exp"], 4 * h + r + 1)
                        nc.scalar.activation(t, t, ACT.Ln, bias=1.0).then_inc(A["softplus"], 1)
                        if r:
                            stick_hi(act, A, h, r - 1, 0)
                    stick_hi(act, A, h, TT - 1, 0)
                    if hh == 0:
                        stage("sb", i, 1)
                    elif not last:
                        stage("sb", i + 1, 0)
                    ahead(BESIDE["sb"], hh, i, 2, SB_HEADS // 2)
                    for r, kt in enumerate(reversed(range(TT))):
                        act.wait_ge(A["summed"], FREE + 4 * h + r + 1)
                        nc.scalar.activation(tmp[:, kt, valid(kt)], banks[kt][:, valid(kt)], ACT.Exp).then_inc(A["w_exp"], 1)
                        if r:
                            stick_hi(act, A, h, r - 1, TT)
                    stick_hi(act, A, h, TT - 1, TT)

            stage("sb", 0, 0, first=True)
            with act.Fori(0, SB_HEADS // 2 - 1) as i:
                stick_pair(i)
            stick_pair(SB_HEADS // 2 - 1, last=True)

            def outputs_hi(kind, pairs):
                for k in range(pairs):
                    act.wait_ge(ATT[kind]["gathered"], FREE + 2 * k + 2)
                    nc.scalar.activation(out_parts(kind, 0, k), output_tile(kind, k), ACT.Copy)\
                        .then_inc(ATT[kind]["o_hi"], 1)

            outputs_hi("sb", SB_HEADS // 2)

            latents = tab.tile[tab.first["c_qkv"]]
            ahead("c_rope", 0)
            for k in range(5):
                act.wait_ge(tile_read, latents + k + 1)
                square(wt(LATENTS[k]), n["sq"], n["sq"] % 2)
                n.add("sq")
            table("sigmoid_and_others")
            for k in range(KT):
                nc.scalar.activation(wt(Y_GATE0 + k), wt(Y_GATE0 + k), ACT.Sigmoid, bias=col(G_BGATE + k))\
                    .then_inc(branch_gate, 1)
            ahead("o_sb", 0)
            for m in range(4):
                nc.scalar.activation(wt(11 + m), wt(TILES["mla"]["gate"] + m), ACT.Sigmoid).then_inc(gate_out, 1)
            table("natural_log_exp_and_others")
            make_rstd(wt(9), Q_LORA)
            make_rstd(wt(10), KV_LORA)
            for k in range(5):
                act.wait_ge(c_normed, k + 1)
                dst = act_b[:, 0, k, :] if k < 3 else head_qk[:, k - 3, :]
                nc.scalar.activation(dst, wt(LATENTS[k]), ACT.Copy).then_inc(c_hi, 1)
            ahead("o_sb", 1)
            for j in range(2):
                ahead("q_up", j)
            ahead("kv_up", 0)

            def softmax_attention(kind, heads):
                A = ATT[kind]

                def exponentials(i, s):
                    j = s % TT
                    act.wait_ge(A["negmax"], 8 * i + s + 1)
                    nc.scalar.activation(tmp[:, s % 4, 0:(j + 1) * P], banks[s % 3][:, 0:(j + 1) * P], ACT.Exp,
                                         bias=negmax[:, s:s + 1], accum_out=rowsum[:, s:s + 1]).then_inc(A["exp"], 1)

                def turned_hi(i, s):
                    hh, j = divmod(s, TT)
                    act.wait_ge(A["turned"], 8 * i + s + 1)
                    if j == 0:
                        act.wait_ge(A["out"], FREE + 2 * i + hh)
                    src = banks[3 + s % 2][:, 0:(j + 1) * P].rearrange("p (b n) -> p b n", b=j + 1)
                    nc.scalar.activation(act_b[:, 0, 0:j + 1, j * P:(j + 1) * P], src, ACT.Copy).then_inc(A["pt_hi"], 1)

                def two_pairs(i, with_unit=True, last=False):
                    for a in range(2):
                        pair = 2 * i + a
                        for what, s in steps(ACT_ORDER):
                            if what == "s":
                                if not (last and a == 1 and s == 2):
                                    stage(kind, pair + s // 2, s % 2)
                            elif what == "w":
                                if with_unit:
                                    ahead(BESIDE[kind], a, i, 2, passes)
                            else:
                                {"e": exponentials, "p": turned_hi}[what](pair, s)

                passes = BESIDE_PASSES[kind]
                stage(kind, 0, 0, first=True)
                with act.Fori(0, heads // 4 - 1) as i:
                    two_pairs(i)
                two_pairs(heads // 4 - 1, with_unit=passes == heads // 4, last=True)
                outputs_hi(kind, heads // 2)

            act.wait_ge(tile_read, tab.end[tab.first["kv_up"]])
            act.wait_ge(rope_spread, 16 * MLA_HEADS)
            softmax_attention("mla", MLA_HEADS)
            table("sigmoid_and_others")
            for k in range(KT):
                nc.scalar.activation(wt(Y_GATE1 + k), wt(Y_GATE1 + k), ACT.Sigmoid, bias=col(G_BGATE + KT + k))\
                    .then_inc(branch_gate, 1)
                if k == 3:
                    ahead("o_mla", 0)
            ahead("o_mla", 1)
            for k in range(KT):
                act.wait_ge(gate_merge, k + 1)
                nc.scalar.activation(act_a[:, 0, k, :], wt(Y_SB + k), ACT.Copy).then_inc(merged_hi, 1)
            table("natural_log_exp_and_others")
            squares_of("w_out", X, 2)
            make_rstd(rstd[:, :], D)

            norm_input(G_NORM2)
            make_rstd(rstd[:, :], D)
            act.wait_ge(decay_done, 1)
            f = tmp[0:FOX_HEADS, 1, :]
            nc.scalar.activation(f, f, ACT.Exp).then_inc(forget_log, 1)
            act.wait_ge(forget_log, 1)
            nc.scalar.activation(f, f, ACT.Ln, bias=1.0).then_inc(forget_log, 1)
            act.wait_ge(decay_done, 2)
            nc.scalar.activation(decay_row[0:FOX_HEADS, 0, :], tmp[0:FOX_HEADS, 2, :], ACT.Copy).then_inc(forget_log, 1)
            for j in range(2):
                ahead("fox_qk", j)
            splits("fox_v", 2)
            act.wait_ge(tile_read, tab.end[tab.first["fox_v"] + 3])
            softmax_attention("fox", FOX_HEADS)

            def mixer_end(name, layer):
                squares_of(name, 8, 2)
                ahead(f"ple_proj{layer}", 0)
                for k in range(2):
                    act.wait_ge(tile_read, tab.extra[f"ple_proj{layer}"] + k + 1)
                    nc.scalar.activation(head_qk[:, k, :], tmp[:, k, :], ACT.Copy).then_inc(p_split, 1)
                make_rstd(rstd[:, :], D)
                ahead(f"ple_proj{layer}", 1)
                norm_input(G_NORM2 + 48 * layer + 16)

            def mlp(layer):
                chunks = D_FF // D
                name = f"mlp{layer}"

                def chunk(i, first=False, last=False):
                    for j in range(8):
                        ahead(name, j, i, 8, chunks)
                        if first and j == 0:
                            make_rstd(rstd[:, :], D)
                        for m in range(2):
                            if j < 4:
                                pl = Place(tab, name, j, i, 8, chunks)
                                act.wait_ge(tile_read, pl.tile + m + 1)
                                nc.scalar.activation(act_b[:, 0, 2 * j + m, :], tmp[:, m, :], ACT.Square)\
                                    .then_inc(hid_hi, 1)
                            elif last:
                                pl = Place(tab, name, j, i, 8, chunks)
                                act.wait_ge(tile_read, pl.tile + m + 1)
                                square(wt(16 + 2 * (j - 4) + m), n["sq"], n["sq"] % 2)
                                n.add("sq")

                chunk(0, first=True)
                with act.Fori(1, chunks - 1) as i:
                    chunk(i)
                chunk(chunks - 1, last=True)
                make_rstd(rstd[:, :], D)
                norm_input(G_NORM2 + 48 * layer + 32)

            def embed_gate(layer):
                name = f"ple_gate{layer}"
                for j in range(4):
                    ahead(name, j)
                    if j == 0:
                        make_rstd(rstd[:, :], D)
                        table("sigmoid_and_others")
                    pl = Place(tab, name, j)
                    for m in range(2):
                        act.wait_ge(tile_read, pl.tile + m + 1)
                        nc.scalar.activation(tmp[:, 2 + m, :], tmp[:, m, :], ACT.Sigmoid).then_inc(gate_out, 1)
                    for m in range(2):
                        act.wait_ge(gated, n.add("gated"))
                        square(wt(2 * j + m), n["sq"], n["sq"] % 2)
                        n.add("sq")
                table("natural_log_exp_and_others")
                make_rstd(rstd[:, :], D)

            mixer_end("fox_out", 0)
            mlp(0)
            embed_gate(0)

            norm_input(G_NORM2 + 48)
            for j in range(12):
                ahead("conv_in", j)
                if j == 0:
                    make_rstd(rstd[:, :], D)
                if j % 3 == 2:
                    for m in range(2):
                        k = 2 * (j // 3) + m
                        act.wait_ge(conv_y, k + 1)
                        nc.scalar.activation(act_b[:, 0, k, :], tmp[:, 2 + m, :], ACT.Copy).then_inc(conv_hi, 1)
            mixer_end("conv_out", 1)
            mlp(1)
            embed_gate(1)

        @block.vector
        def _(dve):
            n = Steps()
            V = nc.vector

            def chain(ins, i=0, per=0):
                ins.then_inc(dve_step, 1)
                dve.wait_ge(dve_step, n.add("step") + per * i)

            def split(pl):
                if not pl.exists:
                    return
                dve.wait_ge(w_hi, pl.u + 1)
                V.tensor_tensor(wsp[:, pl.slot, 1, :], raw[:, pl.slot, :], wsp[:, pl.slot, 0, :].bitcast(F32),
                                ALU.subtract).then_inc(w_split, 1)

            def ahead(name, j, i=0, per=0, passes=1):
                split(Place(tab, name, j, i, per, passes, ahead=1))

            def done(pl, m=0):
                dve.wait_ge(tile_done, pl.tile + m + 1)
                return banks[(pl.bank + m) % 4]

            def scaled(dst, pl, m=0):
                V.tensor_tensor(dst, done(pl, m)[:, :], rstd[:, :], ALU.mult).then_inc(tile_read, 1)

            def wait_rstd(k=1):
                dve.wait_ge(rstd_ready, n.add("stat", k))

            def low(dst, src, hi, sem_, scale=None):
                if scale is None:
                    V.tensor_tensor(dst, src, hi.bitcast(F32), ALU.subtract).then_inc(sem_, 1)
                else:
                    V.scalar_tensor_tensor(out=dst, in0=src, scalar=scale, in1=hi.bitcast(F32), op0=ALU.mult,
                                           op1=ALU.subtract).then_inc(sem_, 1)

            def input_lo(k, gain):
                dve.wait_ge(in_hi, n["in"] + k + 1)
                low(act_a[:, 1, k, :], wt(X + k), act_a[:, 0, k, :], in_ready, col(gain + k))

            def add_normed(tiles_at, gain, next_gain):
                wait_rstd()
                for k in range(KT):
                    m = wt(tiles_at + k)
                    chain(V.scalar_tensor_tensor(out=m, in0=m, scalar=col(gain + k), in1=rstd[:, :], op0=ALU.mult,
                                                 op1=ALU.mult))
                    V.tensor_tensor(wt(X + k), wt(X + k), m, ALU.add).then_inc(x_ready, 1)
                    if k and next_gain is not None:
                        input_lo(k - 1, next_gain)
                if next_gain is not None:
                    input_lo(KT - 1, next_gain)
                    n.add("in", KT)

            def project(name, passes, tiles_at, factor=True, first=0):
                with dve.Fori(first, passes) as i:
                    for j in range(2):
                        ahead(name, j, i, 2, passes)
                        pl = Place(tab, name, j, i, 2, passes)
                        for m in range(2):
                            dst = wt(tiles_at + 4 * i + 2 * j + m)
                            if factor:
                                scaled(dst, pl, m)
                            else:
                                V.tensor_copy(dst, done(pl, m)[:, :]).then_inc(tile_read, 1)

            def values_out(name, j, at, width, i=0, per=0, passes=1):
                pl = Place(tab, name, j, i, per, passes)
                ahead(name, j, i, per, passes)
                for a in range(TT):
                    c = at * S + a * width + 256 * j
                    V.tensor_scalar(work[:, bass.ds(c + 256 * per * i, 256)], done(pl, a)[:, 0:256],
                                    rstd_tok[:, a:a + 1], None, ALU.mult).then_inc(tile_read, 1)

            def turned_rstd():
                dve.wait_ge(rstd_turned, n.add("turned"))
                V.tensor_copy(rstd_tok[:, :], banks[7][:, 0:TT]).then_inc(rstd_tok_ready, 1)
                dve.wait_ge(rstd_tok_ready, n["turned"])

            V.memset(eps[:, :], EPS).then_inc(prologue_ready, 1)
            marks = [(kind, what) for kind in ATT for what in STARTS_FREE[kind]]
            for mark, (kind, what) in enumerate(marks):
                V.memset(free_mark[:, mark:mark + 1], 0.0).then_inc(ATT[kind][what], FREE)
            tile = tab.extra["sb_qk"]
            for at, width in ((0, 120), (120, 37)):
                dve.wait_ge(tile_done, tile + 1)
                V.tensor_copy(gains[:, at:at + width], banks[tile % 4][:, 0:width]).then_inc(tile_read, 1)
                tile += 1
            for k in range(KT):
                dve.wait_ge(tile_done, tile + 1)
                V.tensor_copy(wt(X + k), banks[tile % 4][:, :]).then_inc(tile_read, 1)
                tile += 1
                if k:
                    dve.wait_ge(tile_read, tile - 1)
                    input_lo(k - 1, G_IN)
            dve.wait_ge(tile_read, tile)
            input_lo(KT - 1, G_IN)
            n.add("in", KT)
            split(Place(tab, "sb_qk", 0))
            ahead("sb_qk", 0)
            for dst, src in ((identr[:, :], ident), (trir[:, :], rest["tri"]), (negonesr[:, :], rest["negones"]),
                             (maskr[:, 0, :], rest["foxmask"]), (maskr[:, 1, :], rest["mlamask"]),
                             (maskr[:, 2, :], rest["sbmask"])):
                V.tensor_copy(dst, src).then_inc(const_split, 1)
            V.tensor_copy(onesr[:, :], ones[0:48, :]).then_inc(const_split, 1)
            wf_flat = wf[:, :, :, :].rearrange("p a k n -> p a (k n)")
            V.tensor_copy(wf_flat[:, 0, :], wf_raw[:, :]).then_inc(const_split, 1)
            dve.wait_ge(const_split, CONST_SPLITS - 1)
            low(wf_flat[:, 1, :], wf_raw[:, :], wf_flat[:, 0, :], const_split)

            wait_rstd()
            pl = Place(tab, "sb_qk", 0)
            for m in range(2):
                scaled(wt(m), pl, m)
            ahead("sb_qk", 1)
            pl = Place(tab, "sb_qk", 1)
            for m in range(2):
                scaled(wt(2 + m), pl, m)
            project("sb_qk", 2, 0, first=1)
            turned_rstd()
            for j in range(2):
                values_out("sb_v", j, TILES["sb"]["v"], SB_HEADS * HD)

            def silu(at, sigmoid):
                dve.wait_ge(gate_out, n.add("gate"))
                V.tensor_tensor(wt(at), wt(at), sigmoid, ALU.mult).then_inc(silu_done, 1)

            for j in range(2):
                pl = Place(tab, "sb_gate", j)
                ahead("sb_gate", j)
                for m in range(2):
                    scaled(wt(TILES["sb"]["gate"] + 2 * j + m), pl, m)
                for m in range(2):
                    silu(TILES["sb"]["gate"] + 2 * j + m, tmp[:, m, :])

            def stage(kind, i, hh):
                A = ATT[kind]
                qk = QK_PARTS[hh]
                rows = QK if kind == "mla" else HD
                first = 3 * (2 * i + hh)
                dve.wait_ge(A["stage_hi"], first + 1)
                low(qk(1)[0:rows, :], head_rows(kind, "q", i, hh), qk(0)[0:rows, :], A["staged"], SCALE[kind])
                dve.wait_ge(A["stage_hi"], first + 2)
                low(qk(3)[0:rows, :], head_rows(kind, "k", i, hh), qk(2)[0:rows, :], A["staged"])
                dve.wait_ge(A["stage_hi"], first + 3)
                low(head_v[:, hh, 1, :, :], head_values(kind, i, hh), head_v[:, hh, 0, :, :], A["staged"])
                if kind == "fox":
                    pick = consts[0:48, bass.ds(ccols["sel"].start + 2 * i + hh, 1)]
                    V.tensor_scalar(decay_row[:, hh, :], decay_parts, pick, None, ALU.mult).then_inc(A["staged"], 1)

            def beside_out(dst, pl, m):
                dve.wait_ge(tile_done, pl.tile + m + 1)
                V.tensor_tensor(dst, banks[6 + m][:, :], rstd[:, :], ALU.mult).then_inc(tile_read, 1)

            def clear_padding():
                V.memset(act_b[:, 0:2, TT - 1, 2 * P:3 * P].bitcast(F32), 0.0).then_inc(pad_zero, 1)

            def gather(kind, i, hh):
                A = ATT[kind]
                dve.wait_ge(A["out"], FREE + 2 * i + hh + 1)
                rows = slice(hh * HD, (hh + 1) * HD)
                src, dst = banks[4 + hh if kind == "sb" else 5][0:HD, :], output_tile(kind, i)[rows, :]
                if kind == "fox":
                    V.tensor_scalar(dst, src, 1.0, None, ALU.mult).then_inc(A["gathered"], 1)
                else:
                    V.tensor_tensor(dst, src, wt(TILES[kind]["gate"] + i)[rows, :], ALU.mult).then_inc(A["gathered"], 1)

            def outputs_lo(kind, pairs):
                A = ATT[kind]
                for k in range(pairs):
                    dve.wait_ge(A["o_hi"], k + 1)
                    low(out_parts(kind, 1, k), output_tile(kind, k), out_parts(kind, 0, k), A["o_ready"])

            A = ATT["sb"]
            dve.wait_ge(stash_saved, 16)
            clear_padding()
            dve.wait_ge(silu_done, 4)
            dve.wait_ge(tile_read, tab.end[tab.first["sb_v"] + 1])

            def stick_pair(i, last=False):
                for hh in range(2):
                    h = 2 * i + hh

                    def part_lo(r, offset):
                        kt = TT - 1 - r
                        dve.wait_ge(A["part_hi"], 8 * h + offset + r + 1)
                        low(act_b[:, 1, kt, valid(kt)], tmp[:, kt, valid(kt)], act_b[:, 0, kt, valid(kt)], A["part_ready"])

                    def clip(r):
                        kt = TT - 1 - r
                        dve.wait_ge(A["scores"], 4 * h + r + 1)
                        V.tensor_scalar(tmp[:, kt, valid(kt)], banks[kt][:, valid(kt)], SOFTPLUS_LINEAR, None, ALU.min)                            .then_inc(A["clipped"], 1)

                    def softplus(r):
                        kt = TT - 1 - r
                        t = tmp[:, kt, valid(kt)]
                        dve.wait_ge(A["softplus"], 4 * h + r + 1)
                        V.tensor_tensor(t, banks[kt][:, valid(kt)], t, ALU.max).then_inc(A["normed"], 1)

                    clip(0)
                    clip(1)
                    softplus(0)
                    clip(2)
                    softplus(1)
                    part_lo(0, 0)
                    clip(3)
                    softplus(2)
                    part_lo(1, 0)
                    softplus(3)
                    part_lo(2, 0)
                    part_lo(3, 0)
                    if hh == 0:
                        stage("sb", i, 1)
                    elif not last:
                        stage("sb", i + 1, 0)
                    ahead(BESIDE["sb"], hh, i, 2, SB_HEADS // 2)
                    for r in range(TT):
                        part_lo(r, TT)
                    pl = Place(tab, BESIDE["sb"], hh, i, 2, SB_HEADS // 2)
                    for m in range(2):
                        beside_out(wt(16 + 4 * i + 2 * hh + m), pl, m)
                    gather("sb", i, hh)

            stage("sb", 0, 0)
            with dve.Fori(0, SB_HEADS // 2 - 1) as i:
                stick_pair(i)
            stick_pair(SB_HEADS // 2 - 1, last=True)
            outputs_lo("sb", SB_HEADS // 2)

            ahead("c_rope", 0)
            pl = Place(tab, "c_rope", 0)
            scaled(wt(LATENTS[4]), pl)
            V.tensor_tensor(tmp[0:32, 2, :], done(pl, 1)[0:32, :], rstd[0:32, :], ALU.mult).then_inc(tile_read, 1)
            ahead("o_sb", 0)

            def gated_output(j):
                pl = Place(tab, "o_sb", j)
                for m in range(4):
                    k = 4 * j + m
                    dve.wait_ge(branch_gate, k + 1)
                    V.tensor_tensor(wt(Y_SB + k), done(pl, m)[:, :], wt(Y_GATE0 + k), ALU.mult).then_inc(tile_read, 1)

            dve.wait_ge(rope_swapped, 32)
            V.tensor_tensor(tmp[0:32, 3, :], tmp[32:64, 2, :], rope[32:64, :], ALU.mult).then_inc(dve_step, 1)
            V.tensor_tensor(tmp[0:32, 2, :], tmp[0:32, 2, :], rope[0:32, :], ALU.mult).then_inc(dve_step, 1)
            dve.wait_ge(dve_step, n.add("step", 2))
            V.tensor_tensor(tmp[0:32, 2, :], tmp[0:32, 2, :], tmp[0:32, 3, :], ALU.add).then_inc(rope_k, 1)
            gated_output(0)
            for k in range(5):
                if k in (0, 3):
                    wait_rstd()
                c = wt(LATENTS[k])
                V.scalar_tensor_tensor(out=c, in0=c, scalar=col((G_Q if k < 3 else G_KV - 3) + k),
                                       in1=wt(9 if k < 3 else 10), op0=ALU.mult, op1=ALU.mult).then_inc(c_normed, 1)
            for k in range(5):
                dve.wait_ge(c_hi, k + 1)
                parts = [act_b[:, hl, k, :] if k < 3 else head_qk[:, 2 * hl + k - 3, :] for hl in (0, 1)]
                low(parts[1], wt(LATENTS[k]), parts[0], c_ready)
            ahead("o_sb", 1)
            gated_output(1)
            for m in range(4):
                silu(TILES["mla"]["gate"] + m, wt(11 + m))
            for j in range(2):
                pl = Place(tab, "q_up", j)
                ahead("q_up", j)
                for m in range(4):
                    bank, dst = done(pl, m), wt(TILES["mla"]["q"] + 4 * j + m)
                    V.tensor_copy(dst[0:HD, :], bank[0:HD, :]).then_inc(dve_step, 1)
                    parts = [tmp[64:96, 2 * (m % 2) + a, :] for a in (0, 1)]
                    dve.wait_ge(tile_read, pl.tile + m - 1)
                    V.tensor_tensor(parts[0], bank[96:128, :], rope[96:128, :], ALU.mult).then_inc(dve_step, 1)
                    V.tensor_tensor(parts[1], bank[64:96, :], rope[64:96, :], ALU.mult).then_inc(dve_step, 1)
                    dve.wait_ge(dve_step, n.add("step", 3))
                    V.tensor_tensor(dst[64:96, :], parts[0], parts[1], ALU.add).then_inc(tile_read, 1)
            pl = Place(tab, "kv_up", 0)
            ahead("kv_up", 0)
            for h in range(MLA_HEADS):
                V.tensor_copy(wt(TILES["mla"]["k"] + h)[0:HD, :], done(pl, h)[0:HD, :]).then_inc(tile_read, 1)
            for a in range(TT):
                V.tensor_copy(wt(TILES["mla"]["v"] + a), done(pl, MLA_HEADS + a)[:, :]).then_inc(tile_read, 1)

            def softmax_attention(kind, heads):
                A = ATT[kind]

                def maxima(i, s):
                    dve.wait_ge(A["scores"], FREE + 8 * i + s + 1)
                    V.reduce_max(negmax[:, s:s + 1], banks[s % 3][:, 0:(s % TT + 1) * P], AX, negate=True)                        .then_inc(A["negmax"], 1)

                def normalize(i, s):
                    dve.wait_ge(A["exp"], 8 * i + s + 1)
                    V.reciprocal(rinv[:, s:s + 1], rowsum[:, s:s + 1]).then_inc(A["step"], 1)
                    dve.wait_ge(A["step"], 8 * i + s + 1)
                    t = tmp[:, s % 4, 0:(s % TT + 1) * P]
                    V.tensor_scalar(t, t, rinv[:, s:s + 1], None, ALU.mult).then_inc(A["normed"], 1)

                def turned_lo(i, s):
                    j = s % TT
                    dve.wait_ge(A["pt_hi"], 8 * i + s + 1)
                    src = banks[3 + s % 2][:, 0:(j + 1) * P].rearrange("p (b n) -> p b n", b=j + 1)
                    dst = [act_b[:, hl, 0:j + 1, j * P:(j + 1) * P] for hl in (0, 1)]
                    low(dst[1], src, dst[0], A["pt_ready"])

                def unit_out(i, a, m):
                    pair = 2 * i + a
                    at = Y_GATE1 + 2 * pair + m if kind == "mla" else TILES["fox"][("q", "k")[m]] + pair + 2
                    beside_out(wt(at), Place(tab, BESIDE[kind], a, i, 2, passes), m)

                def two_pairs(i, with_unit=True, last=False):
                    for a in range(2):
                        pair = 2 * i + a
                        for what, s in steps(DVE_ORDER):
                            if what == "s":
                                if not (last and a == 1 and s == 2):
                                    stage(kind, pair + s // 2, s % 2)
                            elif what == "g":
                                gather(kind, pair, s)
                            elif what in "wx":
                                if with_unit and what == "w":
                                    ahead(BESIDE[kind], a, i, 2, passes)
                                elif with_unit:
                                    unit_out(i, a, s)
                            else:
                                {"m": maxima, "n": normalize, "p": turned_lo}[what](pair, s)

                passes = BESIDE_PASSES[kind]
                stage(kind, 0, 0)
                with dve.Fori(0, heads // 4 - 1) as i:
                    two_pairs(i)
                two_pairs(heads // 4 - 1, with_unit=passes == heads // 4, last=True)
                outputs_lo(kind, heads // 2)

            dve.wait_ge(rope_spread, 16 * MLA_HEADS)
            dve.wait_ge(tile_read, tab.end[tab.first["kv_up"]])
            clear_padding()
            softmax_attention("mla", MLA_HEADS)
            def merged_lo(k):
                dve.wait_ge(merged_hi, k + 1)
                low(act_a[:, 1, k, :], wt(Y_SB + k), act_a[:, 0, k, :], merged)

            for j in range(2):
                pl = Place(tab, "o_mla", j)
                ahead("o_mla", j)
                for m in range(4):
                    k = 4 * j + m
                    dve.wait_ge(branch_gate, KT + k + 1)
                    V.tensor_tensor(wt(Y_GATE1 + k), done(pl, m)[:, :], wt(Y_GATE1 + k), ALU.mult).then_inc(tile_read, 1)
                    dve.wait_ge(tile_read, pl.tile + m + 1)
                    V.tensor_tensor(wt(Y_SB + k), wt(Y_SB + k), wt(Y_GATE1 + k), ALU.add).then_inc(gate_merge, 1)
                    if k:
                        merged_lo(k - 1)
            merged_lo(KT - 1)
            dve.wait_ge(stash_back, 16)
            with dve.Fori(0, 2) as i:
                for j in range(2):
                    ahead("w_out", j, i, 2, 2)
                    pl = Place(tab, "w_out", j, i, 2, 2)
                    for m in range(2):
                        x = wt(X + 4 * i + 2 * j + m)
                        V.tensor_tensor(x, done(pl, m)[:, :], x, ALU.add).then_inc(tile_read, 1)
            wait_rstd()
            dve.wait_ge(tile_read, tab.end[tab.first["w_out"] + 3])
            for k in range(KT):
                V.scalar_tensor_tensor(out=wt(X + k), in0=wt(X + k), scalar=col(G_F + k), in1=rstd[:, :], op0=ALU.mult,
                                       op1=ALU.mult).then_inc(x_ready, 1)
                if k:
                    dve.wait_ge(x_ready, k)
                    input_lo(k - 1, G_NORM2)
            dve.wait_ge(x_ready, KT)
            input_lo(KT - 1, G_NORM2)
            n.add("in", KT)

            wait_rstd()
            tile = tab.extra["fox_qk"]
            f, t, total = (tmp[0:FOX_HEADS, a, :] for a in range(3))
            dve.wait_ge(tile_done, tile + 1)
            V.tensor_tensor(f, banks[tile % 4][0:FOX_HEADS, :], rstd[0:FOX_HEADS, :], ALU.mult).then_inc(tile_read, 1)
            dve.wait_ge(tile_read, tile + 1)
            chain(V.tensor_scalar(f, f, b_forget[:, :], None, ALU.add))
            V.tensor_scalar(t, f, -1.0, SOFTPLUS_LINEAR, ALU.mult, ALU.min).then_inc(decay_done, 1)
            dve.wait_ge(forget_log, 2)
            chain(V.scalar_tensor_tensor(out=t, in0=f, scalar=-1.0, in1=t, op0=ALU.mult, op1=ALU.max))
            V.tensor_tensor_scan(total, t, t, 0.0, ALU.add, ALU.max).then_inc(decay_done, 1)
            for j in range(2):
                ahead("fox_qk", j)
                for m in range(2):
                    scaled(wt(TILES["fox"][("q", "k")[m]] + j), Place(tab, "fox_qk", j), m)
            turned_rstd()
            dve.wait_ge(forget_log, 3)
            chain(V.memset(decay_parts, 0.0))
            hi = decay_row[0:FOX_HEADS, 0, :].bitcast(F32)
            V.tensor_copy(decay_parts[0:FOX_HEADS, :], hi).then_inc(dve_step, 1)
            n.add("step")
            chain(V.tensor_tensor(decay_parts[32:32 + FOX_HEADS, :], total, hi, ALU.subtract))
            with dve.Fori(0, 2) as i:
                for j in range(2):
                    values_out("fox_v", j, 16, FOX_HEADS * HD, i, 2, 2)
            dve.wait_ge(tile_read, tab.end[tab.first["fox_v"] + 3])
            clear_padding()
            softmax_attention("fox", FOX_HEADS)

            def mixer_end(name, layer):
                project(name, 2, 8, factor=False)
                tile = tab.extra[f"ple_proj{layer}"]
                ahead(f"ple_proj{layer}", 0)
                for k in range(2):
                    dve.wait_ge(tile_done, tile + k + 1)
                    V.tensor_copy(tmp[:, k, :], banks[(tile + k) % 4][:, :]).then_inc(tile_read, 1)
                dve.wait_ge(tile_read, tile + 2)
                for k in range(2):
                    dve.wait_ge(p_split, 2 * layer + k + 1)
                    low(head_qk[:, 2 + k, :], tmp[:, k, :], head_qk[:, k, :], p_ready)
                for j in range(2):
                    pl = Place(tab, f"ple_proj{layer}", j)
                    if j:
                        ahead(f"ple_proj{layer}", j)
                    for m in range(4):
                        V.tensor_copy(wt(4 * j + m), done(pl, m)[:, :]).then_inc(tile_read, 1)
                add_normed(8, G_NORM2 + 48 * layer + 8, G_NORM2 + 48 * layer + 16)

            def mlp(layer):
                chunks = D_FF // D
                name = f"mlp{layer}"
                hid = n["hid"]
                for k in range(KT):
                    V.memset(wt(16 + k), 0.0).then_inc(sum_zero, 1)
                dve.wait_ge(sum_zero, n.add("zero", KT))

                def chunk(i, first=False):
                    for j in range(8):
                        ahead(name, j, i, 8, chunks)
                        pl = Place(tab, name, j, i, 8, chunks)
                        if first and j == 0:
                            wait_rstd()
                        if j < 4:
                            h = hid + KT * i + 2 * j
                            for m in range(2):
                                V.scalar_tensor_tensor(out=tmp[:, m, :], in0=done(pl, m)[:, :], scalar=0.0,
                                                       in1=rstd[:, :], op0=ALU.max, op1=ALU.mult).then_inc(tile_read, 1)
                            for m in range(2):
                                dve.wait_ge(tile_read, pl.tile + m + 1)
                                V.tensor_tensor(tmp[:, 2 + m, :], tmp[:, m, :], tmp[:, m, :], ALU.mult)                                    .then_inc(hid_square, 1)
                            for m in range(2):
                                dve.wait_ge(hid_square, h + m + 1)
                                dve.wait_ge(hid_hi, h + m + 1)
                                k = 2 * j + m
                                low(act_b[:, 1, k, :], tmp[:, 2 + m, :], act_b[:, 0, k, :], hid_ready)
                        else:
                            for m in range(2):
                                t = wt(16 + 2 * (j - 4) + m)
                                V.tensor_tensor(t, done(pl, m)[:, :], t, ALU.add).then_inc(tile_read, 1)

                chunk(0, first=True)
                with dve.Fori(1, chunks - 1) as i:
                    chunk(i)
                chunk(chunks - 1)
                n.add("hid", KT * chunks)
                add_normed(16, G_NORM2 + 48 * layer + 24, G_NORM2 + 48 * layer + 32)

            def embed_gate(layer):
                name = f"ple_gate{layer}"
                for j in range(4):
                    ahead(name, j)
                    pl = Place(tab, name, j)
                    if j == 0:
                        wait_rstd()
                    for m in range(2):
                        scaled(tmp[:, m, :], pl, m)
                    for m in range(2):
                        dve.wait_ge(gate_out, n.add("gate"))
                        e = wt(2 * j + m)
                        V.tensor_tensor(e, e, tmp[:, 2 + m, :], ALU.mult).then_inc(gated, 1)
                dve.wait_ge(gated, KT * (layer + 1))
                add_normed(0, G_NORM2 + 48 * layer + 40, G_NORM2 + 48 if layer == 0 else None)

            mixer_end("fox_out", 0)
            mlp(0)
            embed_gate(0)

            padded = [work[:, (2 + 2 * m) * S:(2 + 2 * m) * S + S + 2] for m in range(2)]
            for m in range(2):
                V.memset(padded[m][:, 0:2], 0.0).then_inc(conv_pad, 1)
            for j in range(12):
                ahead("conv_in", j)
                pl = Place(tab, "conv_in", j)
                if j == 0:
                    wait_rstd()
                part, pair = j % 3, j // 3
                if part == 0:
                    for m in range(2):
                        scaled(wt(m), pl, m)
                elif part == 1:
                    for m in range(2):
                        scaled(tmp[:, m, :], pl, m)
                    dve.wait_ge(tile_read, pl.tile + 2)
                    for m in range(2):
                        V.tensor_tensor(padded[m][:, 2:S + 2], tmp[:, m, :], wt(m), ALU.mult).then_inc(dve_step, 1)
                    n.add("step", 2)
                    dve.wait_ge(dve_step, n["step"])
                    if pair == 0:
                        dve.wait_ge(conv_pad, 2)
                    for tap in range(3):
                        for m in range(2):
                            w = col(G_CONV + KT * tap + 2 * pair + m)
                            src = padded[m][:, tap:tap + S]
                            if tap == 0:
                                ins_ = V.tensor_scalar(tmp[:, m, :], src, w, None, ALU.mult)
                            else:
                                ins_ = V.scalar_tensor_tensor(out=tmp[:, m, :], in0=src, scalar=w, in1=tmp[:, m, :],
                                                              op0=ALU.mult, op1=ALU.add)
                            ins_.then_inc(dve_step, 1)
                        n.add("step", 2)
                        dve.wait_ge(dve_step, n["step"])
                else:
                    for m in range(2):
                        scaled(tmp[:, 2 + m, :], pl, m)
                    dve.wait_ge(tile_read, pl.tile + 2)
                    for m in range(2):
                        V.tensor_tensor(tmp[:, 2 + m, :], tmp[:, 2 + m, :], tmp[:, m, :], ALU.mult).then_inc(conv_y, 1)
                    for m in range(2):
                        k = 2 * pair + m
                        dve.wait_ge(conv_y, k + 1)
                        dve.wait_ge(conv_hi, k + 1)
                        low(act_b[:, 1, k, :], tmp[:, 2 + m, :], act_b[:, 0, k, :], conv_ready)
            mixer_end("conv_out", 1)
            mlp(1)
            embed_gate(1)

            tile = tab.tiles
            for a in range(2 * TT):
                dve.wait_ge(tile_done, tile + 1)
                V.tensor_copy(wt(a), banks[tile % 4][:, :]).then_inc(tile_read, 1)
                tile += 1

        @block.gpsimd
        def _(pool):
            n = Steps()

            def sum_squares(tiles):
                if n["stat"]:
                    pool.wait_ge(stat_done, n["stat"])
                nc.gpsimd.memset(ssum[:, :], 0.0).then_inc(sq_zero, 1)
                pool.wait_ge(sq_zero, n.add("stat"))
                base = n.add("sq", tiles) - tiles

                def add(at, parity):
                    pool.wait_ge(sq_done, at + 1)
                    nc.gpsimd.tensor_tensor(ssum[:, :], ssum[:, :], sq[:, parity, :], ALU.add).then_inc(sq_added, 1)
                    pool.wait_ge(sq_added, at + 1)

                if tiles == KT:
                    with pool.Fori(0, KT // 2) as i:
                        for m in range(2):
                            add(base + 2 * i + m, (base + m) % 2)
                else:
                    for k in range(tiles):
                        add(base + k, (base + k) % 2)

            sum_squares(KT)
            A = ATT["sb"]
            with pool.Fori(0, SB_HEADS // 2) as i:
                for hh in range(2):
                    h = 2 * i + hh
                    for r in range(TT):
                        kt = TT - 1 - r
                        diagonal = tmp[:, kt, kt * P:(kt + 1) * P]
                        pool.wait_ge(A["normed"], 4 * h + r + 1)
                        nc.gpsimd.tensor_tensor(diagonal, diagonal, strict, ALU.mult).then_inc(A["masked"], 1)
            sum_squares(Q_LORA // P)
            sum_squares(KV_LORA // P)
            for norm in range(13):
                if norm == 2:
                    pool.wait_ge(ATT["fox"]["staged"], 4 * FOX_HEADS)
                sum_squares(KT)



_INS = ["x", "norm_in_g", "w_in", "b_gate", "q_norm_g", "w_q_up", "kv_norm_g", "w_kv_up", "w_o_sb", "w_o_mla", "w_out",
        "norm_f_g", "p_2", "norm_g_2", "w_attn_in_2", "b_forget_2", "w_attn_out_2", "w_conv_in_2", "conv_w_2",
        "w_conv_out_2", "w_mlp_up_2", "w_mlp_down_2", "w_ple_proj_2", "w_ple_gate_2"]


def kernel(**inputs):
    import numpy as _np
    import concourse.bacc as _bacc
    from concourse import mybir as _mybir
    from concourse.bass_utils import run_bass_kernel_spmd as _run

    nc = _bacc.Bacc("TRN2", target_bir_lowering=False, num_devices=1, dynamic_dma_scratch_size=1024)
    arrays, args = {}, {}
    for name in _INS:
        arrays[f"in_{name}"] = _np.ascontiguousarray(inputs[name])
    arrays["in_consts"] = constants()
    for name, a in arrays.items():
        args[name[3:]] = nc.dram_tensor(name, a.shape, _mybir.dt.from_np(a.dtype), kind="ExternalInput").ap()
    out = nc.dram_tensor("out_0", (1, S, D), F32, kind="ExternalOutput").ap()
    hybrid_block_kernel(nc, args, out)
    r = _run(nc, [arrays], core_ids=[0])
    return r.results[0]["out_0"]
```

```python
from contextlib import ExitStack

import concourse.bass as bass
import numpy as np
from concourse import mybir

F32 = mybir.dt.float32
F32R = mybir.dt.float32r
ALU = mybir.AluOpType
ACT = mybir.ActivationFunctionType
AX = mybir.AxisListType.X

P = 128
S = 512
D = 1024
KT = D // P
TT = S // P
HD = 64
SB_HEADS = MLA_HEADS = 8
FOX_HEADS = 16
QK = 96
ROPE = 32
Q_LORA, KV_LORA = 384, 256
D_FF = 4096
CHUNK = 64
EPS = 1e-6
FREE = 1
MASKED = -float(2.0 ** 100)
SOFTPLUS_LINEAR = 20.0
UNIT = 2048
CONST_COLS = dict(ident=128, ones=128, sel=16, rope=S, strict=128, tri=128, negones=128, foxmask=384, mlamask=384, sbmask=384)
KEPT = 128 + 128 + 16 + S + 128
CONST_LOADS = 8
LATE_LOADS = 4
X_CHUNKS = 4
CONST_SPLITS = 9


def const_offsets():
    at, out = 0, {}
    for name, n in CONST_COLS.items():
        out[name] = slice(at, at + n)
        at += n
    return out, at


def constants():
    cols, width = const_offsets()
    c = np.zeros((P, width), np.float32)
    row, col = np.arange(P)[:, None], np.arange(P)[None, :]
    c[:, cols["ident"]] = np.eye(P)
    c[:, cols["tri"]] = np.where(row >= col, -1.0, 0.0)
    c[:, cols["negones"]] = -1.0
    c[:, cols["ones"]] = 1.0
    c[:, cols["strict"]] = np.where(row < col, 1.0, 0.0)
    c[:, cols["sbmask"]][:, P:2 * P] = np.where(row < col, 0.0, MASKED)
    c[:, cols["foxmask"]][:, P:2 * P] = np.where(col <= row, 0.0, MASKED)
    c[:, cols["mlamask"]][:, P:2 * P] = np.where(col // CHUNK <= row // CHUNK, 0.0, MASKED)
    for h in range(FOX_HEADS):
        c[h, cols["sel"].start + h] = 1.0
        c[32 + h, cols["sel"].start + h] = 1.0
    half = ROPE // 2
    inv_freq = (np.float32(10000.0) ** (-np.arange(half, dtype=np.float32) / np.float32(half))).astype(np.float32)
    ang = np.arange(S, dtype=np.float32)[None, :] * inv_freq[:, None]
    cos, sin = np.cos(ang), np.sin(ang)
    c[0:64, cols["rope"]] = 1.0
    c[64:96, cols["rope"]] = np.concatenate([cos, cos])
    c[96:128, cols["rope"]] = np.concatenate([-sin, sin])
    return c


SB_Q, SB_K, SB_V, SB_GATE, C_Q = 0, 512, 1024, 1536, 2048
K_ROPE = C_Q + Q_LORA + KV_LORA
MLA_GATE = K_ROPE + ROPE
GATES = MLA_GATE + 512

UNIT_GROUPS = [
    ("sb_qk", 4, 2, 1), ("sb_v", 2, 4, 1), ("sb_gate", 2, 2, 1),
    ("gate0", 4, 2, 1), ("mla_gate", 2, 2, 1), ("c_qkv", 2, 2, 1),
    ("c_rope", 1, 2, 1), ("o_sb", 2, 4, 1), ("q_up", 2, 4, 12), ("kv_up", 1, 12, 1),
    ("gate1", 4, 2, 1),
    ("o_mla", 2, 4, 1), ("w_out", 4, 2, 1), ("fox_qk", 2, 2, 2), ("fox_v", 4, 4, 1),
    ("fox_qk_next", 6, 2, 2),
    ("fox_out", 4, 2, 2),
    ("ple_first0", 1, 4, 1), ("mlp0", 32, 2, 1), ("ple_second0", 1, 4, 1), ("ple_gate0", 4, 2, 1),
    ("conv_in", 12, 2, 1), ("conv_out", 4, 2, 1),
    ("ple_first1", 1, 4, 1), ("mlp1", 32, 2, 1), ("ple_second1", 1, 4, 1), ("ple_gate1", 4, 2, 1),
]
EXTRA_TILES = {"sb_qk": 2 + KT, "fox_v": 1, "fox_out": 2, "conv_out": 2}
FILLERS = ("ple_first0", "ple_second0", "ple_first1", "ple_second1")


class UnitTable:

    def __init__(self):
        self.first = {}
        self.tile = []
        self.end = []
        self.landed = []
        self.extra = {}
        self.filler = []
        t, slots = 0, [0, 0]
        for name, n, tiles, dmas in UNIT_GROUPS:
            self.first[name] = len(self.tile)
            self.extra[name] = t
            t += EXTRA_TILES.get(name, 0)
            for _ in range(n):
                self.tile.append(t)
                self.filler.append(name in FILLERS)
                t += tiles
                self.end.append(t)
                slots[len(self.landed) % 2] += 16 * dmas
                self.landed.append(slots[len(self.landed) % 2])
        self.count = len(self.tile)
        self.tiles = t


class Place:

    def __init__(self, tab, name, j, i=0, per=0, passes=1, ahead=0):
        assert per % 2 == 0
        self.tab, self.i, self.per, self.passes = tab, i, per, passes
        self.at = tab.first[name] + j + ahead
        self.slot = self.at % 2
        self.exists = self.at < tab.count
        self.u = self.at + per * i

    @property
    def filler(self):
        return isinstance(self.u, int) and self.tab.filler[self.u]

    @property
    def split_cols(self):
        return slice(UNIT // 2, UNIT) if self.filler else slice(0, UNIT)

    @property
    def raw_cols(self):
        return slice(0, UNIT // 2) if self.filler else slice(0, UNIT)

    def column(self, column, v):
        step = 0
        if self.passes > 1 and self.per:
            step = column[v + self.per] - column[v]
            assert all(column[v + self.per * n] == column[v] + step * n for n in range(self.passes))
        return column[v] + step * self.i

    @property
    def landed(self):
        return self.column(self.tab.landed, self.at)

    @property
    def tile(self):
        return self.column(self.tab.tile, self.at)

    @property
    def bank(self):
        assert self.passes == 1 or not self.per or (self.tab.tile[self.at + self.per] - self.tab.tile[self.at]) % 4 == 0
        return self.tab.tile[self.at] % 4

    @property
    def freed(self):
        if self.at < 2:
            return None
        return self.tab.end[self.at - 2] if self.passes == 1 else self.column(self.tab.tile, self.at - 1)

    @property
    def half_freed(self):
        return self.tab.end[self.at - (4 if self.tab.filler[self.at - 2] else 2)]


class Steps:

    def __init__(self):
        self.n = {}

    def add(self, name, k=1):
        self.n[name] = self.n.get(name, 0) + k
        return self.n[name]

    def __getitem__(self, name):
        return self.n.get(name, 0)


def hybrid_block_kernel(nc, ins, out):
    tab = UnitTable()
    ccols, cwidth = const_offsets()

    ctx = ExitStack()
    with ctx:
        def sb(name, shape, dt=F32):
            return ctx.enter_context(nc.sbuf_tensor(name, shape, dt))

        def sem(name):
            return ctx.enter_context(nc.semaphore(name))

        raw = sb("raw_weights", [P, 2, UNIT])
        wsp = sb("split_weights", [P, 2, 2, UNIT], F32R)
        act_a = sb("act_a", [P, 2, KT, S], F32R)
        act_b = sb("act_b", [P, 2, KT, S], F32R)
        head_qk = sb("head_qk", [P, 4, S], F32R)
        head_v = sb("head_v", [P, 2, 2, TT, HD], F32R)
        decay_row = sb("decay_row", [48, 2, S], F32R)
        consts = sb("consts", [P, KEPT])
        identr = sb("identr", [P, P], F32R)
        trir = sb("trir", [P, P], F32R)
        negonesr = sb("negonesr", [P, P], F32R)
        onesr = sb("onesr", [48, P], F32R)
        maskr = sb("maskr", [P, 3, 384], F32R)
        wf_raw = sb("wf_raw", [P, KT * FOX_HEADS])
        wf = sb("wf", [P, 2, KT, FOX_HEADS], F32R)
        work = sb("work", [P, 32 * S])
        tmp = sb("tmp", [P, 4, S])
        sq = sb("sq", [P, 2, S])
        ssum = sb("ssum", [P, S])
        rstd = sb("rstd", [P, S])
        rstd_tok = sb("rstd_tok", [P, TT])
        gains = sb("gains", [P, 160])
        b_forget = sb("b_forget", [FOX_HEADS, 1])
        eps = sb("eps", [P, 1])
        free_mark = sb("free_mark", [1, 9])
        negmax = sb("negmax", [P, 8])
        rowsum = sb("rowsum", [P, 8])
        rinv = sb("rinv", [P, 8])
        banks = [ctx.enter_context(nc.psum_tensor(f"bank{i}", [P, S], F32)) for i in range(8)]
        x_stash = nc.dram_tensor("x_stash", [P, KT * S], F32, kind="Internal").ap()

        ident = consts[:, ccols["ident"]]
        ones = consts[:, ccols["ones"]]
        rope = consts[:, ccols["rope"]]
        strict = consts[:, ccols["strict"]]
        rest = {name: work[:, 10 * S + at.start - KEPT:10 * S + at.stop - KEPT] for name, at in ccols.items()
                if at.start >= KEPT}

        G_NORM2, G_CONV = 0, 96
        G_IN, G_F, G_BGATE, G_Q, G_KV = 120, 128, 136, 152, 155
        vec_raw = work[:, 8 * S:8 * S + 2 * P].rearrange("p (a n) -> p a n", a=2)

        def wt(i):
            return work[:, bass.ds(i * S, S)]

        X = 24

        def col(c):
            return gains[:, bass.ds(c, 1)]

        const_landed = sem("const_landed")
        late_landed = sem("late_landed")
        x_landed = [sem(f"x_landed{i}") for i in range(X_CHUNKS)]
        raw_landed = [sem("raw_landed0"), sem("raw_landed1")]
        w_hi = sem("w_hi")
        w_split = sem("w_split")
        half_hi = sem("half_hi")
        half_split = sem("half_split")
        out_scaled = sem("out_scaled")
        tile_done = sem("tile_done")
        tile_read = sem("tile_read")
        const_split = sem("const_split")
        prologue_ready = sem("prologue_ready")
        stash_saved = sem("stash_saved")
        stash_back = sem("stash_back")
        sq_done = sem("sq_done")
        sq_added = sem("sq_added")
        stat_done = sem("stat_done")
        ln_done = sem("ln_done")
        rstd_ready = sem("rstd_ready")
        rstd_turned = sem("rstd_turned")
        rstd_tok_ready = sem("rstd_tok_ready")
        x_ready = sem("x_ready")
        in_hi = sem("in_hi")
        in_ready = sem("in_ready")
        silu_done = sem("silu_done")
        gate_out = sem("gate_out")
        gated = sem("gated")
        branch_gate = sem("branch_gate")
        gate_merge = sem("gate_merge")
        merged_hi = sem("merged_hi")
        merged = sem("merged")
        conv_pad = sem("conv_pad")
        dve_step = sem("dve_step")
        hid_square = sem("hid_square")
        hid_hi = sem("hid_hi")
        hid_ready = sem("hid_ready")
        pad_zero = sem("pad_zero")
        c_normed = sem("c_normed")
        c_hi = sem("c_hi")
        c_ready = sem("c_ready")
        rope_k = sem("rope_k")
        q_rotated = sem("q_rotated")
        rope_swapped = sem("rope_swapped")
        rope_spread = sem("rope_spread")
        decay_done = sem("decay_done")
        forget_log = sem("forget_log")
        p_landed = sem("p_landed")
        p_split = sem("p_split")
        p_ready = sem("p_ready")
        conv_y = sem("conv_y")
        conv_hi = sem("conv_hi")
        conv_ready = sem("conv_ready")
        gained = sem("gained")
        out_turned = sem("out_turned")
        out_taken = sem("out_taken")
        out_tile = sem("out_tile")
        out_saved = sem("out_saved")

        ATT = {}
        for kind in ("sb", "mla", "fox"):
            ATT[kind] = {n: sem(f"{kind}_{n}") for n in (
                "q_hi", "stage_hi", "staged", "scores", "turned", "clipped", "softplus", "masked", "part_hi",
                "part_ready", "summed", "w_exp", "w_masked", "negmax", "exp", "normed", "pt_hi", "pt_ready",
                "out", "gathered", "o_hi", "o_ready", "step")}

        block = ctx.enter_context(nc.Block())

        def by_k(w):
            return w.rearrange("(k p) n -> p k n", p=P)

        w_in = by_k(ins["w_in"][0])
        attn_in = by_k(ins["w_attn_in_2"][0])
        conv_in = by_k(ins["w_conv_in_2"][0])

        def slot_of(s, k, n):
            return raw[:, s, 0:k * n].rearrange("p (k n) -> p k n", k=k)

        def first_bank(tile):
            return banks[4 + tile % 4]

        MASK = {"fox": 0, "mla": 1, "sb": 2}
        STARTS_FREE = {"sb": ("summed", "out", "gathered"),
                       "mla": ("scores", "out", "gathered"),
                       "fox": ("scores", "out", "gathered")}
        HI_STEPS = {"sb": (3, 5), "mla": (3, 3), "fox": (4, 6)}

        def qk_main(a):
            return head_qk[:, a, :]

        def qk_spare(a):
            return act_b[:, a // 2, 4 + a % 2, :]

        def qk_parts(kind, hh):
            return (qk_main, qk_spare)[hh ^ (kind == "mla")]

        PE_ORDER = "z0 z1 z2 g0 t0 g1 z3 t1 g2 z4 t2 z5 g3 t3 z6 t4 v0 z7 t5 g4 g5 t6 t7 g6 g7 v1"
        ACT_ORDER = "e0 s1 e1 e2 p0 p1 e3 e4 p2 e5 p3 e6 s2 p4 e7 p5 w0 p6 p7"
        DVE_ORDER = "m0 m1 n0 s1 m2 n1 m3 p0 n2 p1 m4 n3 m5 p2 n4 p3 n5 m6 n6 m7 p4 g0 n7 p5 s2 p6 p7 x0 x1 g1"

        PE_LAST = ("z0 z1 t0 z2 t1 z3 t2 z4 z5 t3 z6 t4 v0 g0 z7 g1 t5 t6 g2 t7 v1",
                   "z0 z1 z2 t0 t1 z3 g3 z4 t2 z5 g4 t3 t4 z6 z7 t5 v0 g5 t6 g6 t7 v1")
        ACT_LAST = ("e0 e1 s1 e2 e3 p0 o0 w0 p1 o1 e4 p2 o2 e5 p3 e6 p4 s2 e7 p5 p6 p7 o3",
                    "e0 e1 s1 p0 o4 e2 e3 p1 e4 p2 p3 e5 o5 e6 p4 o6 p5 e7 p6 p7")
        DVE_LAST = ("m0 m1 n0 m2 n1 s1 n2 m3 p0 m4 p1 n3 m5 p2 n4 m6 p3 g0 n5 n6 p4 m7 n7 p5 s2 p6 p7 g1",
                    "m0 m1 n0 n1 m2 s1 m3 n2 p0 p1 m4 n3 m5 p2 n4 p3 n5 m6 n6 m7 g0 p4 n7 p5 p6 p7 g1")
        ACT_MLA_LAST = "e0 s1 e1 e2 p0 e3 p1 e4 p2 e5 p3 e6 p4 e7 p5 w0 o0 o1 p6 p7 o2"
        DVE_MLA_LAST = "m0 m1 n0 s1 m2 n1 m3 p0 n2 p1 m4 n3 m5 p2 n4 p3 n5 m6 n6 m7 p4 g0 n7 p5 o0 p6 o1 p7 x0 x1 o2 g1"
        EARLY_OUT = {"mla": 3, "fox": 7}

        def steps(order):
            return [(w[0], int(w[1:])) for w in order.split()]

        TILES = {"sb": dict(q=0, k=4, v=8, gate=12), "mla": dict(q=8, k=16, v=28, gate=24), "fox": dict(q=0, k=8, v=16)}
        Y_SB, Y_GATE0, Y_GATE1 = 0, 16, 8
        LATENTS = (28, 29, 30, 31, 8)
        BESIDE = {"sb": "gate0", "mla": "gate1", "fox": "fox_qk_next"}
        BESIDE_PASSES = {"mla": MLA_HEADS // 4, "fox": FOX_HEADS // 4 - 1}
        SCALE = {"sb": HD ** -0.5, "fox": HD ** -0.5, "mla": QK ** -0.5}

        def head_rows(kind, which, i, hh):
            if kind == "mla":
                return wt(TILES[kind][which] + 2 * i + hh)[0:QK, :]
            return wt(TILES[kind][which] + i)[hh * HD:(hh + 1) * HD, :]

        def moved(kind, hh):
            return hh == 1 and kind != "mla"

        def moved_rows(which):
            return sq[0:HD, ("q", "k").index(which), :]

        def head_values(kind, i, hh):
            width = (FOX_HEADS if kind == "fox" else SB_HEADS) * HD
            v = work[:, TILES[kind]["v"] * S:TILES[kind]["v"] * S + TT * width].rearrange("p (a n) -> p a n", a=TT)
            return v[:, :, bass.ds(2 * HD * i + hh * HD, HD)]

        decay_parts = ssum[0:48, :]

        def output_tile(kind, i):
            return wt(TILES[kind]["k"] + 2 * i if kind == "mla" else TILES[kind]["q"] + i)

        UPPER = (6, 7, 4, 5)

        def out_parts(kind, hl, k):
            return act_a[:, hl, k, :] if kind == "fox" else act_b[:, hl, UPPER[k], :]

        FIRST_ORDER = "h0 h1 u0 q0 q1 h2 h3 u1 q2 q3 h4 h5 q4 h6 q5 h7 q6 q7"
        FIRST_LO_ORDER = "e0 e1 l0 l1 w0 e2 e3 l2 l3 w1 e4 e5 l4 e6 l5 e7 l6 l7"
        FOX_ORDER = "h0 u1 h1 h2 q0 h3 q1 h4 q2 h5 q3 h6 q4 h7 q5 q6 q7"
        HI_ORDER = "h0 h1 e0 h2 h3 w0 q0 q1 h4 w1 h5 q2 q3 h6 q4 h7 q5 q6 q7"
        HALVED = {"mlp0": (0, 1), "ple_gate0": (0, 1), "conv_in": (1,), "mlp1": (0, 1), "ple_gate1": (0, 1)}
        POOL_ADDS = range(1, 4)
        NORM_ORDER = "m0 a0 m1 m2 l0 m3 l1 m4 l2 a4 l3 w0 m5 a5 l4 m6 a6 l5 m7 a7 l6 l7 w1"

        OUT_X, OUT_E, EG = 8, X, 16

        def token_major(at):
            return work[:, at * S:(at + KT) * S].rearrange("p (a n) -> p a n", a=TT)

        def valid(kt):
            return slice(kt * P, S)

        def stick_hi(act, A, h, r, offset):
            kt = TT - 1 - r
            act.wait_ge(A["w_exp" if offset else "masked"], 4 * h + r + 1)
            if r == 0 and offset == 0:
                act.wait_ge(A["out"], FREE + h)
            if r == 0 and offset:
                act.wait_ge(A["summed"], FREE + 4 * h + TT)
            nc.scalar.activation(act_b[:, 0, kt, valid(kt)], tmp[:, kt, valid(kt)], ACT.Copy).then_inc(A["part_hi"], 1)

        @block.sync
        def _(sp):
            def load(pl, dst, src, first=True):
                if first and pl.at >= 2:
                    sp.wait_ge(w_split, pl.u - 1)
                    sp.nop(nofuse=True)
                sp.dma_start(dst, src).then_inc(raw_landed[pl.slot], 16)

            def loop(name, passes, per, source, k=KT, n=256):
                with sp.Fori(0, passes) as i:
                    for j in range(per):
                        pl = Place(tab, name, j, i, per, passes)
                        load(pl, slot_of(pl.slot, k, n), source(i, j))

            x_in = ins["x"][0].rearrange("(a p) n -> p a n", p=P)
            x_raw = work[:, 0:TT * D].rearrange("p (a n) -> p a n", a=TT)

            def load_x(c):
                cols = slice(c * D // X_CHUNKS, (c + 1) * D // X_CHUNKS)
                sp.dma_start(x_raw[:, :, cols], x_in[:, :, cols]).then_inc(x_landed[c], 16)

            at = ccols["ident"]
            sp.dma_start(consts[:, at], ins["consts"][:, at]).then_inc(const_landed, 16)
            load_x(0)

            def rows(v, n):
                return v.rearrange("(k p) -> k p", p=P)[0:n, :]

            sp.dma_start(vec_raw[0:96, 0, :], ins["norm_g_2"].rearrange("l n (k p) -> (l n k) p", p=P))\
                .then_inc(const_landed, 16)
            sp.dma_start(vec_raw[96:120, 0, :], ins["conv_w_2"][0].rearrange("j (k p) -> (j k) p", p=P))\
                .then_inc(const_landed, 16)
            row = 0
            for name, n in (("norm_in_g", 8), ("norm_f_g", 8), ("b_gate", 16), ("q_norm_g", 3), ("kv_norm_g", 2)):
                v = ins[name] if name == "norm_f_g" else ins[name][0]
                sp.dma_start(vec_raw[row:row + n, 1, :], rows(v, n)).then_inc(const_landed, 16)
                row += n

            def w_in_cols(c):
                return lambda i, j: w_in[:, :, bass.ds(c + 512 * i + 256 * j, 256)]

            for j in range(2):
                load(Place(tab, "sb_qk", j), slot_of(j, KT, 256), w_in_cols(SB_Q)(0, j))
                load_x(1 + j)
            load_x(3)
            sp.dma_start(consts[:, at.stop:KEPT], ins["consts"][:, at.stop:KEPT]).then_inc(late_landed, 16)
            sp.dma_start(work[:, 10 * S:10 * S + cwidth - KEPT], ins["consts"][:, KEPT:cwidth]).then_inc(late_landed, 16)
            sp.dma_start(b_forget[:, :], ins["b_forget_2"].rearrange("a h -> h a")).then_inc(late_landed, 16)
            sp.dma_start(wf_raw[:, :].rearrange("p (k n) -> p k n", k=KT),
                         attn_in[:, :, 3 * D:3 * D + FOX_HEADS]).then_inc(late_landed, 16)
            with sp.Fori(1, 2) as i:
                for j in range(2):
                    pl = Place(tab, "sb_qk", j, i, 2, 2)
                    sp.wait_ge(w_split, pl.u - 1)
                    sp.nop(nofuse=True)
                    sp.dma_start(slot_of(pl.slot, KT, 256), w_in_cols(SB_Q)(i, j)).then_inc(raw_landed[pl.slot], 16)
            sp.wait_ge(in_ready, KT)
            sp.dma_start(x_stash, work[:, X * S:(X + KT) * S]).then_inc(stash_saved, 16)
            loop("sb_v", 1, 2, w_in_cols(SB_V))
            loop("sb_gate", 1, 2, w_in_cols(SB_GATE))
            loop("gate0", 2, 2, w_in_cols(GATES))
            for name, c in (("mla_gate", MLA_GATE), ("c_qkv", C_Q)):
                for j in range(2):
                    pl = Place(tab, name, j)
                    load(pl, slot_of(pl.slot, KT, 256), w_in[:, :, c + 256 * j:c + 256 * j + 256])
            pl = Place(tab, "c_rope", 0)
            load(pl, slot_of(pl.slot, KT, 160), w_in[:, :, C_Q + 512:MLA_GATE])
            o_sb = by_k(ins["w_o_sb"][0])
            for j in range(2):
                pl = Place(tab, "o_sb", j)
                load(pl, slot_of(pl.slot, 4, 512), o_sb[:, :, 512 * j:512 * j + 512])
            sp.wait_ge(tile_read, tab.end[tab.first["c_rope"]])
            sp.dma_start(tmp[96:112, 2, :], tmp[80:96, 2, :]).then_inc(rope_swapped, 16)
            sp.dma_start(tmp[112:128, 2, :], tmp[64:80, 2, :]).then_inc(rope_swapped, 16)
            def spread():
                sp.wait_ge(rope_k, 1)
                sp.wait_ge(tile_read, tab.end[tab.first["o_sb"] + 1])
                for h in range(MLA_HEADS):
                    at = TILES["mla"]["k"] + h
                    sp.dma_start(work[64:96, at * S:(at + 1) * S], tmp[64:96, 2, :]).then_inc(rope_spread, 16)

            q_up = ins["w_q_up"][0].rearrange("(k p) n -> p k n", p=P)
            for j in range(2):
                pl = Place(tab, "q_up", j)
                for h in range(4):
                    src = q_up[:, :, QK * (4 * j + h):QK * (4 * j + h + 1)]
                    dst = raw[:, pl.slot, 0:3 * 512].rearrange("p (k h n) -> p k h n", k=3, h=4)[:, :, h, :]
                    if h == 0:
                        load(pl, dst[:, :, 0:96], src)
                    else:
                        load(pl, dst[:, :, 0:96], src, first=False)
                    load(pl, dst[:, :, 96:112], src[:, :, 80:96], first=False)
                    load(pl, dst[:, :, 112:128], src[:, :, 64:80], first=False)
            kv_up = ins["w_kv_up"][0].rearrange("(k p) n -> p k n", p=P)
            pl = Place(tab, "kv_up", 0)
            load(pl, slot_of(pl.slot, 2, 1024), kv_up)
            spread()
            loop("gate1", 2, 2, w_in_cols(GATES + D))
            o_mla = by_k(ins["w_o_mla"][0])
            loop("o_mla", 1, 2, lambda i, j: o_mla[:, :, 512 * j:512 * j + 512], k=4, n=512)
            w_out = by_k(ins["w_out"][0])
            for j in range(4):
                if j == 2:
                    sp.wait_ge(ATT["mla"]["o_ready"], MLA_HEADS // 2)
                    sp.dma_start(work[:, X * S:(X + KT) * S], x_stash).then_inc(stash_back, 16)
                pl = Place(tab, "w_out", j)
                load(pl, slot_of(pl.slot, KT, 256), w_out[:, :, 256 * j:256 * j + 256])

            def mlp(layer):
                up = by_k(ins["w_mlp_up_2"][layer])
                down = ins["w_mlp_down_2"][layer].rearrange("(c k p) n -> p c k n", p=P, k=KT)
                chunks = D_FF // D

                def source(i, j):
                    if j < 4:
                        return up[:, :, bass.ds(D * i + 256 * j, 256)]
                    return down[:, bass.ds(i, 1), :, 256 * (j - 4):256 * (j - 3)].rearrange("p a k n -> p (a k) n")

                loop(f"mlp{layer}", chunks, 8, source)

            def embedding(layer):
                sp.dma_start(work[:, 16 * S:18 * S].rearrange("p (a n) -> p a n", a=TT),
                             ins["p_2"][layer, 0].rearrange("(a p) n -> p a n", p=P)).then_inc(p_landed, 16)

            def embed_project(name, layer, j):
                proj = ins["w_ple_proj_2"][layer].rearrange("(k p) n -> p k n", p=P)
                pl = Place(tab, name, 0)
                load(pl, slot_of(pl.slot, 2, 512), proj[:, :, 512 * j:512 * j + 512])

            def embed_gate(layer):
                gate = by_k(ins["w_ple_gate_2"][layer])
                loop(f"ple_gate{layer}", 2, 2, lambda i, j: gate[:, :, bass.ds(512 * i + 256 * j, 256)])

            def load_qk(pl, pair):
                for b in range(2):
                    load(pl, slot_of(pl.slot, KT, 256)[:, :, b * P:(b + 1) * P],
                         attn_in[:, :, bass.ds(b * D + P * pair, P)], first=b == 0)

            for j in range(2):
                load_qk(Place(tab, "fox_qk", j), j)
            loop("fox_v", 2, 2, lambda i, j: attn_in[:, :, bass.ds(2 * D + 512 * i + 256 * j, 256)])
            with sp.Fori(0, 3) as i:
                for j in range(2):
                    load_qk(Place(tab, "fox_qk_next", j, i, 2, 3), 2 + 2 * i + j)
            fox_out = by_k(ins["w_attn_out_2"][0])

            def load_out(pl, j):
                for part in range(2):
                    rows = slice(4 * part, 4 * part + 4)
                    load(pl, slot_of(pl.slot, KT, 256)[:, rows, :], fox_out[:, rows, 256 * j:256 * j + 256],
                         first=part == 0)

            for j in range(2):
                pl = Place(tab, "fox_out", j)
                load_out(pl, j)
            sp.wait_ge(ATT["fox"]["staged"], 3 * FOX_HEADS)
            embedding(0)
            for j in range(2, 4):
                pl = Place(tab, "fox_out", j)
                load_out(pl, j)
            embed_project("ple_first0", 0, 0)
            mlp(0)
            embed_project("ple_second0", 0, 1)
            embed_gate(0)

            sp.wait_ge(x_ready, 3 * KT)
            embedding(1)

            def conv_source(i, j):
                part, half = j % 3, j // 3
                return conv_in[:, :, bass.ds((D, 2 * D, 0)[part] + 512 * i + 256 * half, 256)]

            loop("conv_in", 2, 6, conv_source)
            conv_out = by_k(ins["w_conv_out_2"][0])
            loop("conv_out", 2, 2, lambda i, j: conv_out[:, :, bass.ds(512 * i + 256 * j, 256)])
            embed_project("ple_first1", 1, 0)
            mlp(1)
            embed_project("ple_second1", 1, 1)
            embed_gate(1)

            for a in range(TT):
                for half in range(2) if a == TT - 1 else (slice(None),):
                    cols = half if a < TT - 1 else slice(half * D // 2, (half + 1) * D // 2)
                    sp.wait_ge(out_tile, 2 * a + (2 if a < TT - 1 else half + 1))
                    sp.dma_start(out[0, a * P:(a + 1) * P, cols], token_major(OUT_X)[:, a, cols]).then_inc(out_saved, 16)
            sp.wait_ge(out_saved, 16 * (TT + 1))
        @block.tensor
        def _(pe):
            n = Steps()

            def weights(pl, hl, a, b):
                return wsp[:, pl.slot, hl, a:b]

            def bank(pl, m):
                return banks[(pl.bank + m) % 4]

            def empty(tile, m=0):
                if not isinstance(tile, int) or tile + m >= 4:
                    pe.wait_ge(tile_read, tile + m - 3)

            def three(dst, w, a, first, last, done=None):
                nc.tensor.matmul(dst, w[0], a[0], start=first, stop=False)
                nc.tensor.matmul(dst, w[0], a[1], start=False, stop=False)
                mm = nc.tensor.matmul(dst, w[1], a[0], start=False, stop=last)
                if done is not None:
                    mm.then_inc(done, 1)

            def unit(pl, k_tiles, width, m_tiles, x, ready=None, by_tile=False, start=0, whole=None, first_m=0, late=None):
                pe.wait_ge(w_split, pl.u + 1)
                end = whole or k_tiles
                order = [(k, m) for k in range(start, k_tiles) for m in range(first_m, m_tiles)]
                if by_tile:
                    order.sort(key=lambda km: km[1])
                for k, m in order:
                    if late and (k, m) == order[-2]:
                        late()
                    if ready and m == 0:
                        pe.wait_ge(ready[0], ready[1] + k + 1)
                    if k == 0:
                        empty(pl.tile, m)
                    c = k * width + m * P
                    three(bank(pl, m)[:, :], [weights(pl, hl, c, c + P) for hl in (0, 1)],
                          [x(hl, k) for hl in (0, 1)], k == 0, k == end - 1, tile_done if k == end - 1 else None)

            def first_units(name, ready, j=0, between=None):
                a, b = (Place(tab, name, j + u) for u in (0, 1))
                halved = HALVED.get(name, ())
                halves = n.add("halves", len(halved))
                for part, (pl, half) in enumerate(((a, 0), (b, 0), (a, 1), (b, 1))):
                    if between:
                        between(part)
                    if part in halved:
                        pe.wait_ge(half_split, halves - len(halved) + (1 if pl is b else 2))
                    elif not half or part - 2 in halved:
                        pe.wait_ge(w_split, pl.u + 1)
                    if not half and not between:
                        for m in range(2):
                            empty(pl.tile, m)
                    for k in range(half * KT // 2, (half + 1) * KT // 2):
                        if part == 3 and k == KT // 2 + 1:
                            statistics(KT)
                        if pl is a:
                            pe.wait_ge(in_ready, ready + k + 1)
                        for m in range(2):
                            c = k * 256 + m * P
                            three(bank(pl, m)[:, :], [weights(pl, hl, c, c + P) for hl in (0, 1)],
                                  [from_a(hl, k) for hl in (0, 1)], k == 0, k == KT - 1,
                                  tile_done if k == KT - 1 else None)

            def beside(pl, share, read=None, ready=None):
                if share == 0:
                    pe.wait_ge(w_split, pl.u + 1)
                    pe.wait_ge(tile_read, pl.tile if read is None else read)
                if ready:
                    pe.wait_ge(ready, share + 1)
                for m in range(2):
                    c = share * 256 + m * P
                    three(banks[6 + m][:, :], [weights(pl, hl, c, c + P) for hl in (0, 1)],
                          [from_a(hl, share) for hl in (0, 1)], share == 0, share == KT - 1,
                          tile_done if share == KT - 1 else None)

            def unit_tokens(pl, k_tiles, x, cols, rhs):
                pe.wait_ge(w_split, pl.u + 1)
                for a in range(TT):
                    empty(pl.tile, a)
                    for k in range(k_tiles):
                        three(bank(pl, a)[:, 0:cols], [x(hl, k)[:, a * P:(a + 1) * P] for hl in (0, 1)],
                              [rhs(hl, k) for hl in (0, 1)], k == 0, k == k_tiles - 1,
                              tile_done if k == k_tiles - 1 else None)

            def from_a(hl, k):
                return act_a[:, hl, k, :]

            def from_b(hl, k):
                return act_b[:, hl, k, :]

            def upper_b(hl, k):
                return act_b[:, hl, UPPER[k], :]

            def project(name, passes, x, ready=None, first=0):
                with pe.Fori(first, passes) as i:
                    for j in range(2):
                        unit(Place(tab, name, j, i, 2, passes), KT, 256, 2, x, ready if j == 0 else None, by_tile=j == 1)

            def project_normed(name, x, ready=None, first=0):
                for j in range(first, 4):
                    unit(Place(tab, name, j), KT, 256, 2, x, ready if j == 0 else None, by_tile=j == 3,
                         late=begin_statistics if j == 3 else None)

            def statistics(tiles):
                sum_over_features(tiles, tiles).then_inc(stat_done, 1)
                n.add("stat")

            def begin_statistics():
                sum_over_features(KT, KT - 1)

            def end_statistics():
                pe.wait_ge(sq_done, n["squares"])
                nc.tensor.matmul(banks[7][:, :], ones, sq[:, (n["squares"] - 1) % 2, :], start=False, stop=True)\
                    .then_inc(stat_done, 1)
                n.add("stat")

            def sum_over_features(tiles, summed):
                pe.wait_ge(sq_added, n.add("sq", summed))
                if n["stat"]:
                    pe.wait_ge(rstd_ready, n["stat"])
                if n["turned"]:
                    pe.wait_ge(rstd_tok_ready, n["turned"])
                n.add("squares", tiles)
                return nc.tensor.matmul(banks[7][:, :], ones, ssum[:, :], start=True, stop=summed == tiles)

            def turn_rstd():
                pe.wait_ge(rstd_ready, n["stat"])
                for a in range(TT):
                    mm = nc.tensor.matmul(banks[7][:, a:a + 1], rstd[0:1, a * P:(a + 1) * P], ones[0:1, 0:1],
                                          start=a == 0, stop=a == TT - 1)
                mm.then_inc(rstd_turned, 1)
                n.add("turned")

            tile = tab.extra["sb_qk"]
            pe.wait_ge(const_landed, 16 * CONST_LOADS)
            for r, rows in ((0, 120), (1, 37)):
                nc.tensor.transpose(first_bank(tile)[:, 0:rows], vec_raw[0:rows, r, :], ident[0:rows, 0:rows])\
                    .then_inc(tile_done, 1)
                tile += 1

            def turn_x(tiles):
                for k in tiles:
                    pe.wait_ge(x_landed[k * X_CHUNKS // KT], 16)
                    empty(tile + k)
                    for a in range(TT):
                        tr = nc.tensor.transpose(first_bank(tile + k)[:, a * P:(a + 1) * P],
                                                 work[:, a * D + k * P:a * D + (k + 1) * P], ident)
                    tr.then_inc(tile_done, 1)

            def turn_between(part):
                turn_x((range(0, 4), range(4, KT), (), ())[part])
                if part == 3:
                    pe.wait_ge(late_landed, 16 * LATE_LOADS)

            first_units("sb_qk", 0, between=turn_between)
            project("sb_qk", 2, from_a, first=1)
            turn_rstd()
            for j in range(2):
                pl = Place(tab, "sb_v", j)
                unit_tokens(pl, KT, from_a, 256, lambda hl, k: weights(pl, hl, k * 256, (k + 1) * 256))
            for j in range(2):
                unit(Place(tab, "sb_gate", j), KT, 256, 2, from_a)

            A = ATT["sb"]
            pe.wait_ge(tile_read, tab.end[tab.first["sb_gate"] + 1])
            pe.wait_ge(pad_zero, 1)
            pe.wait_ge(const_split, CONST_SPLITS)
            with pe.Fori(0, SB_HEADS // 2) as i:
                for hh in range(2):
                    h = 2 * i + hh
                    pl = Place(tab, BESIDE["sb"], hh, i, 2, SB_HEADS // 2)
                    pe.wait_ge(A["staged"], 3 * h + 3)

                    qk = qk_parts("sb", hh)

                    def scores(kt, last, done=None):
                        c = min(kt * P, S - 2 * P)
                        three(banks[kt][:, c:S], [qk(2 + hl)[0:HD, kt * P:(kt + 1) * P] for hl in (0, 1)],
                              [qk(hl)[0:HD, c:S] for hl in (0, 1)], True, last, done)

                    for kt in reversed(range(TT)):
                        scores(kt, True, A["scores"])
                    beside(pl, 0)
                    beside(pl, 1)
                    for kt in reversed(range(TT)):
                        pe.wait_ge(A["part_ready"], 8 * h + TT - kt)
                        scores(kt, False)
                        for later in range(kt, TT):
                            c = min(later * P, S - 2 * P)
                            m = trir if later == kt else negonesr
                            for hl in (0, 1):
                                nc.tensor.matmul(banks[kt][:, c:S], m[:, :], act_b[:, hl, later, c:S],
                                                 start=False, stop=False)
                        c = min(kt * P, S - 2 * P)
                        m = maskr[:, MASK["sb"], 0:2 * P] if kt == TT - 1 else maskr[:, MASK["sb"], P:3 * P]
                        nc.tensor.matmul(banks[kt][:, c:c + 2 * P], identr[:, :], m, start=False, stop=True)\
                            .then_inc(A["summed"], 1)
                        if kt:
                            beside(pl, 1 + TT - kt)
                    for share in range(5, KT):
                        beside(pl, share)
                    pe.wait_ge(A["part_ready"], 8 * h + 8)
                    pe.wait_ge(A["gathered"], FREE + 2 * i)
                    for kt in range(TT):
                        c = min(kt * P, S - 2 * P)
                        three(banks[4 + hh][0:HD, c:S], [head_v[:, hh, hl, kt, :] for hl in (0, 1)],
                              [act_b[:, hl, kt, c:S] for hl in (0, 1)], kt == 0, kt == TT - 1,
                              A["out"] if kt == TT - 1 else None)

            pl = Place(tab, "c_rope", 0)
            pe.wait_ge(w_split, pl.u + 1)
            for m, rows in ((0, P), (1, ROPE)):
                empty(pl.tile, m)
                for k in range(KT):
                    c = k * 160 + m * P
                    three(bank(pl, m)[0:rows, :], [weights(pl, hl, c, c + rows) for hl in (0, 1)],
                          [from_a(hl, k) for hl in (0, 1)], k == 0, k == KT - 1, tile_done if k == KT - 1 else None)
            pe.wait_ge(A["o_ready"], SB_HEADS // 2)
            statistics(3)
            unit(Place(tab, "o_sb", 0), 4, 512, 4, upper_b, by_tile=True)
            statistics(2)
            unit(Place(tab, "o_sb", 1), 4, 512, 4, upper_b, by_tile=True)
            for j in range(2):
                unit(Place(tab, "q_up", j), 3, 512, 4, from_b, (c_ready, 0) if j == 0 else None, by_tile=True)
            pl = Place(tab, "kv_up", 0)
            pe.wait_ge(w_split, pl.u + 1)
            pe.wait_ge(c_ready, 5)

            def kv_latents(hl, k):
                return head_qk[:, 2 * hl + k, :]

            def v_cols(hl, k):
                return weights(pl, hl, k * 1024, (k + 1) * 1024).rearrange("p (h c) -> p h c", h=8)[:, :, HD:P]

            unit_tokens(pl, 2, kv_latents, S, v_cols)
            for h in range(MLA_HEADS):
                empty(pl.tile, TT + h)
                for k in range(2):
                    c = k * 1024 + h * P
                    three(bank(pl, TT + h)[0:HD, :], [weights(pl, hl, c, c + HD) for hl in (0, 1)],
                          [kv_latents(hl, k) for hl in (0, 1)], k == 0, k == 1, tile_done if k == 1 else None)

            def softmax_attention(kind, heads, width):
                A = ATT[kind]
                mask = maskr[:, MASK[kind], :]

                def scores(i, s):
                    hh, j = divmod(s, TT)
                    qk = qk_parts(kind, hh)
                    if j == 0:
                        pe.wait_ge(A["staged"], 3 * (2 * i + hh) + 3)
                    cols = max((j + 1) * P, 2 * P)
                    dst = banks[s % 3][:, 0:cols]
                    for pass_, (a, b) in enumerate(((0, 2), (0, 3), (1, 2))):
                        nc.tensor.matmul(dst, qk(a)[0:width, j * P:(j + 1) * P], qk(b)[0:width, 0:cols],
                                         start=pass_ == 0, stop=False)
                    if kind == "fox":
                        nc.tensor.matmul(dst, onesr[:, :], decay_row[:, hh, 0:cols], start=False, stop=False)
                    c = max(j - 1, 0) * P
                    m = mask[:, P:3 * P] if j == 0 else mask[:, 0:2 * P]
                    nc.tensor.matmul(banks[s % 3][:, c:c + 2 * P], identr[:, :], m, start=False, stop=True)\
                        .then_inc(A["scores"], 1)

                def turn(i, s):
                    pe.wait_ge(A["normed"], 8 * i + s + 1)
                    if s >= 2:
                        pe.wait_ge(A["pt_ready"], 8 * i + s - 1)
                    for b in range(s % TT + 1):
                        tr = nc.tensor.transpose(banks[3 + s % 2][:, b * P:(b + 1) * P],
                                                 tmp[:, s % 4, b * P:(b + 1) * P], ident)
                    tr.then_inc(A["turned"], 1)

                def values(i, hh):
                    pe.wait_ge(A["pt_ready"], 8 * i + 4 * hh + 4)
                    pe.wait_ge(A["gathered"], FREE + 2 * i + hh)
                    for kt in range(TT):
                        c = min(kt * P, S - 2 * P)
                        three(banks[5][0:HD, c:S], [head_v[:, hh, hl, kt, :] for hl in (0, 1)],
                              [act_b[:, hl, kt, c:S] for hl in (0, 1)], kt == 0, kt == TT - 1,
                              A["out"] if kt == TT - 1 else None)

                def two_pairs(i, orders=(PE_ORDER, PE_ORDER)):
                    for a in range(2):
                        for what, s in steps(orders[a]):
                            if what != "g":
                                {"z": scores, "t": turn, "v": values}[what](2 * i + a, s)
                            elif orders is PE_LAST:
                                beside(Place(tab, "fox_out", 0), s, tab.extra["fox_out"], A["o_ready"])
                            else:
                                beside(Place(tab, BESIDE[kind], a, i, 2, passes), s)

                passes = BESIDE_PASSES[kind]
                with pe.Fori(0, heads // 4 - 1) as i:
                    two_pairs(i)
                two_pairs(heads // 4 - 1, *([PE_LAST] if kind == "fox" else []))

            pe.wait_ge(tile_read, tab.end[tab.first["kv_up"]])
            pe.wait_ge(pad_zero, 2)
            softmax_attention("mla", MLA_HEADS, QK)
            for j in range(2):
                unit(Place(tab, "o_mla", j), 4, 512, 4, upper_b, (ATT["mla"]["o_ready"], 0) if j == 0 else None, by_tile=j == 1)
            project_normed("w_out", from_a, (merged, 0))
            end_statistics()

            n.add("in", KT)
            first_units("fox_qk", n["in"])
            n.add("in", KT)
            tile = tab.extra["fox_v"]
            empty(tile)
            for k in range(KT):
                three(banks[tile % 4][0:FOX_HEADS, :], [wf[:, hl, k, :] for hl in (0, 1)],
                      [from_a(hl, k) for hl in (0, 1)], k == 0, k == KT - 1, tile_done if k == KT - 1 else None)
            turn_rstd()
            for j in range(4):
                pl = Place(tab, "fox_v", j)
                unit_tokens(pl, KT, from_a, 256, lambda hl, k: weights(pl, hl, k * 256, (k + 1) * 256))
            pe.wait_ge(tile_read, tab.end[tab.first["fox_v"] + 3])
            pe.wait_ge(pad_zero, 3)
            softmax_attention("fox", FOX_HEADS, HD)
            def mixer_out(name, layer, x, ready):
                tile = tab.extra[name]
                pe.wait_ge(p_landed, 16 * (layer + 1))
                for k in range(2):
                    empty(tile)
                    for a in range(TT):
                        c = 16 * S + a * 256 + k * P
                        tr = nc.tensor.transpose(banks[tile % 4][:, a * P:(a + 1) * P], work[:, c:c + P], ident)
                    tr.then_inc(tile_done, 1)
                    tile += 1
                if layer == 0:
                    for share in range(EARLY_OUT["fox"], KT):
                        beside(Place(tab, name, 0), share, ready=ready[0])
                    project_normed(name, x, first=1)
                else:
                    project_normed(name, x, ready)
                embed_project(f"ple_first{layer}", layer)

            def embed_project(name, layer):
                pl = Place(tab, name, 0)
                pe.wait_ge(w_split, pl.u + 1)
                pe.wait_ge(p_ready, 2 * layer + 2)
                for m in range(4):
                    if m == 1:
                        end_statistics()
                    empty(pl.tile, m)
                    for k in range(2):
                        c = pl.split_cols.start + k * 512 + m * P
                        three(bank(pl, m)[:, :], [weights(pl, hl, c, c + P) for hl in (0, 1)],
                              [head_qk[:, 2 * hl + k, :] for hl in (0, 1)], k == 0, k == 1, tile_done if k == 1 else None)

            def mlp(layer):
                chunks = D_FF // D
                name = f"mlp{layer}"
                base = n.add("in", KT) - KT
                hid = n.add("hid", KT * chunks) - KT * chunks

                def chunk(i, first=False, last=False):
                    if first:
                        first_units(name, base)
                    for j in range(2 if first else 0, 8):
                        pl = Place(tab, name, j, i, 8, chunks)
                        if j < 4:
                            unit(pl, KT, 256, 2, from_a)
                        else:
                            unit(pl, KT, 256, 2, from_b, (hid_ready, hid + KT * i) if j == 4 else None,
                                 by_tile=last and j == 7, late=begin_statistics if last and j == 7 else None)

                chunk(0, first=True)
                with pe.Fori(1, chunks - 1) as i:
                    chunk(i)
                chunk(chunks - 1, last=True)

            def embed_gate(layer):
                embed_project(f"ple_second{layer}", layer)
                first_units(f"ple_gate{layer}", n.add("in", KT) - KT)
                if layer == 0:
                    project(f"ple_gate{layer}", 2, from_a, first=1)
                    begin_statistics()
                    end_statistics()
                    return
                x_tiles = iter(range(KT))
                addends = iter(range(KT))

                def turn_x(tiles):
                    for _ in range(tiles):
                        turn_out(X + next(x_tiles))

                def turn_addend(tiles):
                    for _ in range(tiles):
                        k = next(addends)
                        pe.wait_ge(gained, k + 1)
                        turn_out(EG + k)

                pl = Place(tab, "ple_gate1", 2)
                turn_x(3)
                unit(pl, KT // 2, 256, 2, from_a, whole=KT)
                turn_x(3)
                unit(pl, KT, 256, 2, from_a, start=KT // 2)
                turn_x(2)
                turn_addend(1)
                pl = Place(tab, "ple_gate1", 3)
                unit(pl, KT, 256, 1, from_a)
                turn_addend(3)
                unit(pl, KT // 2, 256, 2, from_a, whole=KT, first_m=1)
                turn_addend(2)
                unit(pl, KT, 256, 2, from_a, start=KT // 2, first_m=1)
                turn_addend(1)
                token_statistics(lambda: turn_addend(1))

            def turn_out(at):
                t = n.add("turned_out") - 1
                if t >= 3:
                    pe.wait_ge(out_taken, t - 2)
                for a in range(TT):
                    tr = nc.tensor.transpose(banks[4 + t % 3][:, a * P:(a + 1) * P], wt(at)[:, a * P:(a + 1) * P], ident)
                tr.then_inc(out_turned, 1)

            def token_statistics(before_last):
                pe.wait_ge(sq_added, n.add("sq", KT - 2))
                pe.wait_ge(rstd_ready, n["stat"])
                done = n.add("squares", KT)
                for part, squares in enumerate((ssum[:, :], sq[:, done % 2, :], sq[:, (done - 1) % 2, :])):
                    if part == 2:
                        before_last()
                    if part:
                        pe.wait_ge(sq_done, done - 2 + part)
                    for a in range(TT):
                        mm = nc.tensor.matmul(banks[7][:, a:a + 1], squares[:, a * P:(a + 1) * P], ones[:, 0:1],
                                              start=part == 0 and a == 0, stop=part == 2 and a == TT - 1)
                mm.then_inc(stat_done, 1)

            mixer_out("fox_out", 0, from_a, (ATT["fox"]["o_ready"], 0))
            mlp(0)
            embed_gate(0)

            first_units("conv_in", n.add("in", KT) - KT)
            for j in range(2, 12):
                unit(Place(tab, "conv_in", j), KT, 256, 2, from_a)
            mixer_out("conv_out", 1, from_b, (conv_ready, 0))
            mlp(1)
            embed_gate(1)

        @block.scalar
        def _(act):
            n = Steps()

            def table(name):
                nc.scalar.preload_act_table_set(name)

            def split(pl):
                if not pl.exists:
                    return
                act.wait_ge(raw_landed[pl.slot], pl.landed)
                if pl.freed is not None:
                    act.wait_ge(tile_done, pl.freed)
                nc.scalar.activation(wsp[:, pl.slot, 0, pl.split_cols], raw[:, pl.slot, pl.raw_cols], ACT.Copy)\
                    .then_inc(w_hi, 1)

            def split_half(name, j, half):
                pl = Place(tab, name, j)
                cols = slice(half * UNIT // 2, (half + 1) * UNIT // 2)
                act.wait_ge(raw_landed[pl.slot], pl.landed)
                act.wait_ge(tile_done, pl.freed if half else pl.half_freed)
                nc.scalar.activation(wsp[:, pl.slot, 0, cols], raw[:, pl.slot, cols], ACT.Copy)\
                    .then_inc(w_hi if half else half_hi, 1)

            def ahead(name, j, i=0, per=0, passes=1):
                split(Place(tab, name, j, i, per, passes, ahead=1))

            def square(src, k, parity):
                if not isinstance(k, int) or k >= 2:
                    act.wait_ge(sq_added, n["added"] + k - 1)
                nc.scalar.activation(sq[:, parity, :], src, ACT.Square).then_inc(sq_done, 1)

            def squared(tiles, last=False):
                n.add("added", tiles - last)
                n.add("squares", tiles)

            def norm_input(gain, order, following=None, meanwhile=None):
                base, x0 = n["in"], n["x"]
                for what, k in steps(order):
                    if what == "h":
                        if order is FIRST_ORDER:
                            act.wait_ge(tile_read, 2 + k + 1)
                        else:
                            act.wait_ge(x_ready, x0 + k + 1)
                        nc.scalar.activation(act_a[:, 0, k, :], wt(X + k), ACT.Copy, scale=col(gain + k))\
                            .then_inc(in_hi, 1)
                    elif what == "q":
                        square(wt(X + k), k, (n["squares"] + k) % 2)
                    elif what == "u":
                        split(Place(tab, following, k))
                    elif what == "w":
                        if k in HALVED[following]:
                            split_half(following, k, 1)
                    elif meanwhile:
                        meanwhile()
                n.add("in", KT)
                squared(KT)
                if order is not FIRST_ORDER:
                    n.add("x", KT)

            def make_rstd(dst, width):
                act.wait_ge(stat_done, n.add("stat"))
                nc.scalar.activation(dst, banks[7][:, :], ACT.Ln, bias=eps[:, :], scale=1.0 / width).then_inc(ln_done, 1)
                act.wait_ge(ln_done, n["stat"])
                nc.scalar.activation(dst, dst, ACT.Exp, scale=-0.5).then_inc(rstd_ready, 1)

            def squares_of(name, tiles_at, following=None, split_before=0):
                for j in range(4):
                    if j >= split_before:
                        ahead(name, j)
                    pl = Place(tab, name, j)
                    for m in range(2):
                        if j == 3 and m == 1 and following:
                            split_half(following, 1, 0)
                        act.wait_ge(tile_read, pl.tile + m + 1)
                        k = 2 * j + m
                        square(wt(tiles_at + k), k, (n["squares"] + k) % 2)
                squared(KT, last=True)

            table("natural_log_exp_and_others")
            act.wait_ge(prologue_ready, 1)
            act.wait_ge(tile_read, 2)
            norm_input(G_IN, FIRST_ORDER, following="sb_qk")
            ahead("sb_qk", 1)
            make_rstd(rstd[:, :], D)
            for j in range(2, 4):
                ahead("sb_qk", j)
            for j in range(2):
                ahead("sb_v", j)
            def stage(kind, i, hh, first=False):
                A = ATT[kind]
                qk = qk_parts(kind, hh)
                rows = QK if kind == "mla" else HD
                if not first:
                    act.wait_ge(A["summed" if kind == "sb" else "scores"], FREE + TT * (2 * i + hh - 1))
                q, k = (head_rows(kind, which, i, hh) for which in "qk")
                scale = SCALE[kind]
                if moved(kind, hh):
                    at = sum(HI_STEPS[kind]) * i + HI_STEPS[kind][0]
                    act.wait_ge(A["staged"], 3 * (2 * i + 1))
                    nc.scalar.activation(moved_rows("q"), q, ACT.Copy, scale=scale).then_inc(A["stage_hi"], 1)
                    nc.scalar.activation(moved_rows("k"), k, ACT.Copy).then_inc(A["stage_hi"], 1)
                    act.wait_ge(A["stage_hi"], at + 2)
                    q, k, scale = moved_rows("q"), moved_rows("k"), 1.0
                nc.scalar.activation(qk(0)[0:rows, :], q, ACT.Copy, scale=scale).then_inc(A["stage_hi"], 1)
                nc.scalar.activation(qk(2)[0:rows, :], k, ACT.Copy).then_inc(A["stage_hi"], 1)
                if not first:
                    act.wait_ge(A["out"], FREE + 2 * i + hh - 1)
                if kind == "fox":
                    pick = consts[0:48, bass.ds(ccols["sel"].start + 2 * i + hh, 1)]
                    nc.scalar.activation(decay_row[:, hh, :], decay_parts, ACT.Copy, scale=pick).then_inc(A["stage_hi"], 1)
                nc.scalar.activation(head_v[:, hh, 0, :, :], head_values(kind, i, hh), ACT.Copy).then_inc(A["stage_hi"], 1)

            table("sigmoid_and_others")
            for j in range(2):
                ahead("sb_gate", j)
                if j == 0:
                    act.wait_ge(tile_read, tab.end[tab.first["sb_v"] + 1])
                    stage("sb", 0, 0, first=True)
                pl = Place(tab, "sb_gate", j)
                for m in range(2):
                    act.wait_ge(tile_read, pl.tile + m + 1)
                    if j:
                        act.wait_ge(silu_done, m + 1)
                    nc.scalar.activation(tmp[:, m, :], wt(TILES["sb"]["gate"] + 2 * j + m), ACT.Sigmoid).then_inc(gate_out, 1)
            table("natural_log_exp_and_others")

            A = ATT["sb"]

            def stick_pair(i, last=False):
                for hh in range(2):
                    h = 2 * i + hh
                    for r, kt in enumerate(reversed(range(TT))):
                        t = tmp[:, kt, valid(kt)]
                        act.wait_ge(A["clipped"], 4 * h + r + 1)
                        nc.scalar.activation(t, t, ACT.Exp).then_inc(A["exp"], 1)
                        act.wait_ge(A["exp"], 4 * h + r + 1)
                        nc.scalar.activation(t, t, ACT.Ln, bias=1.0).then_inc(A["softplus"], 1)
                        if r:
                            stick_hi(act, A, h, r - 1, 0)
                    stick_hi(act, A, h, TT - 1, 0)
                    if hh == 0:
                        stage("sb", i, 1)
                    elif not last:
                        stage("sb", i + 1, 0)
                    ahead(BESIDE["sb"], hh, i, 2, SB_HEADS // 2)
                    for r, kt in enumerate(reversed(range(TT))):
                        act.wait_ge(A["summed"], FREE + 4 * h + r + 1)
                        nc.scalar.activation(tmp[:, kt, valid(kt)], banks[kt][:, valid(kt)], ACT.Exp).then_inc(A["w_exp"], 1)
                        if r:
                            stick_hi(act, A, h, r - 1, TT)
                    stick_hi(act, A, h, TT - 1, TT)

            with act.Fori(0, SB_HEADS // 2 - 1) as i:
                stick_pair(i)
            stick_pair(SB_HEADS // 2 - 1, last=True)

            def output_hi(kind, k):
                act.wait_ge(ATT[kind]["gathered"], FREE + 2 * k + 2)
                nc.scalar.activation(out_parts(kind, 0, k), output_tile(kind, k), ACT.Copy).then_inc(ATT[kind]["o_hi"], 1)

            for k in range(SB_HEADS // 2):
                output_hi("sb", k)

            latents = tab.tile[tab.first["c_qkv"]]
            ahead("c_rope", 0)
            for k in range(5):
                act.wait_ge(tile_read, latents + k + 1)
                square(wt(LATENTS[k]), k, (n["squares"] + k) % 2)
            squared(5)
            make_rstd(wt(9), Q_LORA)
            ahead("o_sb", 0)

            def latent_hi(k):
                act.wait_ge(c_normed, k + 1)
                dst = act_b[:, 0, k, :] if k < 3 else head_qk[:, k - 3, :]
                nc.scalar.activation(dst, wt(LATENTS[k]), ACT.Copy).then_inc(c_hi, 1)

            table("sigmoid_and_others")
            for k in range(4):
                nc.scalar.activation(wt(Y_GATE0 + k), wt(Y_GATE0 + k), ACT.Sigmoid, bias=col(G_BGATE + k))\
                    .then_inc(branch_gate, 1)
            for k in range(3):
                latent_hi(k)
            for k in range(4, KT):
                nc.scalar.activation(wt(Y_GATE0 + k), wt(Y_GATE0 + k), ACT.Sigmoid, bias=col(G_BGATE + k))\
                    .then_inc(branch_gate, 1)
            for m in range(4):
                nc.scalar.activation(wt(11 + m), wt(TILES["mla"]["gate"] + m), ACT.Sigmoid).then_inc(gate_out, 1)
            table("natural_log_exp_and_others")
            make_rstd(wt(10), KV_LORA)
            ahead("o_sb", 1)
            for k in range(3, 5):
                latent_hi(k)
            for j in range(2):
                ahead("q_up", j)
            ahead("kv_up", 0)
            pl = Place(tab, "kv_up", 0)
            act.wait_ge(tile_read, pl.tile)
            for m in range(TT + MLA_HEADS):
                act.wait_ge(tile_done, pl.tile + m + 1)
                bank = banks[(pl.bank + m) % 4]
                if m < TT:
                    dst, src = wt(TILES["mla"]["v"] + m), bank[:, :]
                else:
                    dst, src = wt(TILES["mla"]["k"] + m - TT)[0:HD, :], bank[0:HD, :]
                nc.scalar.activation(dst, src, ACT.Copy).then_inc(tile_read, 1)
                if m == TT + 1:
                    act.wait_ge(tile_read, pl.tile + TT + 1)
                    act.wait_ge(rope_spread, 16 * MLA_HEADS)
                    stage("mla", 0, 0, first=True)

            def softmax_attention(kind, heads):
                A = ATT[kind]

                def exponentials(i, s):
                    j = s % TT
                    act.wait_ge(A["negmax"], 8 * i + s + 1)
                    nc.scalar.activation(tmp[:, s % 4, 0:(j + 1) * P], banks[s % 3][:, 0:(j + 1) * P], ACT.Exp,
                                         bias=negmax[:, s:s + 1], accum_out=rowsum[:, s:s + 1]).then_inc(A["exp"], 1)

                def turned_hi(i, s):
                    hh, j = divmod(s, TT)
                    act.wait_ge(A["turned"], 8 * i + s + 1)
                    if j == 0:
                        act.wait_ge(A["out"], FREE + 2 * i + hh)
                    src = banks[3 + s % 2][:, 0:(j + 1) * P].rearrange("p (b n) -> p b n", b=j + 1)
                    nc.scalar.activation(act_b[:, 0, 0:j + 1, j * P:(j + 1) * P], src, ACT.Copy).then_inc(A["pt_hi"], 1)

                def two_pairs(i, orders=(ACT_ORDER, ACT_ORDER), last=False):
                    for a in range(2):
                        pair = 2 * i + a
                        for what, s in steps(orders[a]):
                            if what == "s":
                                if not (last and a == 1 and s == 2):
                                    stage(kind, pair + s // 2, s % 2)
                            elif what == "w" and orders is ACT_LAST:
                                ahead("fox_out", 0)
                            elif what == "w":
                                ahead(BESIDE[kind], a, i, 2, passes)
                            elif what == "o":
                                output_hi(kind, s)
                            else:
                                {"e": exponentials, "p": turned_hi}[what](pair, s)

                passes = BESIDE_PASSES[kind]
                with act.Fori(0, heads // 4 - 1) as i:
                    two_pairs(i)
                two_pairs(heads // 4 - 1, ACT_LAST if kind == "fox" else (ACT_ORDER, ACT_MLA_LAST), last=True)
                for k in range(EARLY_OUT[kind], heads // 2):
                    output_hi(kind, k)

            act.wait_ge(tile_read, tab.end[tab.first["kv_up"]])
            softmax_attention("mla", MLA_HEADS)
            ahead("o_mla", 0)
            table("sigmoid_and_others")
            for k in range(KT):
                nc.scalar.activation(wt(Y_GATE1 + k), wt(Y_GATE1 + k), ACT.Sigmoid, bias=col(G_BGATE + KT + k))\
                    .then_inc(branch_gate, 1)
            for k in range(KT):
                if k == 4:
                    ahead("o_mla", 1)
                act.wait_ge(gate_merge, k + 1)
                nc.scalar.activation(act_a[:, 0, k, :], wt(Y_SB + k), ACT.Copy).then_inc(merged_hi, 1)
            table("natural_log_exp_and_others")
            squares_of("w_out", X)
            make_rstd(rstd[:, :], D)

            norm_input(G_NORM2, FOX_ORDER, following="fox_qk")
            ahead("fox_qk", 1)
            make_rstd(rstd[:, :], D)
            act.wait_ge(decay_done, 1)
            f = tmp[0:FOX_HEADS, 1, :]
            nc.scalar.activation(f, f, ACT.Exp).then_inc(forget_log, 1)
            act.wait_ge(forget_log, 1)
            nc.scalar.activation(f, f, ACT.Ln, bias=1.0).then_inc(forget_log, 1)
            act.wait_ge(decay_done, 2)
            nc.scalar.activation(decay_row[0:FOX_HEADS, 0, :], tmp[0:FOX_HEADS, 2, :], ACT.Copy).then_inc(forget_log, 1)
            for j in range(4):
                ahead("fox_v", j)
                if j == 2:
                    act.wait_ge(tile_read, tab.end[tab.first["fox_v"]])
                    stage("fox", 0, 0, first=True)
            act.wait_ge(tile_read, tab.end[tab.first["fox_v"] + 3])
            softmax_attention("fox", FOX_HEADS)

            def embed_out(name, j, m0):
                pl = Place(tab, name, 0)
                for m in (m0, m0 + 1):
                    act.wait_ge(tile_done, pl.tile + m + 1)
                    nc.scalar.activation(wt(4 * j + m), banks[(pl.bank + m) % 4][:, :], ACT.Copy).then_inc(tile_read, 1)

            def mixer_end(name, layer):
                for k in range(2):
                    act.wait_ge(tile_read, tab.extra[name] + k + 1)
                    nc.scalar.activation(head_qk[:, k, :], tmp[:, k, :], ACT.Copy).then_inc(p_split, 1)
                squares_of(name, 8, following=f"mlp{layer}", split_before=1 if layer == 0 else 0)
                split_half(f"mlp{layer}", 0, 0)
                make_rstd(rstd[:, :], D)
                embed_out(f"ple_first{layer}", 0, 0)
                norm_input(G_NORM2 + 48 * layer + 16, HI_ORDER, following=f"mlp{layer}",
                           meanwhile=lambda: embed_out(f"ple_first{layer}", 0, 2))

            def mlp(layer):
                chunks = D_FF // D
                name = f"mlp{layer}"

                def chunk(i, first=False, last=False):
                    for j in range(8):
                        if first and j == 0:
                            ahead(name, 1)
                            make_rstd(rstd[:, :], D)
                        elif not (first and j == 1):
                            ahead(name, j, i, 8, chunks)
                        for m in range(2):
                            if j < 4:
                                pl = Place(tab, name, j, i, 8, chunks)
                                act.wait_ge(tile_read, pl.tile + m + 1)
                                nc.scalar.activation(act_b[:, 0, 2 * j + m, :], tmp[:, m, :], ACT.Square)\
                                    .then_inc(hid_hi, 1)
                            elif last:
                                pl = Place(tab, name, j, i, 8, chunks)
                                if j == 7 and m == 1:
                                    split_half(f"ple_gate{layer}", 1, 0)
                                act.wait_ge(tile_read, pl.tile + m + 1)
                                k = 2 * (j - 4) + m
                                square(wt(16 + k), k, (n["squares"] + k) % 2)

                chunk(0, first=True)
                with act.Fori(1, chunks - 1) as i:
                    chunk(i)
                chunk(chunks - 1, last=True)
                squared(KT, last=True)
                split_half(f"ple_gate{layer}", 0, 0)
                make_rstd(rstd[:, :], D)
                embed_out(f"ple_second{layer}", 1, 0)
                norm_input(G_NORM2 + 48 * layer + 32, HI_ORDER, following=f"ple_gate{layer}",
                           meanwhile=lambda: embed_out(f"ple_second{layer}", 1, 2))

            def take_out(k, at):
                t = n.add("turned_out") - 1
                act.wait_ge(out_turned, t + 1)
                nc.scalar.activation(token_major(at)[:, :, k * P:(k + 1) * P],
                                     banks[4 + t % 3][:, :].rearrange("p (a n) -> p a n", a=TT), ACT.Copy)\
                    .then_inc(out_taken, 1)

            def embed_gate(layer):
                name = f"ple_gate{layer}"
                for j in range(4):
                    if j == 0:
                        ahead(name, 1)
                        make_rstd(rstd[:, :], D)
                        table("sigmoid_and_others")
                    elif j > 1:
                        ahead(name, j)
                    pl = Place(tab, name, j)
                    if layer == 1 and j == 2:
                        for k in range(3, 6):
                            take_out(k, OUT_X)

                    def sigmoid(m):
                        act.wait_ge(tile_read, pl.tile + m + 1)
                        nc.scalar.activation(tmp[:, 2 + m, :], tmp[:, m, :], ACT.Sigmoid).then_inc(gate_out, 1)

                    def square_gated(m):
                        act.wait_ge(gated, n.add("gated"))
                        k = 2 * j + m
                        square(wt(k), k, (n["squares"] + k) % 2)

                    if layer == 0 and j == 3:
                        sigmoid(0)
                        square_gated(0)
                        sigmoid(1)
                        table("natural_log_exp_and_others")
                        square_gated(1)
                        break
                    if layer == 1 and j == 3:
                        sigmoid(0)
                        for k in range(1, 3):
                            take_out(k, OUT_E)
                        square_gated(0)
                        for k in range(3, 6):
                            take_out(k, OUT_E)
                        sigmoid(1)
                        table("natural_log_exp_and_others")
                        square_gated(1)
                        take_out(6, OUT_E)
                        break
                    for m in range(2):
                        sigmoid(m)
                    for m in range(2):
                        square_gated(m)
                    if layer == 1:
                        for k in ((), (0, 1, 2), (6, 7))[j]:
                            take_out(k, OUT_X)
                        if j == 2:
                            take_out(0, OUT_E)
                if layer == 0:
                    squared(KT, last=True)
                    split_half("conv_in", 1, 0)
                    make_rstd(rstd[:, :], D)
                    return
                squared(KT, last=2)
                take_out(KT - 1, OUT_E)
                act.wait_ge(stat_done, n.add("stat"))
                nc.scalar.activation(rstd_tok[:, :], banks[7][:, 0:TT], ACT.Ln, bias=eps[:, :], scale=1.0 / D)\
                    .then_inc(ln_done, 1)
                act.wait_ge(ln_done, n["stat"])
                nc.scalar.activation(rstd_tok[:, :], rstd_tok[:, :], ACT.Exp, scale=-0.5).then_inc(rstd_ready, 1)

            mixer_end("fox_out", 0)
            mlp(0)
            embed_gate(0)

            norm_input(G_NORM2 + 48, HI_ORDER, following="conv_in")
            for j in range(12):
                if j == 0:
                    ahead("conv_in", 1)
                    make_rstd(rstd[:, :], D)
                elif j > 1:
                    ahead("conv_in", j)
                if j % 3 == 2:
                    for m in range(2):
                        k = 2 * (j // 3) + m
                        act.wait_ge(conv_y, k + 1)
                        nc.scalar.activation(act_b[:, 0, k, :], tmp[:, 2 + m, :], ACT.Copy).then_inc(conv_hi, 1)
            mixer_end("conv_out", 1)
            mlp(1)
            embed_gate(1)

        @block.vector
        def _(dve):
            n = Steps()
            V = nc.vector

            def chain(ins, i=0, per=0):
                ins.then_inc(dve_step, 1)
                dve.wait_ge(dve_step, n.add("step") + per * i)

            def split(pl):
                if not pl.exists:
                    return
                dve.wait_ge(w_hi, pl.u + 1)
                cols = pl.split_cols
                V.tensor_tensor(wsp[:, pl.slot, 1, cols], raw[:, pl.slot, pl.raw_cols], wsp[:, pl.slot, 0, cols].bitcast(F32),
                                ALU.subtract).then_inc(w_split, 1)

            def split_half(name, j, half):
                pl = Place(tab, name, j)
                cols = slice(half * UNIT // 2, (half + 1) * UNIT // 2)
                dve.wait_ge(*((w_hi, pl.u + 1) if half else (half_hi, n.add("halves"))))
                V.tensor_tensor(wsp[:, pl.slot, 1, cols], raw[:, pl.slot, cols], wsp[:, pl.slot, 0, cols].bitcast(F32),
                                ALU.subtract).then_inc(w_split if half else half_split, 1)

            def ahead(name, j, i=0, per=0, passes=1):
                split(Place(tab, name, j, i, per, passes, ahead=1))

            def third_after_norm(name):
                dve.wait_ge(w_split, Place(tab, name, 1).u + 1)
                ahead(name, 1)

            def done(pl, m=0):
                dve.wait_ge(tile_done, pl.tile + m + 1)
                return banks[(pl.bank + m) % 4]

            def scaled(dst, pl, m=0):
                V.tensor_tensor(dst, done(pl, m)[:, :], rstd[:, :], ALU.mult).then_inc(tile_read, 1)

            def wait_rstd(k=1):
                dve.wait_ge(rstd_ready, n.add("stat", k))

            def low(dst, src, hi, sem_, scale=None):
                if scale is None:
                    V.tensor_tensor(dst, src, hi.bitcast(F32), ALU.subtract).then_inc(sem_, 1)
                else:
                    V.scalar_tensor_tensor(out=dst, in0=src, scalar=scale, in1=hi.bitcast(F32), op0=ALU.mult,
                                           op1=ALU.subtract).then_inc(sem_, 1)

            def input_lo(k, gain):
                dve.wait_ge(in_hi, n["in"] + k + 1)
                low(act_a[:, 1, k, :], wt(X + k), act_a[:, 0, k, :], in_ready, col(gain + k))

            def add_normed(tiles_at, gain, next_gain, following):
                wait_rstd()

                def scale(k):
                    m = wt(tiles_at + k)
                    V.scalar_tensor_tensor(out=m, in0=m, scalar=col(gain + k), in1=rstd[:, :], op0=ALU.mult, op1=ALU.mult)\
                        .then_inc(out_scaled, 1)

                def add(k):
                    if k == POOL_ADDS.stop:
                        dve.wait_ge(x_ready, n["x"] + k)
                    dve.wait_ge(out_scaled, n["scaled"] + k + 1)
                    V.tensor_tensor(wt(X + k), wt(X + k), wt(tiles_at + k), ALU.add).then_inc(x_ready, 1)

                for what, k in steps(NORM_ORDER):
                    if what == "l":
                        input_lo(k, next_gain)
                    elif what != "w":
                        {"m": scale, "a": add}[what](k)
                    elif k in HALVED[following]:
                        split_half(following, k, 1)
                n.add("scaled", KT)
                n.add("x", KT)
                n.add("in", KT)

            def project(name, passes, tiles_at, factor=True, first=0):
                with dve.Fori(first, passes) as i:
                    for j in range(2):
                        ahead(name, j, i, 2, passes)
                        pl = Place(tab, name, j, i, 2, passes)
                        for m in range(2):
                            dst = wt(tiles_at + 4 * i + 2 * j + m)
                            if factor:
                                scaled(dst, pl, m)
                            else:
                                V.tensor_copy(dst, done(pl, m)[:, :]).then_inc(tile_read, 1)

            def values_out(name, j, at, width, i=0, per=0, passes=1):
                pl = Place(tab, name, j, i, per, passes)
                ahead(name, j, i, per, passes)
                for a in range(TT):
                    c = at * S + a * width + 256 * j
                    V.tensor_scalar(work[:, bass.ds(c + 256 * per * i, 256)], done(pl, a)[:, 0:256],
                                    rstd_tok[:, a:a + 1], None, ALU.mult).then_inc(tile_read, 1)

            def turned_rstd():
                dve.wait_ge(rstd_turned, n.add("turned"))
                V.tensor_copy(rstd_tok[:, :], banks[7][:, 0:TT]).then_inc(rstd_tok_ready, 1)
                dve.wait_ge(rstd_tok_ready, n["turned"])

            V.memset(eps[:, :], EPS).then_inc(prologue_ready, 1)
            marks = [(kind, what) for kind in ATT for what in STARTS_FREE[kind]]
            for mark, (kind, what) in enumerate(marks):
                V.memset(free_mark[:, mark:mark + 1], 0.0).then_inc(ATT[kind][what], FREE)
            tile = tab.extra["sb_qk"]
            for at, width in ((0, 120), (120, 37)):
                dve.wait_ge(tile_done, tile + 1)
                V.tensor_copy(gains[:, at:at + width], first_bank(tile)[:, 0:width]).then_inc(tile_read, 1)
                tile += 1
            for what, k in steps(FIRST_LO_ORDER):
                if what == "e":
                    dve.wait_ge(tile_done, tile + k + 1)
                    V.tensor_copy(wt(X + k), first_bank(tile + k)[:, :]).then_inc(tile_read, 1)
                elif what == "l":
                    dve.wait_ge(tile_read, tile + k + 1)
                    input_lo(k, G_IN)
                else:
                    split(Place(tab, "sb_qk", k))
            n.add("in", KT)
            dve.wait_ge(late_landed, 16 * LATE_LOADS)
            for dst, src in ((identr[:, :], ident), (trir[:, :], rest["tri"]), (negonesr[:, :], rest["negones"]),
                             (maskr[:, 0, :], rest["foxmask"]), (maskr[:, 1, :], rest["mlamask"]),
                             (maskr[:, 2, :], rest["sbmask"])):
                V.tensor_copy(dst, src).then_inc(const_split, 1)
            V.tensor_copy(onesr[:, :], ones[0:48, :]).then_inc(const_split, 1)
            wf_flat = wf[:, :, :, :].rearrange("p a k n -> p a (k n)")
            V.tensor_copy(wf_flat[:, 0, :], wf_raw[:, :]).then_inc(const_split, 1)
            dve.wait_ge(const_split, CONST_SPLITS - 1)
            low(wf_flat[:, 1, :], wf_raw[:, :], wf_flat[:, 0, :], const_split)

            third_after_norm("sb_qk")
            wait_rstd()
            pl = Place(tab, "sb_qk", 0)
            for m in range(2):
                scaled(wt(m), pl, m)
            pl = Place(tab, "sb_qk", 1)
            for m in range(2):
                scaled(wt(2 + m), pl, m)
            project("sb_qk", 2, 0, first=1)
            turned_rstd()
            for j in range(2):
                values_out("sb_v", j, TILES["sb"]["v"], SB_HEADS * HD)

            def silu(at, sigmoid):
                dve.wait_ge(gate_out, n.add("gate"))
                V.tensor_tensor(wt(at), wt(at), sigmoid, ALU.mult).then_inc(silu_done, 1)

            def stage(kind, i, hh):
                A = ATT[kind]
                qk = qk_parts(kind, hh)
                rows = QK if kind == "mla" else HD
                end = sum(HI_STEPS[kind]) * i + sum(HI_STEPS[kind][0:hh + 1])
                before_v = 2 if kind == "fox" else 1
                q, k = (head_rows(kind, which, i, hh) for which in "qk")
                scale = SCALE[kind]
                if moved(kind, hh):
                    q, k, scale = moved_rows("q"), moved_rows("k"), None
                dve.wait_ge(A["stage_hi"], end - before_v - 1)
                low(qk(1)[0:rows, :], q, qk(0)[0:rows, :], A["staged"], scale)
                dve.wait_ge(A["stage_hi"], end - before_v)
                low(qk(3)[0:rows, :], k, qk(2)[0:rows, :], A["staged"])
                dve.wait_ge(A["stage_hi"], end)
                low(head_v[:, hh, 1, :, :], head_values(kind, i, hh), head_v[:, hh, 0, :, :], A["staged"])

            def clear_padding():
                V.memset(act_b[:, 0:2, TT - 1, 2 * P:3 * P].bitcast(F32), 0.0).then_inc(pad_zero, 1)

            for j in range(2):
                pl = Place(tab, "sb_gate", j)
                ahead("sb_gate", j)
                if j == 0:
                    clear_padding()
                    dve.wait_ge(tile_read, tab.end[tab.first["sb_v"] + 1])
                    stage("sb", 0, 0)
                for m in range(2):
                    scaled(wt(TILES["sb"]["gate"] + 2 * j + m), pl, m)
                for m in range(2):
                    silu(TILES["sb"]["gate"] + 2 * j + m, tmp[:, m, :])

            def beside_out(dst, pl, m):
                dve.wait_ge(tile_done, pl.tile + m + 1)
                V.tensor_tensor(dst, banks[6 + m][:, :], rstd[:, :], ALU.mult).then_inc(tile_read, 1)

            def gather(kind, i, hh):
                A = ATT[kind]
                dve.wait_ge(A["out"], FREE + 2 * i + hh + 1)
                rows = slice(hh * HD, (hh + 1) * HD)
                src, dst = banks[4 + hh if kind == "sb" else 5][0:HD, :], output_tile(kind, i)[rows, :]
                if kind == "fox":
                    V.tensor_scalar(dst, src, 1.0, None, ALU.mult).then_inc(A["gathered"], 1)
                else:
                    V.tensor_tensor(dst, src, wt(TILES[kind]["gate"] + i)[rows, :], ALU.mult).then_inc(A["gathered"], 1)

            def output_lo(kind, k):
                dve.wait_ge(ATT[kind]["o_hi"], k + 1)
                low(out_parts(kind, 1, k), output_tile(kind, k), out_parts(kind, 0, k), ATT[kind]["o_ready"])

            A = ATT["sb"]
            dve.wait_ge(stash_saved, 16)
            dve.wait_ge(silu_done, 4)

            def stick_pair(i, last=False):
                for hh in range(2):
                    h = 2 * i + hh

                    def part_lo(r, offset):
                        kt = TT - 1 - r
                        dve.wait_ge(A["part_hi"], 8 * h + offset + r + 1)
                        low(act_b[:, 1, kt, valid(kt)], tmp[:, kt, valid(kt)], act_b[:, 0, kt, valid(kt)], A["part_ready"])

                    def clip(r):
                        kt = TT - 1 - r
                        dve.wait_ge(A["scores"], 4 * h + r + 1)
                        V.tensor_scalar(tmp[:, kt, valid(kt)], banks[kt][:, valid(kt)], SOFTPLUS_LINEAR, None, ALU.min)                            .then_inc(A["clipped"], 1)

                    def softplus(r):
                        kt = TT - 1 - r
                        t = tmp[:, kt, valid(kt)]
                        dve.wait_ge(A["softplus"], 4 * h + r + 1)
                        V.tensor_tensor(t, banks[kt][:, valid(kt)], t, ALU.max).then_inc(A["normed"], 1)

                    clip(0)
                    clip(1)
                    softplus(0)
                    clip(2)
                    softplus(1)
                    part_lo(0, 0)
                    clip(3)
                    softplus(2)
                    part_lo(1, 0)
                    softplus(3)
                    part_lo(2, 0)
                    part_lo(3, 0)
                    if hh == 0:
                        stage("sb", i, 1)
                    elif not last:
                        stage("sb", i + 1, 0)
                    ahead(BESIDE["sb"], hh, i, 2, SB_HEADS // 2)
                    for r in range(TT):
                        part_lo(r, TT)
                    pl = Place(tab, BESIDE["sb"], hh, i, 2, SB_HEADS // 2)
                    for m in range(2):
                        beside_out(wt(16 + 4 * i + 2 * hh + m), pl, m)
                    gather("sb", i, hh)

            with dve.Fori(0, SB_HEADS // 2 - 1) as i:
                stick_pair(i)
            stick_pair(SB_HEADS // 2 - 1, last=True)
            for k in range(SB_HEADS // 2):
                output_lo("sb", k)

            ahead("c_rope", 0)
            pl = Place(tab, "c_rope", 0)
            scaled(wt(LATENTS[4]), pl)
            V.tensor_tensor(tmp[64:96, 2, :], done(pl, 1)[0:32, :], rstd[0:32, :], ALU.mult).then_inc(tile_read, 1)

            def gated_output(j):
                pl = Place(tab, "o_sb", j)
                for m in range(4):
                    k = 4 * j + m
                    dve.wait_ge(branch_gate, k + 1)
                    V.tensor_tensor(wt(Y_SB + k), done(pl, m)[:, :], wt(Y_GATE0 + k), ALU.mult).then_inc(tile_read, 1)

            def normed_latents(tiles, factor):
                wait_rstd()
                for k in tiles:
                    c = wt(LATENTS[k])
                    V.scalar_tensor_tensor(out=c, in0=c, scalar=col((G_Q if k < 3 else G_KV - 3) + k), in1=factor,
                                           op0=ALU.mult, op1=ALU.mult).then_inc(c_normed, 1)

            def latents_lo(tiles):
                for k in tiles:
                    dve.wait_ge(c_hi, k + 1)
                    parts = [act_b[:, hl, k, :] if k < 3 else head_qk[:, 2 * hl + k - 3, :] for hl in (0, 1)]
                    low(parts[1], wt(LATENTS[k]), parts[0], c_ready)

            normed_latents(range(3), wt(9))
            ahead("o_sb", 0)
            dve.wait_ge(rope_swapped, 32)
            V.tensor_tensor(tmp[64:96, 3, :], tmp[96:128, 2, :], rope[96:128, :], ALU.mult).then_inc(dve_step, 1)
            V.tensor_tensor(tmp[64:96, 2, :], tmp[64:96, 2, :], rope[64:96, :], ALU.mult).then_inc(dve_step, 1)
            dve.wait_ge(dve_step, n.add("step", 2))
            V.tensor_tensor(tmp[64:96, 2, :], tmp[64:96, 2, :], tmp[64:96, 3, :], ALU.add).then_inc(rope_k, 1)
            latents_lo(range(3))
            gated_output(0)
            normed_latents(range(3, 5), wt(10))
            ahead("o_sb", 1)
            latents_lo(range(3, 5))
            gated_output(1)
            for m in range(4):
                silu(TILES["mla"]["gate"] + m, wt(11 + m))
            for j in range(2):
                pl = Place(tab, "q_up", j)
                if j == 0:
                    ahead("q_up", 0)
                for m in range(4):
                    dst = wt(TILES["mla"]["q"] + 4 * j + m)
                    bank, part = done(pl, m), tmp[64:96, m % 2, :]
                    V.tensor_tensor(dst[0:96, :], bank[0:96, :], rope[0:96, :], ALU.mult).then_inc(dve_step, 1)
                    if 4 * j + m > 1:
                        dve.wait_ge(q_rotated, 4 * j + m - 1)
                    V.tensor_tensor(part, bank[96:128, :], rope[96:128, :], ALU.mult).then_inc(tile_read, 1)
                    dve.wait_ge(dve_step, n.add("step"))
                    dve.wait_ge(tile_read, pl.tile + m + 1)
                    V.tensor_tensor(dst[64:96, :], dst[64:96, :], part, ALU.add).then_inc(q_rotated, 1)
            def softmax_attention(kind, heads):
                A = ATT[kind]

                def maxima(i, s):
                    dve.wait_ge(A["scores"], FREE + 8 * i + s + 1)
                    V.reduce_max(negmax[:, s:s + 1], banks[s % 3][:, 0:(s % TT + 1) * P], AX, negate=True)                        .then_inc(A["negmax"], 1)

                def normalize(i, s):
                    dve.wait_ge(A["exp"], 8 * i + s + 1)
                    V.reciprocal(rinv[:, s:s + 1], rowsum[:, s:s + 1]).then_inc(A["step"], 1)
                    dve.wait_ge(A["step"], 8 * i + s + 1)
                    t = tmp[:, s % 4, 0:(s % TT + 1) * P]
                    V.tensor_scalar(t, t, rinv[:, s:s + 1], None, ALU.mult).then_inc(A["normed"], 1)

                def turned_lo(i, s):
                    j = s % TT
                    dve.wait_ge(A["pt_hi"], 8 * i + s + 1)
                    src = banks[3 + s % 2][:, 0:(j + 1) * P].rearrange("p (b n) -> p b n", b=j + 1)
                    dst = [act_b[:, hl, 0:j + 1, j * P:(j + 1) * P] for hl in (0, 1)]
                    low(dst[1], src, dst[0], A["pt_ready"])

                def unit_out(i, a, m):
                    pair = 2 * i + a
                    at = Y_GATE1 + 2 * pair + m if kind == "mla" else TILES["fox"][("q", "k")[m]] + pair + 2
                    beside_out(wt(at), Place(tab, BESIDE[kind], a, i, 2, passes), m)

                def two_pairs(i, orders=(DVE_ORDER, DVE_ORDER), last=False):
                    for a in range(2):
                        pair = 2 * i + a
                        for what, s in steps(orders[a]):
                            if what == "s":
                                if not (last and a == 1 and s == 2):
                                    stage(kind, pair + s // 2, s % 2)
                            elif what == "g":
                                gather(kind, pair, s)
                            elif what == "x":
                                unit_out(i, a, s)
                            elif what == "o":
                                output_lo(kind, s)
                            else:
                                {"m": maxima, "n": normalize, "p": turned_lo}[what](pair, s)

                passes = BESIDE_PASSES[kind]
                with dve.Fori(0, heads // 4 - 1) as i:
                    two_pairs(i)
                two_pairs(heads // 4 - 1, DVE_LAST if kind == "fox" else (DVE_ORDER, DVE_MLA_LAST), last=True)
                if kind == "fox":
                    dve.wait_ge(A["o_ready"], EARLY_OUT[kind])
                for k in range(EARLY_OUT[kind], heads // 2):
                    output_lo(kind, k)
                dve.wait_ge(w_split, tab.first[BESIDE[kind]] + 2 * passes + (2 if kind == "fox" else 1))

            clear_padding()
            dve.wait_ge(rope_spread, 16 * MLA_HEADS)
            dve.wait_ge(tile_read, Place(tab, "kv_up", 0).tile + TT + 1)
            stage("mla", 0, 0)
            dve.wait_ge(tile_read, tab.end[tab.first["kv_up"]])
            softmax_attention("mla", MLA_HEADS)
            def merged_lo(k):
                dve.wait_ge(merged_hi, k + 1)
                low(act_a[:, 1, k, :], wt(Y_SB + k), act_a[:, 0, k, :], merged)

            for j in range(2):
                pl = Place(tab, "o_mla", j)
                ahead("o_mla", j)
                for m in range(4):
                    k = 4 * j + m
                    dve.wait_ge(branch_gate, KT + k + 1)
                    V.tensor_tensor(wt(Y_GATE1 + k), done(pl, m)[:, :], wt(Y_GATE1 + k), ALU.mult).then_inc(tile_read, 1)
                    dve.wait_ge(tile_read, pl.tile + m + 1)
                    V.tensor_tensor(wt(Y_SB + k), wt(Y_SB + k), wt(Y_GATE1 + k), ALU.add).then_inc(gate_merge, 1)
                for k in range(4 * j, 4 * j + 4):
                    merged_lo(k)
            dve.wait_ge(stash_back, 16)
            with dve.Fori(0, 2) as i:
                for j in range(2):
                    ahead("w_out", j, i, 2, 2)
                    pl = Place(tab, "w_out", j, i, 2, 2)
                    for m in range(2):
                        x = wt(X + 4 * i + 2 * j + m)
                        V.tensor_tensor(x, done(pl, m)[:, :], x, ALU.add).then_inc(tile_read, 1)
            wait_rstd()
            dve.wait_ge(tile_read, tab.end[tab.first["w_out"] + 3])
            n.add("x", KT)
            for k in range(KT):
                V.scalar_tensor_tensor(out=wt(X + k), in0=wt(X + k), scalar=col(G_F + k), in1=rstd[:, :], op0=ALU.mult,
                                       op1=ALU.mult).then_inc(x_ready, 1)
                if k:
                    dve.wait_ge(x_ready, k)
                    input_lo(k - 1, G_NORM2)
            dve.wait_ge(x_ready, KT)
            input_lo(KT - 1, G_NORM2)
            n.add("in", KT)

            third_after_norm("fox_qk")
            wait_rstd()
            for j in range(2):
                for m in range(2):
                    scaled(wt(TILES["fox"][("q", "k")[m]] + j), Place(tab, "fox_qk", j), m)
            tile = tab.extra["fox_v"]
            f, t, total = (tmp[0:FOX_HEADS, a, :] for a in range(3))
            dve.wait_ge(tile_done, tile + 1)
            V.tensor_tensor(f, banks[tile % 4][0:FOX_HEADS, :], rstd[0:FOX_HEADS, :], ALU.mult).then_inc(tile_read, 1)
            dve.wait_ge(tile_read, tile + 1)
            chain(V.tensor_scalar(f, f, b_forget[:, :], None, ALU.add))
            V.tensor_scalar(t, f, -1.0, SOFTPLUS_LINEAR, ALU.mult, ALU.min).then_inc(decay_done, 1)
            dve.wait_ge(forget_log, 2)
            chain(V.scalar_tensor_tensor(out=t, in0=f, scalar=-1.0, in1=t, op0=ALU.mult, op1=ALU.max))
            V.tensor_tensor_scan(total, t, t, 0.0, ALU.add, ALU.max).then_inc(decay_done, 1)
            turned_rstd()
            dve.wait_ge(forget_log, 3)
            chain(V.memset(decay_parts, 0.0))
            hi = decay_row[0:FOX_HEADS, 0, :].bitcast(F32)
            V.tensor_copy(decay_parts[0:FOX_HEADS, :], hi).then_inc(dve_step, 1)
            n.add("step")
            chain(V.tensor_tensor(decay_parts[32:32 + FOX_HEADS, :], total, hi, ALU.subtract))
            clear_padding()
            for j in range(4):
                values_out("fox_v", j, 16, FOX_HEADS * HD)
                if j == 2:
                    dve.wait_ge(tile_read, tab.end[tab.first["fox_v"]])
                    stage("fox", 0, 0)
            dve.wait_ge(tile_read, tab.end[tab.first["fox_v"] + 3])
            softmax_attention("fox", FOX_HEADS)

            def mixer_end(name, layer):
                tile = tab.extra[name]
                for k in range(2):
                    dve.wait_ge(tile_done, tile + k + 1)
                    V.tensor_copy(tmp[:, k, :], banks[(tile + k) % 4][:, :]).then_inc(tile_read, 1)
                dve.wait_ge(tile_read, tile + 2)
                for k in range(2):
                    dve.wait_ge(p_split, 2 * layer + k + 1)
                    low(head_qk[:, 2 + k, :], tmp[:, k, :], head_qk[:, k, :], p_ready)
                for j in range(4):
                    pl = Place(tab, name, j)
                    if layer or j:
                        ahead(name, j)
                    for m in range(2):
                        if j == 3 and m == 1:
                            split_half(f"mlp{layer}", 1, 0)
                        if layer == 0 and j == 0:
                            dve.wait_ge(tile_done, pl.tile + m + 1)
                            src = banks[6 + m]
                        else:
                            src = done(pl, m)
                        V.tensor_copy(wt(8 + 2 * j + m), src[:, :]).then_inc(tile_read, 1)
                split_half(f"mlp{layer}", 0, 0)
                add_normed(8, G_NORM2 + 48 * layer + 8, G_NORM2 + 48 * layer + 16, f"mlp{layer}")

            def mlp(layer):
                chunks = D_FF // D
                name = f"mlp{layer}"
                hid = n["hid"]
                def chunk(i, first=False, last=False):
                    for j in range(8):
                        if first and j == 0:
                            third_after_norm(name)
                        elif not (first and j == 1):
                            ahead(name, j, i, 8, chunks)
                        pl = Place(tab, name, j, i, 8, chunks)
                        if first and j == 0:
                            wait_rstd()
                        if j < 4:
                            h = hid + KT * i + 2 * j
                            for m in range(2):
                                V.scalar_tensor_tensor(out=tmp[:, m, :], in0=done(pl, m)[:, :], scalar=0.0,
                                                       in1=rstd[:, :], op0=ALU.max, op1=ALU.mult).then_inc(tile_read, 1)
                            for m in range(2):
                                dve.wait_ge(tile_read, pl.tile + m + 1)
                                V.tensor_tensor(tmp[:, 2 + m, :], tmp[:, m, :], tmp[:, m, :], ALU.mult)                                    .then_inc(hid_square, 1)
                            for m in range(2):
                                dve.wait_ge(hid_square, h + m + 1)
                                dve.wait_ge(hid_hi, h + m + 1)
                                k = 2 * j + m
                                low(act_b[:, 1, k, :], tmp[:, 2 + m, :], act_b[:, 0, k, :], hid_ready)
                        else:
                            for m in range(2):
                                if last and j == 7 and m == 1:
                                    split_half(f"ple_gate{layer}", 1, 0)
                                t = wt(16 + 2 * (j - 4) + m)
                                if first:
                                    V.tensor_copy(t, done(pl, m)[:, :]).then_inc(tile_read, 1)
                                else:
                                    V.tensor_tensor(t, done(pl, m)[:, :], t, ALU.add).then_inc(tile_read, 1)

                chunk(0, first=True)
                with dve.Fori(1, chunks - 1) as i:
                    chunk(i)
                chunk(chunks - 1, last=True)
                n.add("hid", KT * chunks)
                split_half(f"ple_gate{layer}", 0, 0)
                add_normed(16, G_NORM2 + 48 * layer + 24, G_NORM2 + 48 * layer + 32, f"ple_gate{layer}")

            def embed_gate(layer):
                name = f"ple_gate{layer}"
                for j in range(4):
                    pl = Place(tab, name, j)
                    if j == 0:
                        third_after_norm(name)
                        wait_rstd()
                    elif j > 1:
                        ahead(name, j)
                    late = j == 3
                    scaled(tmp[:, 0, :], pl, 0)
                    if not late:
                        scaled(tmp[:, 1, :], pl, 1)
                    for m in range(2):
                        if late and m:
                            scaled(tmp[:, 1, :], pl, 1)
                        dve.wait_ge(gate_out, n.add("gate"))
                        k = 2 * j + m
                        V.tensor_tensor(wt(k), wt(k), tmp[:, 2 + m, :], ALU.mult).then_inc(gated, 1)
                        if layer == 1:
                            dve.wait_ge(gated, KT + k + 1)
                            V.tensor_scalar(wt(EG + k), wt(k), col(G_NORM2 + 48 + 40 + k), None, ALU.mult).then_inc(gained, 1)
                dve.wait_ge(gated, KT * (layer + 1))
                if layer == 0:
                    split_half("conv_in", 1, 0)
                    add_normed(0, G_NORM2 + 40, G_NORM2 + 48, "conv_in")
                    return
                wait_rstd()
                dve.wait_ge(out_taken, 2 * KT)
                for a in range(TT):
                    for half in range(2):
                        x, e = (token_major(at)[:, a, half * D // 2:(half + 1) * D // 2] for at in (OUT_X, OUT_E))
                        V.scalar_tensor_tensor(out=x, in0=e, scalar=rstd_tok[:, a:a + 1], in1=x, op0=ALU.mult, op1=ALU.add)\
                            .then_inc(out_tile, 1)

            mixer_end("fox_out", 0)
            mlp(0)
            embed_gate(0)

            padded = [work[:, (2 + 2 * m) * S:(2 + 2 * m) * S + S + 2] for m in range(2)]
            for m in range(2):
                V.memset(padded[m][:, 0:2], 0.0).then_inc(conv_pad, 1)
            for j in range(12):
                pl = Place(tab, "conv_in", j)
                if j == 0:
                    third_after_norm("conv_in")
                    wait_rstd()
                elif j > 1:
                    ahead("conv_in", j)
                part, pair = j % 3, j // 3
                if part == 0:
                    for m in range(2):
                        scaled(wt(m), pl, m)
                elif part == 1:
                    for m in range(2):
                        scaled(tmp[:, m, :], pl, m)
                    dve.wait_ge(tile_read, pl.tile + 2)
                    for m in range(2):
                        V.tensor_tensor(padded[m][:, 2:S + 2], tmp[:, m, :], wt(m), ALU.mult).then_inc(dve_step, 1)
                    n.add("step", 2)
                    dve.wait_ge(dve_step, n["step"])
                    if pair == 0:
                        dve.wait_ge(conv_pad, 2)
                    for tap in range(3):
                        for m in range(2):
                            w = col(G_CONV + KT * tap + 2 * pair + m)
                            src = padded[m][:, tap:tap + S]
                            if tap == 0:
                                ins_ = V.tensor_scalar(tmp[:, m, :], src, w, None, ALU.mult)
                            else:
                                ins_ = V.scalar_tensor_tensor(out=tmp[:, m, :], in0=src, scalar=w, in1=tmp[:, m, :],
                                                              op0=ALU.mult, op1=ALU.add)
                            ins_.then_inc(dve_step, 1)
                        n.add("step", 2)
                        dve.wait_ge(dve_step, n["step"])
                else:
                    for m in range(2):
                        scaled(tmp[:, 2 + m, :], pl, m)
                    dve.wait_ge(tile_read, pl.tile + 2)
                    for m in range(2):
                        V.tensor_tensor(tmp[:, 2 + m, :], tmp[:, 2 + m, :], tmp[:, m, :], ALU.mult).then_inc(conv_y, 1)
                    for m in range(2):
                        k = 2 * pair + m
                        dve.wait_ge(conv_y, k + 1)
                        dve.wait_ge(conv_hi, k + 1)
                        low(act_b[:, 1, k, :], tmp[:, 2 + m, :], act_b[:, 0, k, :], conv_ready)
            mixer_end("conv_out", 1)
            mlp(1)
            embed_gate(1)


        @block.gpsimd
        def _(pool):
            n = Steps()

            def sum_squares(tiles, last=0):
                if n["stat"]:
                    pool.wait_ge(stat_done, n["stat"])
                n.add("stat")
                done = n.add("squares", tiles) - tiles
                added = n.add("added", tiles - last) - (tiles - last)

                def add(k, parity):
                    pool.wait_ge(sq_done, done + k + 1)
                    nc.gpsimd.tensor_tensor(ssum[:, :], ssum[:, :], sq[:, parity, :], ALU.add).then_inc(sq_added, 1)
                    pool.wait_ge(sq_added, added + k + 1)

                pool.wait_ge(sq_done, done + 2)
                nc.gpsimd.tensor_tensor(ssum[:, :], sq[:, 0, :], sq[:, 1, :], ALU.add).then_inc(sq_added, 2)
                pool.wait_ge(sq_added, added + 2)
                pairs = (tiles - last) // 2
                if pairs > 1:
                    with pool.Fori(1, pairs) as i:
                        for m in range(2):
                            add(2 * i + m, (done + m) % 2)
                if (tiles - last) % 2:
                    add(tiles - last - 1, (done + tiles - last - 1) % 2)

            def split(name, j=1):
                pl = Place(tab, name, j)
                pool.wait_ge(w_hi, pl.u + 1)
                if pl.u:
                    pool.wait_ge(w_split, pl.u)
                nc.gpsimd.tensor_tensor(wsp[:, pl.slot, 1, :], raw[:, pl.slot, :], wsp[:, pl.slot, 0, :].bitcast(F32),
                                        ALU.subtract).then_inc(w_split, 1)

            def split_beside(kind):
                passes = BESIDE_PASSES[kind]
                with pool.Fori(0, passes) as i:
                    for a in range(2):
                        pl = Place(tab, BESIDE[kind], a, i, 2, passes, ahead=1)
                        pool.wait_ge(w_hi, pl.u + 1)
                        pool.wait_ge(w_split, pl.u)
                        nc.gpsimd.tensor_tensor(wsp[:, pl.slot, 1, :], raw[:, pl.slot, :],
                                                wsp[:, pl.slot, 0, :].bitcast(F32), ALU.subtract).then_inc(w_split, 1)

            def add_outputs(tiles_at):
                for k in POOL_ADDS:
                    pool.wait_ge(out_scaled, n["scaled"] + k + 1)
                    pool.wait_ge(x_ready, n["x"] + KT + k)
                    nc.gpsimd.tensor_tensor(wt(X + k), wt(X + k), wt(tiles_at + k), ALU.add).then_inc(x_ready, 1)
                n.add("scaled", KT)
                n.add("x", KT)

            sum_squares(KT)
            A = ATT["sb"]
            with pool.Fori(0, SB_HEADS // 2) as i:
                for hh in range(2):
                    h = 2 * i + hh
                    for r in range(TT):
                        kt = TT - 1 - r
                        diagonal = tmp[:, kt, kt * P:(kt + 1) * P]
                        pool.wait_ge(A["normed"], 4 * h + r + 1)
                        nc.gpsimd.tensor_tensor(diagonal, diagonal, strict, ALU.mult).then_inc(A["masked"], 1)
            sum_squares(Q_LORA // P)
            sum_squares(KV_LORA // P)
            split("kv_up", 0)
            split("gate1", 0)
            split_beside("mla")
            sum_squares(KT, last=True)
            split("fox_qk")
            sum_squares(KT)
            split_beside("fox")
            split("fox_out")
            for k in range(EARLY_OUT["fox"]):
                pool.wait_ge(ATT["fox"]["o_hi"], k + 1)
                nc.gpsimd.tensor_tensor(out_parts("fox", 1, k), output_tile("fox", k), out_parts("fox", 0, k).bitcast(F32),
                                        ALU.subtract).then_inc(ATT["fox"]["o_ready"], 1)
            pool.wait_ge(ATT["fox"]["staged"], 3 * FOX_HEADS)
            OUTPUTS_AT = {"mlp0": 8, "ple_gate0": 16, "conv_in": 0, "mlp1": 8, "ple_gate1": 16}
            for following in ("mlp0", "ple_gate0", "conv_in", "mlp1", "ple_gate1"):
                sum_squares(KT, last=True)
                add_outputs(OUTPUTS_AT[following])
                sum_squares(KT)
            sum_squares(KT, last=2)

_INS = ["x", "norm_in_g", "w_in", "b_gate", "q_norm_g", "w_q_up", "kv_norm_g", "w_kv_up", "w_o_sb", "w_o_mla", "w_out",
        "norm_f_g", "p_2", "norm_g_2", "w_attn_in_2", "b_forget_2", "w_attn_out_2", "w_conv_in_2", "conv_w_2",
        "w_conv_out_2", "w_mlp_up_2", "w_mlp_down_2", "w_ple_proj_2", "w_ple_gate_2"]


def kernel(**inputs):
    import numpy as _np
    import concourse.bacc as _bacc
    from concourse import mybir as _mybir
    from concourse.bass_utils import run_bass_kernel_spmd as _run

    nc = _bacc.Bacc("TRN2", target_bir_lowering=False, num_devices=1, dynamic_dma_scratch_size=1024)
    arrays, args = {}, {}
    for name in _INS:
        arrays[f"in_{name}"] = _np.ascontiguousarray(inputs[name])
    arrays["in_consts"] = constants()
    for name, a in arrays.items():
        args[name[3:]] = nc.dram_tensor(name, a.shape, _mybir.dt.from_np(a.dtype), kind="ExternalInput").ap()
    out = nc.dram_tensor("out_0", (1, S, D), F32, kind="ExternalOutput").ap()
    hybrid_block_kernel(nc, args, out)
    r = _run(nc, [arrays], core_ids=[0])
    return r.results[0]["out_0"]
```
